# Optimizing a Trainium2 kernel written in Bass

```python
import math
import jax, jax.numpy as jnp
from jax import lax
import numpy as np

D_MODEL = 1024
BATCH = 1
SEQ = 1024
DEPTH = 1
DEC_BATCH = 1
DEC_SEQ = 256
PAST_LEN = 128

HEAD_DIM = 64
N_Q_HEADS = 16
N_KV_HEADS = 4
GQA_GROUP = N_Q_HEADS // N_KV_HEADS
ATTN_WIDTH = N_Q_HEADS * HEAD_DIM
KV_WIDTH = N_KV_HEADS * HEAD_DIM
WINDOW = 128
BLOCK = 128
ROPE_THETA = 10000.0
SSM_HEADS = 8
SSM_HEAD_DIM = 64
SSM_INNER = SSM_HEADS * SSM_HEAD_DIM
SSM_GROUPS = 2
SSM_STATE = 128
SSM_CONV = 5
SSM_CHUNK = 128
XBC_WIDTH = SSM_INNER + 2 * SSM_GROUPS * SSM_STATE
DT_WIDTH = 2 * SSM_HEADS
N_MEM = 256
MEM_HEADS = 4
MEM_HEAD_DIM = 128
MEM_WIDTH = MEM_HEADS * MEM_HEAD_DIM
MIX_WIDTH = ATTN_WIDTH + SSM_INNER + MEM_WIDTH
IN_WIDTH = ATTN_WIDTH + 2 * KV_WIDTH + SSM_INNER + XBC_WIDTH + DT_WIDTH + MEM_WIDTH
D_FF = 2816
FFN_CONV = 3
EPS = 1e-6

kernel_name = "hymba_window_ssd_memory_encoder"

def rms_norm(x, w):
    xf = x.astype(jnp.float32)
    y = xf * lax.rsqrt(jnp.mean(xf * xf, axis=-1, keepdims=True) + EPS)
    return (y * w.astype(jnp.float32)).astype(x.dtype)

def rope(x, pos):
    d = x.shape[-1]
    inv = ROPE_THETA ** (-jnp.arange(0, d, 2, dtype=jnp.float32) / d)
    ang = pos.astype(jnp.float32)[:, None] * inv[None, :]
    cos = jnp.cos(ang)[None, :, None, :]
    sin = jnp.sin(ang)[None, :, None, :]
    xf = x.astype(jnp.float32)
    x1, x2 = xf[..., : d // 2], xf[..., d // 2:]
    return jnp.concatenate([x1 * cos - x2 * sin, x2 * cos + x1 * sin], axis=-1).astype(x.dtype)

def dwconv_centred(x, w, b):
    k = w.shape[0]
    pad = k // 2
    s = x.shape[1]
    xp = jnp.pad(x, ((0, 0), (pad, pad), (0, 0)))
    y = xp[:, 0:s] * w[0].astype(x.dtype) + b.astype(x.dtype)
    for t in range(1, k):
        y = y + xp[:, t:t + s] * w[t].astype(x.dtype)
    return y

def windowed_gqa(q, k, v, sink):
    b, s, _, dh = q.shape
    nb = s // BLOCK
    qb = jnp.moveaxis(q.reshape(b, nb, BLOCK, N_KV_HEADS, GQA_GROUP, dh), 1, 0)
    kp = jnp.pad(k, ((0, 0), (BLOCK, BLOCK), (0, 0), (0, 0)))
    vp = jnp.pad(v, ((0, 0), (BLOCK, BLOCK), (0, 0), (0, 0)))
    sink_f = sink.astype(jnp.float32).reshape(N_KV_HEADS, GQA_GROUP)[None, :, :, None]
    scale = dh ** -0.5
    q_off = jnp.arange(BLOCK)
    k_off = jnp.arange(3 * BLOCK)
    band = jnp.abs((k_off[None, :] - BLOCK) - q_off[:, None]) <= WINDOW

    def one_block(args):
        i, qi = args
        start = i * BLOCK
        ki = lax.dynamic_slice_in_dim(kp, start, 3 * BLOCK, axis=1)
        vi = lax.dynamic_slice_in_dim(vp, start, 3 * BLOCK, axis=1)
        kpos = start - BLOCK + k_off
        valid = band & ((kpos >= 0) & (kpos < s))[None, :]
        sc = jnp.einsum('bqhgd,bkhd->bhgqk', qi, ki, preferred_element_type=jnp.float32) * scale
        sc = jnp.where(valid, sc, -jnp.inf)
        m = jnp.maximum(jnp.max(sc, axis=-1), sink_f)
        p = jnp.exp(sc - m[..., None])
        denom = jnp.sum(p, axis=-1) + jnp.exp(sink_f - m)
        p = p / denom[..., None]
        o = jnp.einsum('bhgqk,bkhd->bqhgd', p, vi.astype(jnp.float32))
        return o.astype(q.dtype)

    out = lax.map(one_block, (jnp.arange(nb), qb))
    return jnp.moveaxis(out, 0, 1).reshape(b, s, N_Q_HEADS * dh)

def segsum_exp(a):
    t = a.shape[-1]
    cs = jnp.cumsum(a, axis=-1)
    diff = cs[..., :, None] - cs[..., None, :]
    mask = jnp.tril(jnp.ones((t, t), dtype=bool))
    return jnp.exp(jnp.where(mask, diff, -jnp.inf))

def ssd_scan(x, dt, a_neg, bm, cm):
    b, s, nh, hp = x.shape
    nc = s // SSM_CHUNK
    ln = SSM_CHUNK
    e = nh // SSM_GROUPS
    xf = (x.astype(jnp.float32) * dt[..., None]).reshape(b, nc, ln, SSM_GROUPS, e, hp)
    a = jnp.transpose((dt * a_neg).reshape(b, nc, ln, SSM_GROUPS, e), (0, 1, 3, 4, 2))
    bf = bm.astype(jnp.float32).reshape(b, nc, ln, SSM_GROUPS, SSM_STATE)
    cf = cm.astype(jnp.float32).reshape(b, nc, ln, SSM_GROUPS, SSM_STATE)
    a_cs = jnp.cumsum(a, axis=-1)
    lmat = segsum_exp(a)
    cb = jnp.einsum('bclgn,bcsgn->bcgls', cf, bf)
    y_diag = jnp.einsum('bcgls,bcgels,bcsgep->bclgep', cb, lmat, xf)
    decay_states = jnp.exp(a_cs[..., -1:] - a_cs)
    states = jnp.einsum('bclgn,bcgel,bclgep->bcgepn', bf, decay_states, xf)
    chunk_decay = jnp.exp(a_cs[..., -1])

    def step(h, inp):
        st, dec = inp
        return h * dec[..., None, None] + st, h

    h0 = jnp.zeros((b, SSM_GROUPS, e, hp, SSM_STATE), jnp.float32)
    _, h_prev = lax.scan(step, h0, (jnp.moveaxis(states, 1, 0), jnp.moveaxis(chunk_decay, 1, 0)))
    h_prev = jnp.moveaxis(h_prev, 0, 1)
    y_off = jnp.einsum('bclgn,bcgepn,bcgel->bclgep', cf, h_prev, jnp.exp(a_cs))
    return (y_diag + y_off).reshape(b, s, nh, hp)

def ssd_bidirectional(z, xbc, dt_raw, conv_w, conv_b, dt_bias, a_log, d_skip, norm_w):
    b, s, _ = z.shape
    xbc = jax.nn.silu(dwconv_centred(xbc, conv_w, conv_b))
    xs = xbc[..., :SSM_INNER].reshape(b, s, SSM_HEADS, SSM_HEAD_DIM)
    bm = xbc[..., SSM_INNER:SSM_INNER + SSM_GROUPS * SSM_STATE].reshape(b, s, SSM_GROUPS, SSM_STATE)
    cm = xbc[..., SSM_INNER + SSM_GROUPS * SSM_STATE:].reshape(b, s, SSM_GROUPS, SSM_STATE)
    dt = jax.nn.softplus(dt_raw.astype(jnp.float32).reshape(b, s, 2, SSM_HEADS)
                         + dt_bias.astype(jnp.float32))
    a_neg = -jnp.exp(a_log.astype(jnp.float32))
    y_f = ssd_scan(xs, dt[:, :, 0], a_neg[0], bm, cm)
    y_b = ssd_scan(xs[:, ::-1], dt[:, ::-1, 1], a_neg[1], bm[:, ::-1], cm[:, ::-1])[:, ::-1]
    y = y_f + y_b + d_skip.astype(jnp.float32)[:, None] * xs.astype(jnp.float32)
    y = y.reshape(b, s, SSM_INNER) * jax.nn.silu(z.astype(jnp.float32))
    return rms_norm(y, norm_w).astype(z.dtype)

def memory_attention(mq, mk, mv):
    b, s = mq.shape[:2]
    sc = jnp.einsum('bshd,bmhd->bhsm', mq, mk, preferred_element_type=jnp.float32) * (MEM_HEAD_DIM ** -0.5)
    p = jax.nn.softmax(sc, axis=-1)
    o = jnp.einsum('bhsm,bmhd->bshd', p, mv.astype(jnp.float32))
    return o.astype(mq.dtype).reshape(b, s, MEM_WIDTH)

def encoder_layer(x, mem, norm1_w, w_in, q_norm_w, k_norm_w, attn_sink, ssm_conv_w, ssm_conv_b,
                  ssm_dt_bias, ssm_A_log, ssm_D, ssm_norm_w, mem_norm_w, w_mem_kv, mq_norm_w,
                  mk_norm_w, w_out, norm2_w, w_ffn_up, ffn_conv_w, ffn_conv_b, w_ffn_down):
    b, s, _ = x.shape
    h = rms_norm(x, norm1_w)
    proj = h @ w_in
    sizes = (ATTN_WIDTH, KV_WIDTH, KV_WIDTH, SSM_INNER, XBC_WIDTH, DT_WIDTH)
    q, k, v, z, xbc, dt_raw, mq = jnp.split(proj, np.cumsum(sizes).tolist(), axis=-1)
    pos = jnp.arange(s)
    q = rope(rms_norm(q.reshape(b, s, N_Q_HEADS, HEAD_DIM), q_norm_w), pos)
    k = rope(rms_norm(k.reshape(b, s, N_KV_HEADS, HEAD_DIM), k_norm_w), pos)
    v = v.reshape(b, s, N_KV_HEADS, HEAD_DIM)
    attn_out = windowed_gqa(q, k, v, attn_sink)
    ssm_out = ssd_bidirectional(z, xbc, dt_raw, ssm_conv_w, ssm_conv_b, ssm_dt_bias, ssm_A_log, ssm_D, ssm_norm_w)
    m = mem.shape[1]
    mkv = rms_norm(mem, mem_norm_w) @ w_mem_kv
    mk = rms_norm(mkv[..., :MEM_WIDTH].reshape(b, m, MEM_HEADS, MEM_HEAD_DIM), mk_norm_w)
    mv = mkv[..., MEM_WIDTH:].reshape(b, m, MEM_HEADS, MEM_HEAD_DIM)
    mq = rms_norm(mq.reshape(b, s, MEM_HEADS, MEM_HEAD_DIM), mq_norm_w)
    mem_out = memory_attention(mq, mk, mv)
    mix = jnp.concatenate([attn_out, ssm_out, mem_out], axis=-1)
    x = x + mix @ w_out
    u = dwconv_centred(rms_norm(x, norm2_w) @ w_ffn_up, ffn_conv_w, ffn_conv_b)
    gate, up = u[..., :D_FF], u[..., D_FF:]
    return x + (jax.nn.silu(gate) * up) @ w_ffn_down

def setup_inputs(seed: int = 0) -> dict:
    key = jax.random.key(seed)
    ks = jax.random.split(key, 32)
    f32 = jnp.float32

    def nrm(k, shape, scale):
        return jax.random.normal(k, shape, f32) * scale

    def gain(k, shape):
        return 1.0 + 0.02 * jax.random.normal(k, shape, f32)

    dt0 = jnp.exp(jax.random.uniform(ks[12], (DEPTH, 2, SSM_HEADS), f32, math.log(1e-3), math.log(1e-1)))
    return {
        "x_prompt": nrm(ks[0], (BATCH, SEQ, D_MODEL), 1.0),
        "x_sample": nrm(ks[1], (DEC_BATCH, DEC_SEQ, D_MODEL), 1.0),
        "mem_prompt": nrm(ks[2], (BATCH, N_MEM, D_MODEL), 1.0),
        "mem_sample": nrm(ks[3], (DEC_BATCH, N_MEM, D_MODEL), 1.0),
        "norm1_w": gain(ks[4], (DEPTH, D_MODEL)),
        "w_in": nrm(ks[5], (DEPTH, D_MODEL, IN_WIDTH), D_MODEL ** -0.5),
        "q_norm_w": gain(ks[6], (DEPTH, HEAD_DIM)),
        "k_norm_w": gain(ks[7], (DEPTH, HEAD_DIM)),
        "attn_sink": nrm(ks[8], (DEPTH, N_Q_HEADS), 0.5),
        "ssm_conv_w": nrm(ks[9], (DEPTH, SSM_CONV, XBC_WIDTH), SSM_CONV ** -0.5),
        "ssm_conv_b": nrm(ks[10], (DEPTH, XBC_WIDTH), 0.01),
        "ssm_dt_bias": dt0 + jnp.log(-jnp.expm1(-dt0)),
        "ssm_A_log": jnp.log(jax.random.uniform(ks[11], (DEPTH, 2, SSM_HEADS), f32, 1.0, 16.0)),
        "ssm_D": gain(ks[13], (DEPTH, SSM_HEADS)),
        "ssm_norm_w": gain(ks[14], (DEPTH, SSM_INNER)),
        "mem_norm_w": gain(ks[15], (DEPTH, D_MODEL)),
        "w_mem_kv": nrm(ks[16], (DEPTH, D_MODEL, 2 * MEM_WIDTH), D_MODEL ** -0.5),
        "mq_norm_w": gain(ks[17], (DEPTH, MEM_HEAD_DIM)),
        "mk_norm_w": gain(ks[18], (DEPTH, MEM_HEAD_DIM)),
        "w_out": nrm(ks[19], (DEPTH, MIX_WIDTH, D_MODEL), MIX_WIDTH ** -0.5),
        "norm2_w": gain(ks[20], (DEPTH, D_MODEL)),
        "w_ffn_up": nrm(ks[21], (DEPTH, D_MODEL, 2 * D_FF), D_MODEL ** -0.5),
        "ffn_conv_w": nrm(ks[22], (DEPTH, FFN_CONV, 2 * D_FF), FFN_CONV ** -0.5),
        "ffn_conv_b": nrm(ks[23], (DEPTH, 2 * D_FF), 0.01),
        "w_ffn_down": nrm(ks[24], (DEPTH, D_FF, D_MODEL), D_FF ** -0.5),
    }

def reference(x_prompt, x_sample, mem_prompt, mem_sample, norm1_w, w_in, q_norm_w, k_norm_w, attn_sink,
              ssm_conv_w, ssm_conv_b, ssm_dt_bias, ssm_A_log, ssm_D, ssm_norm_w, mem_norm_w, w_mem_kv,
              mq_norm_w, mk_norm_w, w_out, norm2_w, w_ffn_up, ffn_conv_w, ffn_conv_b, w_ffn_down):
    weights = (norm1_w, w_in, q_norm_w, k_norm_w, attn_sink, ssm_conv_w, ssm_conv_b, ssm_dt_bias,
               ssm_A_log, ssm_D, ssm_norm_w, mem_norm_w, w_mem_kv, mq_norm_w, mk_norm_w, w_out,
               norm2_w, w_ffn_up, ffn_conv_w, ffn_conv_b, w_ffn_down)
    y_prompt = x_prompt
    y_sample = x_sample
    for layer in range(DEPTH):
        layer_w = [w[layer] for w in weights]
        y_prompt = encoder_layer(y_prompt, mem_prompt, *layer_w)
        y_sample = encoder_layer(y_sample, mem_sample, *layer_w)
    return (y_prompt, y_sample)


_drawn_inputs = setup_inputs


def setup_inputs(seed=0):
    import zlib

    import numpy as np

    out = dict(_drawn_inputs(seed))
    spreads = {}
    factors = {'norm1_w': 3.878,
     'q_norm_w': 8.0,
     'k_norm_w': 8.0,
     'attn_sink': 8.0,
     'ssm_conv_b': 6.549,
     'ssm_D': 8.0,
     'ssm_norm_w': 5.925,
     'mem_norm_w': 8.0,
     'mq_norm_w': 8.0,
     'mk_norm_w': 8.0,
     'norm2_w': 4.253,
     'ffn_conv_b': 8.0}
    for name, (base, spread) in spreads.items():
        noise = np.random.default_rng([zlib.crc32(name.encode()), seed]).standard_normal(out[name].shape)
        drawn = base * np.exp(spread * noise) if base else spread * noise
        out[name] = __import__('jax').numpy.asarray(drawn.astype(out[name].dtype))
    for name, factor in factors.items():
        out[name] = (out[name] * factor).astype(out[name].dtype)
    return out
```

```python
import concourse.bass as bass
from concourse import mybir
from contextlib import ExitStack
import numpy as np

FP32 = mybir.dt.float32
F32R = mybir.dt.float32r
ALU = mybir.AluOpType
ACT = mybir.ActivationFunctionType
AX = mybir.AxisListType

P = 128
D = 1024
KC = D // P
SEQ, DEC = 1024, 256
TP, TS = SEQ // P, DEC // P
NT = TP + TS
TOK = NT * P
NMT = 4
HQ, HKV, DH = 16, 4, 64
HM, DM = 4, 128
NS, PS, NG, ST = 8, 64, 2, 128
XBC = NS * PS + 2 * NG * ST
F = 2816
NF = F // P
EPS = 1e-6
PW = 512
CUT = 448
TOKEN_CUTS = ((0, CUT), (CUT, CUT), (2 * CUT, TOK - 2 * CUT))
NPAN = 5
NEG = -1e30
KB = NT + 3


def ds(a, n):
    return bass.ds(a, n)


class Bufs:

    def __init__(self, nc, ctx):
        self.nc, self.ctx, self.own = nc, ctx, []

    def sb(self, name, shape, dt=FP32):
        return self.ctx.enter_context(self.nc.sbuf_tensor(name, shape, dt))

    def ps(self, name, shape):
        return self.ctx.enter_context(self.nc.psum_tensor(name, shape, FP32))

    def sem(self, name):
        self.own.append(self.ctx.enter_context(self.nc.semaphore(name)))
        return self.own[-1]

    def sems(self, name, n):
        return [self.sem(f"{name}{i}") for i in range(n)]

    def block(self):
        self.ctx.callback(self.clear)
        return self.ctx.enter_context(self.nc.Block())

    def clear(self):
        with self.nc.Block() as block:
            @block.gpsimd
            def _(pool):
                for s in self.own:
                    pool.sem_clear(s)


def norm_transpose(nc, tag, tiles, weight_rows, ident_dram, hi, lo, src_dram=None, src_sb=None):
    with ExitStack() as ctx:
        b = Bufs(nc, ctx)
        ident = b.sb(f"{tag}_ident", [P, P])
        wb = b.sb(f"{tag}_w", [P, len(weight_rows), D])
        x = b.sb(f"{tag}_x", [P, tiles, D]) if src_dram is not None else None
        xn = b.sb(f"{tag}_xn", [P, 2, D])
        junk = b.sb(f"{tag}_junk", [P, 2, D])
        ms = b.sb(f"{tag}_ms", [P, tiles])
        mse = b.sb(f"{tag}_mse", [P, tiles])
        rstd = b.sb(f"{tag}_rstd", [P, tiles])
        half = b.sb(f"{tag}_half", [P, 1])
        eps = b.sb(f"{tag}_eps", [P, 1])
        xt = b.ps(f"{tag}_xt", [P, 2, KC, P])
        const_loaded = b.sem(f"{tag}_const")
        x_loaded = b.sems(f"{tag}_xl", 2)
        half_set = b.sem(f"{tag}_halfset")
        squared, mse_done, rstd_done = b.sem(f"{tag}_sq"), b.sem(f"{tag}_mse"), b.sem(f"{tag}_rs")
        normed, transposed, hi_done, lo_done = (b.sem(f"{tag}_{n}") for n in ("xn", "tr", "hi", "lo"))
        block = b.block()

        @block.sync
        def _(sp):
            sp.dma_start(ident[:, :], ident_dram).then_inc(const_loaded, 16)
            for i, (w, _, _) in enumerate(weight_rows):
                sp.wait_ge(const_loaded, 16 * (i + 1))
                sp.dma_start(wb[:, i], w.broadcast_to([P, D])).then_inc(const_loaded, 16)
            if src_dram is not None:
                for s in range(2):
                    sp.dma_start(x[:, s], src_dram[s * P:(s + 1) * P, :]).then_inc(x_loaded[s], 16)
                with sp.Fori(1, tiles // 2) as j:
                    for s in range(2):
                        sp.wait_ge(x_loaded[s], 16 * j)
                        sp.dma_start(x[:, ds(2 * j + s, 1)], src_dram[ds((2 * j + s) * P, P), :]
                                     ).then_inc(x_loaded[s], 16)

        def source(t):
            rows = x if src_dram is not None else src_sb
            return rows[:, t, :] if isinstance(t, int) else rows[:, ds(t, 1), :]

        @block.scalar
        def _(act):
            def square(j, s):
                t = 2 * j + s
                if src_dram is not None:
                    act.wait_ge(x_loaded[s], 16 * j + 16)
                if not (isinstance(j, int) and j == 0):
                    act.wait_ge(squared, t - 1)
                nc.scalar.activation(junk[:, s], source(t), ACT.Square, scale=D ** -0.5,
                                     accum_out=ms[:, ds(t, 1)]).then_inc(squared, 1)

            def high(j, s):
                t = 2 * j + s
                act.wait_ge(transposed, t + 1)
                nc.scalar.activation(hi[:, :, ds(t * P, P)], xt[:, s], ACT.Copy).then_inc(hi_done, 1)

            for s in range(2):
                square(0, s)
            with act.Fori(0, tiles // 2 - 1) as j:
                for s in range(2):
                    square(j + 1, s)
                    high(j, s)
            for s in range(2):
                high(tiles // 2 - 1, s)

        @block.gpsimd
        def _(pool):
            nc.gpsimd.memset(half[:, :], -0.5).then_inc(half_set, 1)
            nc.gpsimd.memset(eps[:, :], EPS).then_inc(half_set, 1)
            pool.wait_ge(half_set, 2)
            with pool.Fori(0, tiles) as t:
                pool.wait_ge(squared, t + 1)
                nc.gpsimd.tensor_tensor(mse[:, ds(t, 1)], ms[:, ds(t, 1)], eps[:, :],
                                        ALU.add).then_inc(mse_done, 1)
                pool.wait_ge(mse_done, t + 1)
                nc.gpsimd.tensor_tensor(rstd[:, ds(t, 1)], mse[:, ds(t, 1)], half[:, :],
                                        ALU.pow).then_inc(rstd_done, 1)

        @block.vector
        def _(dve):
            def norm(t, s, weight, first=False):
                dve.wait_ge(rstd_done, t + 1)
                if not first:
                    dve.wait_ge(transposed, t - 1)
                nc.vector.scalar_tensor_tensor(xn[:, s], source(t), rstd[:, ds(t, 1)], wb[:, weight],
                                               ALU.mult, ALU.mult).then_inc(normed, 1)

            def low(t, s):
                dve.wait_ge(hi_done, t + 1)
                nc.vector.tensor_tensor(lo[:, :, ds(t * P, P)], xt[:, s],
                                        hi[:, :, ds(t * P, P)].bitcast(FP32),
                                        ALU.subtract).then_inc(lo_done, 1)

            dve.wait_ge(const_loaded, 16 * (1 + len(weight_rows)))
            for s in range(2):
                norm(s, s, 0, True)
            for i, (_, first, count) in enumerate(weight_rows):
                with dve.Fori(max(first // 2, 1), (first + count) // 2) as j:
                    for s in range(2):
                        low(2 * j + s - 2, s)
                        norm(2 * j + s, s, i)
            for s in range(2):
                low(tiles - 2 + s, s)

        @block.tensor
        def _(pe):
            pe.wait_ge(const_loaded, 16 * (1 + len(weight_rows)))

            def one(t, s, first):
                pe.wait_ge(normed, t + 1)
                if not first:
                    pe.wait_ge(lo_done, t - 1)
                for k in range(KC):
                    m = nc.tensor.transpose(xt[:, s, k], xn[:, s, k * P:(k + 1) * P], ident[:, :])
                m.then_inc(transposed, 1)

            for s in range(2):
                one(s, s, True)
            with pe.Fori(1, tiles // 2) as j:
                for s in range(2):
                    one(2 * j + s, s, False)


def projections(nc, hi, lo, w_in, w_mem, proj, mem_proj, xbc_t, dt_t):
    PIECES, RAW = 4, 4
    rows = KC // PIECES
    with ExitStack() as ctx:
        b = Bufs(nc, ctx)
        raw = b.sb("pj_raw", [P, RAW, rows, PW])
        w_hi = b.sb("pj_whi", [P, 2, KC, PW], F32R)
        w_lo = b.sb("pj_wlo", [P, 2, KC, PW], F32R)
        dt_raw = b.sb("pj_dtraw", [P, KC, 16])
        dt_hi = b.sb("pj_dthi", [P, KC, 16], F32R)
        dt_lo = b.sb("pj_dtlo", [P, KC, 16], F32R)
        stage = b.sb("pj_stage", [P, 4, PW])
        bank = b.ps("pj_bank", [P, 8, PW])
        raw_loaded = b.sems("pj_rawl", RAW)
        dt_loaded = b.sem("pj_dtl")
        w_hi_done, w_split = b.sem("pj_whid"), b.sem("pj_split")
        multiplied = b.sem("pj_mm")
        copied = b.sem("pj_copied")
        stored = b.sems("pj_stored", 4)
        block = b.block()

        w_mem_v = w_mem.rearrange("(k p) n -> p k n", p=P)
        w_in_v = w_in.rearrange("(k p) n -> p k n", p=P)
        MEM0, TOK0, XBC0 = 0, 2 * NMT, 2 * NMT + NPAN * NT
        DT0 = XBC0 + 2 * 12
        GROUPS = DT0 + 3

        def col(n):
            return n * PW

        @block.sync
        def _(sp):
            sp.dma_start(dt_raw[:, :, :], w_in_v[:, :, 3584:3600]).then_inc(dt_loaded, 16)

            def load(n, src, c):
                for q in range(PIECES):
                    if not isinstance(n, int) or n > 0:
                        sp.wait_ge(w_split, PIECES * (n - 1) + q + 1)
                    sp.dma_start(raw[:, q], src[:, q * rows:(q + 1) * rows, c]).then_inc(raw_loaded[q], 16)

            for n in range(2):
                load(n, w_mem_v, slice(col(n), col(n + 1)))
            with sp.Fori(0, NPAN + 2) as m:
                load(m + 2, w_in_v, ds(m * PW, PW))

        @block.vector
        def _(dve):
            dve.wait_ge(dt_loaded, 16)
            nc.vector.tensor_copy(dt_hi[:, :, :], dt_raw[:, :, :]).then_inc(w_hi_done, 1)
            dve.wait_ge(w_hi_done, 1)
            nc.vector.tensor_tensor(dt_lo[:, :, :], dt_raw[:, :, :], dt_hi[:, :, :].bitcast(FP32),
                                    ALU.subtract).then_inc(w_hi_done, 1)

            def split(n, s, free):
                if free is not None:
                    dve.wait_ge(multiplied, free)
                for q in range(PIECES):
                    dve.wait_ge(raw_loaded[q], 16 * (n + 1))
                    k = slice(q * rows, (q + 1) * rows)
                    nc.vector.tensor_copy(w_hi[:, s, k], raw[:, q]).then_inc(w_hi_done, 1)
                    dve.wait_ge(w_hi_done, 2 + PIECES * n + q + 1)
                    nc.vector.tensor_tensor(w_lo[:, s, k], raw[:, q], w_hi[:, s, k].bitcast(FP32),
                                            ALU.subtract).then_inc(w_split, 1)

            split(0, 0, None)
            split(1, 1, None)
            split(2, 0, MEM0 + NMT)
            split(3, 1, TOK0)
            with dve.Fori(0, 2) as j:
                split(2 * j + 4, 0, TOK0 + NT * (2 * j + 1))
                split(2 * j + 5, 1, TOK0 + NT * (2 * j + 2))
            split(8, 0, XBC0)

        @block.tensor
        def _(pe):
            W = (w_hi, w_lo)
            X = (hi, lo)

            def token_panel(n, s, tiles, t0, g0, bank0):
                pe.wait_ge(w_split, PIECES * (n + 1))
                for t in range(tiles):
                    g = g0 + t
                    if not (isinstance(g, int) and g < 8):
                        pe.wait_ge(copied, g - 7)
                    for k in range(KC):
                        for i, (a, c) in enumerate(((0, 0), (0, 1), (1, 0))):
                            m = nc.tensor.matmul(bank[:, (bank0 + t) % 8],
                                                 X[a][:, k, (t0 + t) * P:(t0 + t + 1) * P],
                                                 W[c][:, s, k], start=(k == 0 and i == 0),
                                                 stop=(k == KC - 1 and i == 2))
                    m.then_inc(multiplied, 1)

            def channel_group(g, bk, width, lhs, t0, n):
                pe.wait_ge(copied, g - 7)
                for k in range(KC):
                    for i, (a, c) in enumerate(((0, 0), (0, 1), (1, 0))):
                        m = nc.tensor.matmul(bank[0:width, bk, 0:n], lhs(a, k), X[c][:, k, t0:t0 + n],
                                             start=(k == 0 and i == 0), stop=(k == KC - 1 and i == 2))
                m.then_inc(multiplied, 1)

            token_panel(0, 0, NMT, NT, 0, 0)
            token_panel(1, 1, NMT, NT, NMT, NMT)
            token_panel(2, 0, NT, 0, TOK0, 0)
            token_panel(3, 1, NT, 0, TOK0 + NT, NT)
            token_panel(4, 0, NT, 0, TOK0 + 2 * NT, 2 * NT)
            token_panel(5, 1, NT, 0, TOK0 + 3 * NT, 3 * NT)
            token_panel(6, 0, NT, 0, TOK0 + 4 * NT, 4 * NT)
            pe.wait_ge(w_hi_done, 2)
            for n, s in ((7, 1), (8, 0)):
                pe.wait_ge(w_split, PIECES * (n + 1))
                for m4 in range(4):
                    for i, (t0, w) in enumerate(((0, 512), (512, 512), (1024, 256))):
                        g = XBC0 + (n - 7) * 12 + m4 * 3 + i
                        channel_group(g, g % 8, P,
                                      lambda a, k, s=s, m4=m4: W[a][:, s, k, m4 * P:(m4 + 1) * P], t0, w)
            for i, (t0, w) in enumerate(((0, 512), (512, 512), (1024, 256))):
                g = DT0 + i
                channel_group(g, g % 8, 16, lambda a, k: (dt_hi, dt_lo)[a][:, k], t0, w)

        @block.scalar
        def _(act):
            def out(g, s, bk, rows_, n, dst, first=False):
                act.wait_ge(multiplied, g + 1)
                if not first:
                    act.wait_ge(stored[s], 16 * (g // 4) if isinstance(g, int) else 16 * (g - s) // 4)
                nc.scalar.activation(stage[0:rows_, s, 0:n], bank[0:rows_, bk, 0:n], ACT.Copy).then_inc(copied, 1)
                act.wait_ge(copied, g + 1)
                act.dma_start(dst, stage[0:rows_, s, 0:n]).then_inc(stored[s], 16)

            for n in range(2):
                for t in range(NMT):
                    g = NMT * n + t
                    out(g, g % 4, g % 8, P, PW, mem_proj[t * P:(t + 1) * P, col(n):col(n + 1)], g < 4)
            for n in range(NPAN):
                for t in range(NT):
                    g = TOK0 + NT * n + t
                    out(g, g % 4, g % 8, P, PW, proj[t * P:(t + 1) * P, col(n):col(n + 1)])
            for n in range(8):
                for i, (t0, w) in enumerate(((0, 512), (512, 512), (1024, 256))):
                    g = XBC0 + 3 * n + i
                    out(g, g % 4, g % 8, P, w, xbc_t[n * P:(n + 1) * P, t0:t0 + w])
            for i, (t0, w) in enumerate(((0, 512), (512, 512), (1024, 256))):
                g = DT0 + i
                out(g, g % 4, g % 8, 16, w, dt_t[:, t0:t0 + w])
            for s in range(4):
                act.wait_ge(stored[s], 16 * len(range(s, GROUPS, 4)))


def bc(ap, shape):
    return ap.broadcast_to(shape)


def attention(nc, proj, ident_dram, mask_dram, rope_dram, small, mix_t):
    q_w, k_w, sink = small["q_norm_w"], small["k_norm_w"], small["attn_sink"]
    WIN = 3 * P
    with ExitStack() as ctx:
        b = Bufs(nc, ctx)
        ident = b.sb("at_ident", [P, P])
        mask = b.sb("at_mask", [P, 2, WIN])
        rope = b.sb("at_rope", [P, 2, TP, DH])
        wrow = b.sb("at_wrow", [P, 4, DH])
        table = b.sb("at_table", [P, 4, TP, DH])
        k_raw = b.sb("at_kraw", [P, NT, HKV, DH])
        k_a = b.sb("at_ka", [P, NT, HKV, DH])
        k_two = b.sb("at_ktwo", [P, NT, HKV, 2, DH])
        k_b = k_two[:, :, :, 0]
        k_ss = b.sb("at_kss", [P, NT * HKV])
        k_mse = b.sb("at_kmse", [P, NT * HKV])
        k_rstd = b.sb("at_krstd", [P, NT * HKV])
        v_sb = b.sb("at_v", [P, KB, HKV * DH])
        kt_hi = b.sb("at_kthi", [P, HKV, KB * P], F32R)
        kt_lo = b.sb("at_ktlo", [P, HKV, KB * P], F32R)
        half = b.sb("at_half", [P, NT * HKV])
        eps = b.sb("at_eps", [P, NT * HKV])
        sinkb = b.sb("at_sink", [P, HQ])
        nsink = b.sb("at_nsink", [P, HQ])
        q_raw = b.sb("at_qraw", [P, 2, HQ, DH])
        q_sq = b.sb("at_qsq", [P, HQ, DH])
        q_c = b.sb("at_qc", [P, 2, HQ, DH])
        q_b = b.sb("at_qb", [P, HQ, DH])
        q_n = b.sb("at_qn", [P, HQ, DH])
        q_two = b.sb("at_qtwo", [P, HQ, 2, DH])
        q_ss = b.sb("at_qss", [P, 2, HQ])
        q_mse = b.sb("at_qmse", [P, 2, HQ])
        q_rstd = b.sb("at_qrstd", [P, 2, HQ])
        qt = b.sb("at_qt", [P, 2, HQ, P], F32R)
        sm = b.sb("at_sm", [P, 4, WIN])
        pr = b.sb("at_pr", [P, 4, WIN])
        pt = b.sb("at_pt", [P, 2, 3, P])
        nm = b.sb("at_nm", [P, 2, HQ])
        rowsum = b.sb("at_rowsum", [P, 2, HQ])
        t1 = b.sb("at_t1", [P, HQ])
        es = b.sb("at_es", [P, HQ])
        den = b.sb("at_den", [P, HQ])
        rec = b.sb("at_rec", [P, HQ])
        o_sb = b.sb("at_o", [P, HQ, DH])
        ot = b.sb("at_ot", [P, KC * P])
        s_ps = b.ps("at_sps", [P, 2, PW])
        t_ps = b.ps("at_tps", [P, 2, 4, P])
        o_ps = b.ps("at_ops", [P, HQ, DH])
        x_ps = b.ps("at_xps", [P, 8, P])
        names = ("const", "kvl", "ksq", "kred", "krs", "kprep", "kt", "khi", "klo", "half", "vzero", "table",
                 "qss", "qred", "qpow", "qmse", "qrot", "qn", "qhi", "qlo", "s", "m", "e", "t", "pt", "v",
                 "t1", "es", "den", "oscaled", "x", "xcopy", "ready")
        S = {n: b.sem(f"at_s_{n}") for n in names}
        q_loaded, m_loaded = b.sems("at_ql", 2), b.sems("at_ml", 2)
        stored = b.sem("at_stored")
        block = b.block()

        def blk(t):
            return (t if t < TP else t + 1) if isinstance(t, int) else t

        def tile_loop(engine, body):
            for s in range(2):
                body(s, s)
            with engine.Fori(1, TP // 2) as j:
                for s in range(2):
                    body(2 * j + s, s)
            for s in range(2):
                body(TP + s, s)

        @block.sync
        def _(sp):
            kv = proj.rearrange("(t p) n -> p t n", p=P)
            loads = [(ident[:, :], ident_dram), (rope[:, :, :, :], rope_dram),
                     (wrow[:, 0], q_w.broadcast_to([P, DH])), (wrow[:, 2], k_w.broadcast_to([P, DH])),
                     (wrow[:, 1, 0:32], q_w[:, 32:64].broadcast_to([P, 32])),
                     (wrow[:, 1, 32:64], q_w[:, 0:32].broadcast_to([P, 32])),
                     (wrow[:, 3, 0:32], k_w[:, 32:64].broadcast_to([P, 32])),
                     (wrow[:, 3, 32:64], k_w[:, 0:32].broadcast_to([P, 32])),
                     (sinkb[:, :], sink.broadcast_to([P, HQ]))]
            for dst, src in loads:
                sp.dma_start(dst, src).then_inc(S["const"], 16)
            sp.dma_start(k_raw[:, :, :, :], kv[:, :, 1024:1280]).then_inc(S["kvl"], 16)
            sp.wait_ge(S["vzero"], 1)
            sp.dma_start(v_sb[:, 1:1 + TP, :], kv[:, 0:TP, 1280:1536]).then_inc(S["kvl"], 16)
            sp.dma_start(v_sb[:, TP + 2:TP + 2 + TS, :], kv[:, TP:NT, 1280:1536]).then_inc(S["kvl"], 16)

            def load(t, s):
                if not (isinstance(t, int) and t < 2):
                    sp.wait_ge(S["qrot"], t - 1)
                    sp.wait_ge(S["qss"], t - 1)
                rows = slice(t * P, (t + 1) * P) if isinstance(t, int) else ds(t * P, P)
                sp.dma_start(q_raw[:, s], proj[rows, 0:1024]).then_inc(q_loaded[s], 16)
                if not (isinstance(t, int) and t < 2):
                    sp.wait_ge(S["m"], HQ * (t - 1))
                sp.dma_start(mask[:, s], mask_dram[t] if isinstance(t, int) else mask_dram[ds(t, 1)]
                             ).then_inc(m_loaded[s], 16)

            tile_loop(sp, load)

        @block.gpsimd
        def _(pool):
            g = nc.gpsimd
            g.memset(half[:, :], -0.5).then_inc(S["half"], 1)
            g.memset(eps[:, :], EPS).then_inc(S["half"], 1)
            pool.wait_ge(S["half"], 2)
            pool.wait_ge(S["kred"], 1)
            g.tensor_tensor(k_mse[:, :], k_ss[:, :], eps[:, :], ALU.add).then_inc(S["krs"], 1)
            pool.wait_ge(S["krs"], 1)
            g.tensor_tensor(k_rstd[:, :], k_mse[:, :], half[:, :], ALU.pow).then_inc(S["krs"], 1)
            pool.wait_ge(S["table"], 4)

            def queries(t, s):
                j = t if isinstance(t, int) else (t - s)
                pos = (t % TP) if isinstance(t, int) else t
                first = isinstance(t, int) and t < 2
                pool.wait_ge(q_loaded[s], (16 * (t // 2 + 1)) if isinstance(t, int) else 8 * (t - s) + 16)
                if not first:
                    pool.wait_ge(S["qn"], t - 1)
                if not (isinstance(t, int) and t == 0):
                    pool.wait_ge(S["qrot"], t)
                tab = [table[:, i, pos:pos + 1, :] if isinstance(pos, int) else table[:, i, ds(pos, 1), :]
                       for i in range(2)]
                g.tensor_tensor(q_c[:, s], q_raw[:, s], bc(tab[0], [P, HQ, DH]), ALU.mult).then_inc(S["qpow"], 1)
                for lo_, hi_ in ((0, 32), (32, 64)):
                    g.tensor_tensor(q_b[:, :, lo_:lo_ + 32], q_raw[:, s, :, 32 - lo_:64 - lo_],
                                    bc(tab[1][:, :, lo_:hi_], [P, HQ, 32]), ALU.mult).then_inc(S["qpow"], 1)
                pool.wait_ge(S["qpow"], 3 * t + 3)
                g.tensor_tensor(q_c[:, s], q_c[:, s], q_b[:, :, :], ALU.add).then_inc(S["qrot"], 1)
                pool.wait_ge(S["qred"], t + 1)
                g.tensor_tensor(q_mse[:, s], q_ss[:, s], eps[:, 0:HQ], ALU.add).then_inc(S["qmse"], 1)
                pool.wait_ge(S["qmse"], 2 * t + 1)
                g.tensor_tensor(q_rstd[:, s], q_mse[:, s], half[:, 0:HQ], ALU.pow).then_inc(S["qmse"], 1)

            tile_loop(pool, queries)

        def q_loaded_value(t, s):
            return 16 * (t // 2 + 1) if isinstance(t, int) else 8 * (t - s) + 16

        def unit(t, kind):
            if isinstance(t, int) and t == 0:
                return {"q0": 3, "q1": 4}[kind]
            return 3 * t + {"o": 2, "q0": 3, "q1": 4}[kind]

        def queries_units(t):
            return 2 if isinstance(t, int) and t == 0 else 3 * t + 1

        def square(act, t, s):
            act.wait_ge(q_loaded[s], q_loaded_value(t, s))
            if not (isinstance(t, int) and t == 0):
                act.wait_ge(S["qred"], t)
            nc.scalar.activation(q_sq[:, :, :], q_raw[:, s], ACT.Square, scale=DH ** -0.5).then_inc(S["qss"], 1)

        def high(act, t):
            act.wait_ge(S["qn"], t + 1)
            if not (isinstance(t, int) and t == 0):
                act.wait_ge(S["x"], queries_units(t - 1))
            nc.scalar.activation(q_two[:, :, 0].bitcast(F32R), q_n[:, :, :], ACT.Copy).then_inc(S["qhi"], 1)

        def q_evac(act, s, h, n):
            act.wait_ge(S["x"], n)
            nc.scalar.activation(qt[:, s, 8 * h:8 * h + 8], x_ps[:, :, :], ACT.Copy).then_inc(S["xcopy"], 1)

        @block.scalar
        def _(act):
            act.wait_ge(S["kvl"], 48)
            nc.scalar.activation(k_a[:, :, :, :], k_raw[:, :, :, :], ACT.Square, scale=DH ** -0.5).then_inc(S["ksq"], 1)
            def key_high(t, s):
                act.wait_ge(S["kt"], t + 1)
                nc.scalar.activation(kt_hi[:, :, ds((blk(t) + 1) * P, P)], t_ps[:, s], ACT.Copy
                                     ).then_inc(S["khi"], 1)

            tile_loop(act, key_high)
            square(act, 0, 0)
            high(act, 0)
            q_evac(act, 0, 0, 1)
            q_evac(act, 0, 1, 2)

            def tile(t, s):
                last = isinstance(t, int) and t == NT - 1
                zero = isinstance(t, int) and t == 0
                for h in range(HQ):
                    n = HQ * t + h
                    act.wait_ge(S["m"], n + 1)
                    if not (zero and h < 4):
                        act.wait_ge(S["t"], n - 3)
                    nc.scalar.activation(pr[:, h % 4], sm[:, h % 4], ACT.Exp, bias=nm[:, s, h:h + 1],
                                         scale=-1.0, accum_out=rowsum[:, s, h:h + 1]).then_inc(S["e"], 1)
                    if h == 0 and not last:
                        square(act, t + 1, 1 - s)
                    if h == 1 and not zero:
                        act.wait_ge(S["t1"], t)
                        nc.scalar.activation(es[:, :], t1[:, :], ACT.Exp).then_inc(S["es"], 1)
                    if h == 7 and not zero:
                        store_output(t - 1, unit(t, "o"))
                    if h == 6 and not last:
                        high(act, t + 1)
                    if h == 10 and not last:
                        q_evac(act, 1 - s, 0, unit(t, "q0"))
                    if h == 13 and not last:
                        q_evac(act, 1 - s, 1, unit(t, "q1"))

            def store_output(t, u):
                act.wait_ge(S["x"], u)
                if not (isinstance(t, int) and t == 0):
                    act.wait_ge(stored, 16 * t)
                nc.scalar.activation(ot[:, :], x_ps[:, :, :], ACT.Copy).then_inc(S["xcopy"], 1)
                act.wait_ge(S["xcopy"], u)
                dst = mix_t[t] if isinstance(t, int) else mix_t[ds(t, 1)]
                act.dma_start(dst[..., 0:KC * P], ot[:, :]).then_inc(stored, 16)

            tile_loop(act, tile)
            act.wait_ge(S["t1"], NT)
            nc.scalar.activation(es[:, :], t1[:, :], ACT.Exp).then_inc(S["es"], 1)
            store_output(NT - 1, 3 * NT)
            act.wait_ge(stored, 16 * NT)

        @block.vector
        def _(dve):
            v = nc.vector
            v.memset(v_sb[:, :, :], 0.0).then_inc(S["vzero"], 1)
            for i, z in enumerate((0, TP + 1, KB - 1)):
                v.memset(kt_hi[:, :, z * P:(z + 1) * P].bitcast(FP32), 0.0)
                last = v.memset(kt_lo[:, :, z * P:(z + 1) * P].bitcast(FP32), 0.0)
            dve.wait_ge(S["const"], 16 * 9)
            for i in range(4):
                v.tensor_tensor(table[:, i], rope[:, i % 2], bc(wrow[:, i:i + 1, :], [P, TP, DH]),
                                ALU.mult).then_inc(S["table"], 1)
            v.tensor_scalar(nsink[:, :], sinkb[:, :], -1.0, None, ALU.mult).then_inc(S["table"], 1)
            dve.wait_ge(S["ksq"], 1)
            v.reduce_sum(k_ss[:, :], k_a[:, :, :, :], AX.X).then_inc(S["kred"], 1)
            dve.wait_ge(S["table"], 5)
            dve.wait_ge(S["kred"], 1)
            n = 0
            for t0, m in ((0, TP), (TP, TS)):
                c = table[:, 2, 0:m].unsqueeze(2)
                sn = table[:, 3, 0:m].unsqueeze(2)
                v.tensor_tensor(k_a[:, t0:t0 + m], k_raw[:, t0:t0 + m], bc(c, [P, m, HKV, DH]),
                                ALU.mult).then_inc(S["kprep"], 1)
                for a in (0, 32):
                    v.tensor_tensor(k_b[:, t0:t0 + m, :, a:a + 32], k_raw[:, t0:t0 + m, :, 32 - a:64 - a],
                                    bc(sn[:, :, :, a:a + 32], [P, m, HKV, 32]),
                                    ALU.mult).then_inc(S["kprep"], 1)
            dve.wait_ge(S["kprep"], 6)
            v.tensor_tensor(k_a[:, :, :, :], k_a[:, :, :, :], k_b[:, :, :, :], ALU.add).then_inc(S["kprep"], 1)
            dve.wait_ge(S["kprep"], 7)
            dve.wait_ge(S["krs"], 2)
            kr = k_rstd[:, :].rearrange("p (t h) -> p t h", h=HKV).unsqueeze(3)
            for i in range(2):
                v.tensor_tensor(k_two[:, :, :, i], k_a[:, :, :, :], bc(kr, [P, NT, HKV, DH]),
                                ALU.mult).then_inc(S["kprep"], 1)
            def key_low(t, s):
                cols = ds((blk(t) + 1) * P, P)
                dve.wait_ge(S["khi"], t + 1)
                v.tensor_tensor(kt_lo[:, :, cols], t_ps[:, s], kt_hi[:, :, cols].bitcast(FP32),
                                ALU.subtract).then_inc(S["klo"], 1)

            tile_loop(dve, key_low)

            def reduce(t, s):
                dve.wait_ge(S["qss"], t + 1)
                if not (isinstance(t, int) and t < 2):
                    dve.wait_ge(S["qmse"], 2 * (t - 1))
                v.reduce_sum(q_ss[:, s], q_sq[:, :, :], AX.X).then_inc(S["qred"], 1)

            def scaled(t, s):
                dve.wait_ge(S["qmse"], 2 * t + 2)
                v.tensor_tensor(q_n[:, :, :], q_c[:, s], bc(q_rstd[:, s].unsqueeze(2), [P, HQ, DH]),
                                ALU.mult).then_inc(S["qn"], 1)

            def low(t):
                dve.wait_ge(S["qhi"], t + 1)
                v.tensor_tensor(q_two[:, :, 1].bitcast(F32R), q_n[:, :, :], q_two[:, :, 0],
                                ALU.subtract).then_inc(S["qlo"], 1)

            reduce(0, 0)
            scaled(0, 0)
            low(0)

            def finish(t, s):
                dve.wait_ge(S["es"], t + 1)
                v.tensor_tensor(den[:, :], rowsum[:, s], es[:, :], ALU.add).then_inc(S["den"], 1)
                dve.wait_ge(S["den"], 2 * t + 1)
                v.reciprocal(rec[:, :], den[:, :]).then_inc(S["den"], 1)
                dve.wait_ge(S["den"], 2 * t + 2)
                dve.wait_ge(S["v"], HQ * (t + 1))
                if not (isinstance(t, int) and t == 0):
                    dve.wait_ge(S["x"], unit(t, "o"))
                for c in range(2):
                    m = v.tensor_tensor(o_sb[:, 8 * c:8 * c + 8], o_ps[:, 8 * c:8 * c + 8],
                                        bc(rec[:, 8 * c:8 * c + 8].unsqueeze(2), [P, 8, DH]), ALU.mult)
                m.then_inc(S["oscaled"], 1)

            def sink_term(t, s):
                dve.wait_ge(S["m"], HQ * (t + 1))
                if not (isinstance(t, int) and t == 0):
                    dve.wait_ge(S["es"], t)
                v.tensor_tensor(t1[:, :], nm[:, s], sinkb[:, :], ALU.add).then_inc(S["t1"], 1)

            def copy_pt(n, h):
                dve.wait_ge(S["t"], n + 1)
                if not (isinstance(n, int) and n < 2):
                    dve.wait_ge(S["v"], n - 1)
                v.tensor_copy(pt[:, h % 2], t_ps[:, h % 2, 0:3]).then_inc(S["pt"], 1)

            def tile(t, s):
                last = isinstance(t, int) and t == NT - 1
                zero = isinstance(t, int) and t == 0
                dve.wait_ge(m_loaded[s], q_loaded_value(t, s))
                for h in range(HQ):
                    n = HQ * t + h
                    if h == 0 and not zero:
                        sink_term(t - 1, 1 - s)
                    if not (zero and h < 3):
                        copy_pt(n - 3, h + 1)
                    dve.wait_ge(S["s"], n + 1)
                    if not (zero and h < 4):
                        dve.wait_ge(S["e"], n - 3)
                    dve.sem_inc(S["ready"], 1)
                    v.tensor_tensor_reduce(out=sm[:, h % 4], in0=s_ps[:, h % 2, 0:WIN], in1=mask[:, s],
                                           scale=-(DH ** -0.5), scalar=nsink[:, h:h + 1], op0=ALU.add,
                                           op1=ALU.min, accum_out=nm[:, s, h:h + 1]).then_inc(S["m"], 1)
                    if h == 4 and not zero:
                        finish(t - 1, 1 - s)
                    if h == 1 and not last:
                        reduce(t + 1, 1 - s)
                    if h == 5 and not last:
                        scaled(t + 1, 1 - s)
                    if h == 7 and not last:
                        low(t + 1)

            tile_loop(dve, tile)
            for n in range(HQ * NT - 3, HQ * NT):
                copy_pt(n, n % 2)
            sink_term(NT - 1, 1)
            finish(NT - 1, 1)

        @block.tensor
        def _(pe):
            T = nc.tensor
            pe.wait_ge(S["const"], 16 * 9)
            pe.wait_ge(S["kprep"], 9)

            for t in range(NT):
                if t >= 2:
                    pe.wait_ge(S["klo"], t - 1)
                for j in range(HKV):
                    m = T.transpose(t_ps[:, t % 2, j], k_two[:, t, j], ident[:, :])
                m.then_inc(S["kt"], 1)
            pe.wait_ge(S["klo"], NT)

            def q_unit(c, before):
                if before is not None:
                    pe.wait_ge(S["xcopy"], before)
                for h in range(8):
                    m = T.transpose(x_ps[:, h], q_two[:, 8 * c + h], ident[:, :])
                m.then_inc(S["x"], 1)

            pe.wait_ge(S["qlo"], 1)
            q_unit(0, None)
            q_unit(1, 1)

            def o_unit(t, u):
                pe.wait_ge(S["oscaled"], t + 1)
                pe.wait_ge(S["xcopy"], u - 1)
                for c in range(KC):
                    m = T.transpose(x_ps[:, c], o_sb[:, 2 * c:2 * c + 2], ident[:, :])
                m.then_inc(S["x"], 1)

            def weights_t(n, h):
                pe.wait_ge(S["e"], n + 1)
                if not (isinstance(n, int) and n < 2):
                    pe.wait_ge(S["pt"], n - 1)
                for k in range(3):
                    m = T.transpose(t_ps[:, h % 2, k], pr[:, h % 4, k * P:(k + 1) * P], ident[:, :])
                m.then_inc(S["t"], 1)

            def values(n, t, h):
                pe.wait_ge(S["pt"], n + 1)
                if h == 0 and not (isinstance(t, int) and t == 0):
                    pe.wait_ge(S["oscaled"], t)
                g = (h // 4) * DH
                for k in range(3):
                    kb = blk(t) + k
                    rhs = v_sb[:, kb, g:g + DH] if isinstance(kb, int) else v_sb[:, ds(kb, 1), g:g + DH]
                    m = T.matmul(o_ps[:, h], pt[:, h % 2, k], rhs, start=(k == 0), stop=(k == 2))
                m.then_inc(S["v"], 1)

            def tile(t, s):
                last = isinstance(t, int) and t == NT - 1
                zero = isinstance(t, int) and t == 0
                pe.wait_ge(S["xcopy"], queries_units(t))
                for h in range(HQ):
                    n = HQ * t + h
                    if not (zero and h < 2):
                        pe.wait_ge(S["m"], n - 1)
                    k0 = blk(t) * P
                    cols = slice(k0, k0 + WIN) if isinstance(k0, int) else ds(k0, WIN)
                    T.matmul(s_ps[:, h % 2, 0:WIN], qt[:, s, h], kt_hi[:, h // 4, cols], start=True, stop=False)
                    T.matmul(s_ps[:, h % 2, 0:WIN], qt[:, s, h], kt_lo[:, h // 4, cols], start=False,
                             stop=True).then_inc(S["s"], 1)
                    if not (zero and h < 2):
                        weights_t(n - 2, (h + 2) % 4)
                    if not (zero and h < 4):
                        if h >= 4:
                            values(n - 4, t, h - 4)
                        else:
                            values(n - 4, t - 1, h + HQ - 4)
                    if h == 6 and not zero:
                        o_unit(t - 1, unit(t, "o"))
                    if h == 9 and not last:
                        pe.wait_ge(S["qlo"], t + 2)
                        q_unit(0, unit(t, "q0") - 1)
                    if h == 12 and not last:
                        q_unit(1, unit(t, "q1") - 1)

            tile_loop(pe, tile)
            weights_t(HQ * NT - 2, 2)
            values(HQ * NT - 4, NT - 1, HQ - 4)
            weights_t(HQ * NT - 1, 3)
            for h in range(HQ - 3, HQ):
                values(HQ * (NT - 1) + h, NT - 1, h)
            o_unit(NT - 1, 3 * NT)


def memory(nc, proj, mem_proj, ident_dram, small, mix_t):
    MT = NMT // 2
    NK = MT * P
    SC = DM ** -0.5
    with ExitStack() as ctx:
        b = Bufs(nc, ctx)
        ident = b.sb("me_ident", [P, P])
        wq = b.sb("me_wq", [P, 1, DM])
        wk = b.sb("me_wk", [P, 1, DM])
        half = b.sb("me_half", [P, NMT * HM])
        eps = b.sb("me_eps", [P, NMT * HM])
        k_raw = b.sb("me_kraw", [P, NMT, HM, DM])
        k_sq = b.sb("me_ksq", [P, NMT, HM, DM])
        k_n = b.sb("me_kn", [P, NMT, HM, DM])
        k_ss = b.sb("me_kss", [P, NMT * HM])
        k_mse = b.sb("me_kmse", [P, NMT * HM])
        k_rstd = b.sb("me_krstd", [P, NMT * HM])
        v_sb = b.sb("me_v", [P, NMT, HM, DM])
        kt = b.sb("me_kt", [P, HM, NMT * P])
        q_raw = b.sb("me_qraw", [P, 2, HM, DM])
        q_sq = b.sb("me_qsq", [P, HM, DM])
        q_w = b.sb("me_qw", [P, HM, DM])
        q_n = b.sb("me_qn", [P, HM, DM])
        q_ss = b.sb("me_qss", [P, HM])
        q_mse = b.sb("me_qmse", [P, HM])
        q_rstd = b.sb("me_qrstd", [P, HM])
        qt = b.sb("me_qt", [P, HM, P])
        mx = b.sb("me_mx", [P, HM])
        nm = b.sb("me_nm", [P, HM])
        rowsum = b.sb("me_rowsum", [P, 2, HM])
        rec = b.sb("me_rec", [P, HM])
        pr = b.sb("me_pr", [P, HM, NK])
        pt = b.sb("me_pt", [P, HM, MT, P])
        o_sb = b.sb("me_o", [P, HM, DM])
        ot = b.sb("me_ot", [P, HM * P])
        s_ps = b.ps("me_sps", [P, HM, NK])
        t_ps = b.ps("me_tps", [P, HM, MT, P])
        q_ps = b.ps("me_qps", [P, HM, P])
        o_ps = b.ps("me_ops", [P, HM, DM])
        ot_ps = b.ps("me_otps", [P, HM, P])
        S = {n: b.sem(f"me_s_{n}") for n in (
            "const", "kv", "ksq", "kred", "kpow", "kn", "kt", "kcopy", "half",
            "sq", "red", "pow", "qw", "qn", "qt", "qcopy", "s", "mx", "nm", "e", "t", "tcopy", "o", "rec",
            "oscaled", "ot", "otcopy")}
        q_loaded = b.sems("me_ql", 2)
        stored = b.sem("me_stored")
        block = b.block()

        def steps(engine, body, first=0, last=NT):
            for t in range(first, 2):
                body(t, t % 2)
            with engine.Fori(1, TP // 2) as j:
                for s in range(2):
                    body(2 * j + s, s)
            for t in range(TP, last):
                body(t, t % 2)

        def is0(t, n=0):
            return isinstance(t, int) and t <= n

        @block.sync
        def _(sp):
            kv = mem_proj.rearrange("(t p) n -> p t n", p=P)
            for dst, src in ((ident[:, :], ident_dram), (wq[:, 0], small["mq_norm_w"].broadcast_to([P, DM])),
                             (wk[:, 0], small["mk_norm_w"].broadcast_to([P, DM]))):
                sp.dma_start(dst, src).then_inc(S["const"], 16)
            sp.dma_start(k_raw[:, :, :, :], kv[:, :, 0:512]).then_inc(S["kv"], 16)
            sp.dma_start(v_sb[:, :, :, :], kv[:, :, 512:1024]).then_inc(S["kv"], 16)

            def load(t, s):
                if not is0(t, 1):
                    sp.wait_ge(S["sq"], t - 1)
                    sp.wait_ge(S["qw"], t - 1)
                rows = slice(t * P, (t + 1) * P) if isinstance(t, int) else ds(t * P, P)
                sp.dma_start(q_raw[:, s], proj[rows, 2048:2560]).then_inc(q_loaded[s], 16)

            steps(sp, load)

        def loaded(t, s):
            return 16 * (t // 2 + 1) if isinstance(t, int) else 8 * (t - s) + 16

        @block.gpsimd
        def _(pool):
            g = nc.gpsimd
            g.memset(half[:, :], -0.5).then_inc(S["half"], 1)
            g.memset(eps[:, :], EPS).then_inc(S["half"], 1)
            pool.wait_ge(S["half"], 2)
            pool.wait_ge(S["kred"], 1)
            g.tensor_tensor(k_mse[:, :], k_ss[:, :], eps[:, :], ALU.add).then_inc(S["kpow"], 1)
            pool.wait_ge(S["kpow"], 1)
            g.tensor_tensor(k_rstd[:, :], k_mse[:, :], half[:, :], ALU.pow).then_inc(S["kpow"], 1)
            pool.wait_ge(S["const"], 48)

            def queries(t, s):
                pool.wait_ge(q_loaded[s], loaded(t, s))
                if not is0(t):
                    pool.wait_ge(S["qn"], t)
                g.tensor_tensor(q_w[:, :, :], q_raw[:, s], bc(wq[:, :, :], [P, HM, DM]), ALU.mult
                                ).then_inc(S["qw"], 1)
                pool.wait_ge(S["red"], t + 1)
                g.tensor_tensor(q_mse[:, :], q_ss[:, :], eps[:, 0:HM], ALU.add).then_inc(S["pow"], 1)
                pool.wait_ge(S["pow"], 2 * t + 1)
                g.tensor_tensor(q_rstd[:, :], q_mse[:, :], half[:, 0:HM], ALU.pow).then_inc(S["pow"], 1)

            steps(pool, queries)

        @block.scalar
        def _(act):
            a = nc.scalar
            act.wait_ge(S["kv"], 32)
            a.activation(k_sq[:, :, :, :], k_raw[:, :, :, :], ACT.Square, scale=SC).then_inc(S["ksq"], 1)
            for i in range(2):
                for m in range(2):
                    act.wait_ge(S["kt"], 2 * i + m + 1)
                    k = 2 * i + m
                    a.activation(kt[:, :, k * P:(k + 1) * P], (t_ps[:, 0:2] if m == 0 else t_ps[:, 2:4]
                                 ).rearrange("p a b c -> p (a b) c"), ACT.Copy).then_inc(S["kcopy"], 1)

            def square(t, s):
                act.wait_ge(q_loaded[s], loaded(t, s))
                if not is0(t):
                    act.wait_ge(S["red"], t)
                a.activation(q_sq[:, :, :], q_raw[:, s], ACT.Square, scale=SC).then_inc(S["sq"], 1)

            def q_copy(t):
                act.wait_ge(S["qt"], t + 1)
                if not is0(t):
                    act.wait_ge(S["s"], t)
                a.activation(qt[:, :, :], q_ps[:, :, :], ACT.Copy).then_inc(S["qcopy"], 1)

            square(0, 0)
            q_copy(0)

            def tile(t, s):
                if not (isinstance(t, int) and t == NT - 1):
                    square(t + 1, 1 - s)
                act.wait_ge(S["nm"], t + 1)
                if not is0(t):
                    act.wait_ge(S["t"], t)
                for h in range(HM):
                    m = a.activation(pr[:, h], s_ps[:, h], ACT.Exp, bias=nm[:, h:h + 1], scale=SC,
                                     accum_out=rowsum[:, s, h:h + 1])
                m.then_inc(S["e"], 1)
                if not (isinstance(t, int) and t == NT - 1):
                    q_copy(t + 1)
                if not is0(t):
                    store(t - 1)

            def store(t):
                act.wait_ge(S["ot"], t + 1)
                if not is0(t):
                    act.wait_ge(stored, 16 * t)
                a.activation(ot[:, :], ot_ps[:, :, :], ACT.Copy).then_inc(S["otcopy"], 1)
                act.wait_ge(S["otcopy"], t + 1)
                dst = mix_t[t] if isinstance(t, int) else mix_t[ds(t, 1)]
                act.dma_start(dst[..., 12 * P:16 * P], ot[:, :]).then_inc(stored, 16)

            steps(act, tile)
            store(NT - 1)
            act.wait_ge(stored, 16 * NT)

        @block.vector
        def _(dve):
            v = nc.vector
            dve.wait_ge(S["ksq"], 1)
            v.reduce_sum(k_ss[:, :], k_sq[:, :, :, :], AX.X).then_inc(S["kred"], 1)
            dve.wait_ge(S["const"], 48)
            v.tensor_tensor(k_n[:, :, :, :], k_raw[:, :, :, :], bc(wk[:, :, :].unsqueeze(1), [P, NMT, HM, DM]),
                            ALU.mult).then_inc(S["kn"], 1)
            dve.wait_ge(S["kpow"], 2)
            dve.wait_ge(S["kn"], 1)
            kr = k_rstd[:, :].rearrange("p (t h) -> p t h", h=HM).unsqueeze(3)
            v.tensor_tensor(k_n[:, :, :, :], k_n[:, :, :, :], bc(kr, [P, NMT, HM, DM]), ALU.mult
                            ).then_inc(S["kn"], 1)

            def queries(t):
                dve.wait_ge(S["sq"], t + 1)
                if not is0(t):
                    dve.wait_ge(S["pow"], 2 * t)
                v.reduce_sum(q_ss[:, :], q_sq[:, :, :], AX.X).then_inc(S["red"], 1)
                dve.wait_ge(S["pow"], 2 * t + 2)
                dve.wait_ge(S["qw"], t + 1)
                if not is0(t):
                    dve.wait_ge(S["qt"], t)
                v.tensor_tensor(q_n[:, :, :], q_w[:, :, :], bc(q_rstd[:, :].unsqueeze(2), [P, HM, DM]),
                                ALU.mult).then_inc(S["qn"], 1)

            queries(0)

            def tile(t, s):
                dve.wait_ge(S["s"], t + 1)
                v.reduce_max(mx[:, :], s_ps[:, :, :], AX.X).then_inc(S["mx"], 1)
                dve.wait_ge(S["mx"], t + 1)
                if not is0(t):
                    dve.wait_ge(S["e"], t)
                v.tensor_scalar(nm[:, :], mx[:, :], -SC, None, ALU.mult).then_inc(S["nm"], 1)
                if not (isinstance(t, int) and t == NT - 1):
                    queries(t + 1)
                dve.wait_ge(S["t"], t + 1)
                if not is0(t):
                    dve.wait_ge(S["o"], t)
                for c in range(2):
                    m = v.tensor_copy(pt[:, 2 * c:2 * c + 2], t_ps[:, 2 * c:2 * c + 2])
                m.then_inc(S["tcopy"], 1)
                v.reciprocal(rec[:, :], rowsum[:, s]).then_inc(S["rec"], 1)
                dve.wait_ge(S["rec"], t + 1)
                dve.wait_ge(S["o"], t + 1)
                if not is0(t):
                    dve.wait_ge(S["ot"], t)
                v.tensor_tensor(o_sb[:, :, :], o_ps[:, :, :], bc(rec[:, :].unsqueeze(2), [P, HM, DM]),
                                ALU.mult).then_inc(S["oscaled"], 1)

            steps(dve, tile)

        @block.tensor
        def _(pe):
            T = nc.tensor
            pe.wait_ge(S["const"], 48)
            pe.wait_ge(S["kn"], 2)
            for k in range(NMT):
                if k >= 2:
                    pe.wait_ge(S["kcopy"], k - 1)
                for h in range(HM):
                    m = T.transpose(t_ps[:, 2 * (k % 2) + h // 2, h % 2], k_n[:, k, h], ident[:, :])
                m.then_inc(S["kt"], 1)
            pe.wait_ge(S["kcopy"], NMT)

            def q_t(t):
                pe.wait_ge(S["qn"], t + 1)
                if not is0(t):
                    pe.wait_ge(S["qcopy"], t)
                for h in range(HM):
                    m = T.transpose(q_ps[:, h], q_n[:, h], ident[:, :])
                m.then_inc(S["qt"], 1)

            def scores(t, tile_int):
                pe.wait_ge(S["qcopy"], t + 1)
                if not is0(t):
                    pe.wait_ge(S["e"], t)
                c0 = tile_int * NK
                for h in range(HM):
                    m = T.matmul(s_ps[:, h], qt[:, h], kt[:, h, c0:c0 + NK], start=True, stop=True)
                m.then_inc(S["s"], 1)

            def o_t(t):
                pe.wait_ge(S["oscaled"], t + 1)
                if not is0(t):
                    pe.wait_ge(S["otcopy"], t)
                for h in range(HM):
                    m = T.transpose(ot_ps[:, h], o_sb[:, h], ident[:, :])
                m.then_inc(S["ot"], 1)

            def seq(t):
                return int(isinstance(t, int) and t >= TP)

            q_t(0)
            scores(0, 0)

            def tile(t, s, last_of_prompt=False):
                end = isinstance(t, int) and t == NT - 1
                if not end:
                    q_t(t + 1)
                pe.wait_ge(S["e"], t + 1)
                if not is0(t):
                    pe.wait_ge(S["tcopy"], t)
                for h in range(HM):
                    for k in range(MT):
                        m = T.transpose(t_ps[:, h, k], pr[:, h, k * P:(k + 1) * P], ident[:, :])
                m.then_inc(S["t"], 1)
                if not end:
                    scores(t + 1, 1 if last_of_prompt else seq(t))
                if not is0(t):
                    o_t(t - 1)
                pe.wait_ge(S["tcopy"], t + 1)
                for h in range(HM):
                    for k in range(MT):
                        m = T.matmul(o_ps[:, h], pt[:, h, k], v_sb[:, MT * seq(t) + k, h],
                                     start=(k == 0), stop=(k == MT - 1))
                m.then_inc(S["o"], 1)

            for t in range(2):
                tile(t, t)
            with pe.Fori(1, TP // 2 - 1) as j:
                for s in range(2):
                    tile(2 * j + s, s)
            for t in range(TP - 2, NT):
                tile(t, t % 2, t == TP - 1)
            o_t(NT - 1)


def ssm_convolution(nc, xbc_t, conv_dram, xbc_c):
    TAPS, NCH = 5, XBC // P
    PADW = TOK + 6
    SPAN = TOK + 2
    S0, S1 = 2, SEQ + 4
    with ExitStack() as ctx:
        b = Bufs(nc, ctx)
        taps = b.sb("cv_taps", [P, NCH, TAPS + 1])
        x = b.sb("cv_x", [P, 2, PADW])
        y = b.sb("cv_y", [P, 2, SPAN])
        act_y = b.sb("cv_act", [P, 2, SPAN])
        const_loaded, zeroed, tapped = b.sem("cv_const"), b.sem("cv_zero"), b.sem("cv_tap")
        silued = b.sem("cv_silu")
        x_loaded, stored = b.sems("cv_xl", 2), b.sems("cv_st", 2)
        block = b.block()

        @block.sync
        def _(sp):
            sp.dma_start(taps[:, :, :], conv_dram).then_inc(const_loaded, 16)
            sp.wait_ge(zeroed, 1)

            def load(c, s, first=False):
                if not first:
                    sp.wait_ge(tapped, TAPS * (c - 1))
                rows = slice(c * P, (c + 1) * P) if isinstance(c, int) else ds(c * P, P)
                sp.dma_start(x[:, s, S0:S0 + SEQ], xbc_t[rows, 0:SEQ]).then_inc(x_loaded[s], 16)
                sp.dma_start(x[:, s, S1:S1 + DEC], xbc_t[rows, SEQ:TOK]).then_inc(x_loaded[s], 16)

            for s in range(2):
                load(s, s, True)
            with sp.Fori(1, NCH // 2) as j:
                for s in range(2):
                    load(2 * j + s, s)

        @block.vector
        def _(dve):
            nc.vector.memset(x[:, :, :], 0.0).then_inc(zeroed, 1)
            dve.wait_ge(const_loaded, 16)

            def conv(c, s, j, first=False):
                dve.wait_ge(x_loaded[s], 32 * j + 32)
                if not first:
                    dve.wait_ge(silued, c - 1)
                w = (lambda k: taps[:, c:c + 1, k]) if isinstance(c, int) else (lambda k: taps[:, ds(c, 1), k])
                nc.vector.tensor_scalar(y[:, s], x[:, s, 0:SPAN], w(0), w(TAPS), ALU.mult,
                                        ALU.add).then_inc(tapped, 1)
                for k in range(1, TAPS):
                    dve.wait_ge(tapped, TAPS * c + k)
                    nc.vector.scalar_tensor_tensor(y[:, s], x[:, s, k:k + SPAN], w(k), y[:, s],
                                                   ALU.mult, ALU.add).then_inc(tapped, 1)

            for s in range(2):
                conv(s, s, 0, True)
            with dve.Fori(1, NCH // 2) as j:
                for s in range(2):
                    conv(2 * j + s, s, j)

        @block.scalar
        def _(act):
            def silu(c, s, j, first=False):
                act.wait_ge(tapped, TAPS * (c + 1))
                if not first:
                    act.wait_ge(stored[s], 32 * j)
                nc.scalar.activation(act_y[:, s], y[:, s], ACT.Silu).then_inc(silued, 1)
                act.wait_ge(silued, c + 1)
                col = slice(c * P, (c + 1) * P) if isinstance(c, int) else ds(c * P, P)
                dst = xbc_c.rearrange("t p n -> p t n")
                act.dma_start(dst[:, 0:TP, col], act_y[:, s, 0:SEQ].rearrange("p (t n) -> p t n", n=P)
                              ).then_inc(stored[s], 16)
                act.dma_start(dst[:, TP:NT, col], act_y[:, s, SEQ + 2:SPAN].rearrange("p (t n) -> p t n", n=P)
                              ).then_inc(stored[s], 16)

            for s in range(2):
                silu(s, s, 0, True)
            with act.Fori(1, NCH // 2) as j:
                for s in range(2):
                    silu(2 * j + s, s, j)
            for s in range(2):
                act.wait_ge(stored[s], 32 * (NCH // 2))


def ssm_steps_sizes(nc, dt_t, ident_dram, tri_dram, small, R):
    H2 = 2 * NS
    W = NT * H2
    with ExitStack() as ctx:
        b = Bufs(nc, ctx)
        raw = b.sb("sz_raw", [H2, TOK])
        ident = b.sb("sz_ident", [P, P])
        ones = b.sb("sz_ones", [P, P])
        bias = b.sb("sz_bias", [P, 1, H2])
        a_log = b.sb("sz_alog", [P, 1, H2])
        a_neg = b.sb("sz_aneg", [P, 1, H2])
        v1 = b.sb("sz_v1", [P, NT, H2])
        v2 = b.sb("sz_v2", [P, NT, H2])
        v3 = b.sb("sz_v3", [P, NT, H2])
        v4 = b.sb("sz_v4", [P, NT, H2])
        t_ps = b.ps("sz_tps", [P, NT, H2])
        c_ps = b.ps("sz_cps", [P, NT, H2])
        tot_ps = b.ps("sz_tot", [P, NT, H2])
        loaded, turned, step, summed = b.sem("sz_l"), b.sem("sz_t"), b.sem("sz_step"), b.sem("sz_sum")
        act_done, ones_set, want_exp = b.sem("sz_act"), b.sem("sz_ones_s"), b.sem("sz_want")
        block = b.block()
        dt, acs, e_acs, e_tot, dec = R["dt"], R["acs"], R["e_acs"], R["e_tot"], R["dec"]
        a_sb, tri = R["a"], R["tri"]

        @block.sync
        def _(sp):
            for dst, src in ((raw[:, :], dt_t), (ident[:, :], ident_dram), (tri[:, :, :], tri_dram),
                             (bias[:, 0], small["ssm_dt_bias"].broadcast_to([P, H2])),
                             (a_log[:, 0], small["ssm_A_log"].broadcast_to([P, H2]))):
                sp.dma_start(dst, src).then_inc(loaded, 16)

        @block.tensor
        def _(pe):
            pe.wait_ge(loaded, 80)
            for t in range(NT):
                m = nc.tensor.transpose(t_ps[:, t], raw[:, t * P:(t + 1) * P], ident[0:H2, 0:H2])
            m.then_inc(turned, 1)
            pe.wait_ge(ones_set, 1)
            pe.wait_ge(want_exp, 2)
            for d in range(2):
                nc.tensor.matmul(c_ps[:, :, d * NS:(d + 1) * NS], tri[:, d],
                                 a_sb[:, :, d * NS:(d + 1) * NS], start=True, stop=True)
            nc.tensor.matmul(tot_ps[:, :, :], ones[:, :], a_sb[:, :, :], start=True, stop=True
                             ).then_inc(summed, 1)

        @block.vector
        def _(dve):
            v = nc.vector
            n = [0]

            def then(ins):
                n[0] += 1
                ins.then_inc(step, 1)
                dve.wait_ge(step, n[0])

            v.memset(ones[:, :], 1.0).then_inc(ones_set, 1)
            dve.wait_ge(loaded, 80)
            dve.wait_ge(turned, 1)
            then(v.tensor_tensor(v1[:, :, :], t_ps[:, :, :], bc(bias[:, :, :], [P, NT, H2]), ALU.add))
            then(v.tensor_scalar(v2[:, :, :], v1[:, :, :], -1.0, None, ALU.mult))
            then(v.tensor_tensor(v3[:, :, :], v1[:, :, :], v2[:, :, :], ALU.min))
            v.tensor_scalar(v1[:, :, :], v1[:, :, :], 0.0, None, ALU.max).then_inc(want_exp, 1)
            dve.wait_ge(act_done, 2)
            then(v.tensor_scalar(v2[:, :, :], v4[:, :, :], 2.0, None, ALU.add))
            then(v.reciprocal(v3[:, :, :], v2[:, :, :]))
            then(v.tensor_tensor(v4[:, :, :], v4[:, :, :], v3[:, :, :], ALU.mult))
            then(v.tensor_tensor(v2[:, :, :], v4[:, :, :], v4[:, :, :], ALU.mult))
            then(v.tensor_scalar(v3[:, :, :], v2[:, :, :], 1.0 / 17, 1.0 / 15, ALU.mult, ALU.add))
            for k in (13, 11, 9, 7, 5, 3, 1):
                then(v.tensor_tensor(v3[:, :, :], v3[:, :, :], v2[:, :, :], ALU.mult))
                then(v.tensor_scalar(v3[:, :, :], v3[:, :, :], 1.0 / k, None, ALU.add))
            then(v.tensor_tensor(v3[:, :, :], v3[:, :, :], v4[:, :, :], ALU.mult))
            then(v.scalar_tensor_tensor(dt[:, :, :], v3[:, :, :], 2.0, v1[:, :, :], ALU.mult, ALU.add))
            then(v.tensor_scalar(a_neg[:, :, :], a_neg[:, :, :], -1.0, None, ALU.mult))
            v.tensor_tensor(a_sb[:, :, :], dt[:, :, :], bc(a_neg[:, :, :], [P, NT, H2]), ALU.mult
                            ).then_inc(want_exp, 1)
            dve.wait_ge(summed, 1)
            then(v.tensor_copy(acs[:, :, :], c_ps[:, :, :]))
            v.tensor_tensor(v1[:, :, :], tot_ps[:, :, :], acs[:, :, :], ALU.subtract).then_inc(want_exp, 1)
            dve.wait_ge(act_done, 5)
            v.tensor_tensor(dec[:, :, :], v2[:, :, :], dt[:, :, :], ALU.mult).then_inc(step, 1)

        @block.scalar
        def _(act):
            a = nc.scalar
            act.wait_ge(loaded, 80)
            a.activation(a_neg[:, :, :], a_log[:, :, :], ACT.Exp).then_inc(act_done, 1)
            act.wait_ge(want_exp, 1)
            a.activation(v4[:, :, :], v3[:, :, :], ACT.Exp).then_inc(act_done, 1)
            act.wait_ge(want_exp, 3)
            a.activation(e_acs[:, :, :], acs[:, :, :], ACT.Exp).then_inc(act_done, 1)
            a.activation(e_tot[:, :, :], tot_ps[:, :, :], ACT.Exp).then_inc(act_done, 1)
            a.activation(v2[:, :, :], v1[:, :, :], ACT.Exp).then_inc(act_done, 1)


def ssm_backward(nc, xbc_c, ident_dram, R):
    XW = NS * PS
    with ExitStack() as ctx:
        b = Bufs(nc, ctx)
        ident = b.sb("sb_ident", [P, P])
        xc = b.sb("sb_xc", [P, 2, XBC])
        x_dec = b.sb("sb_xdec", [P, NS, PS])
        b_tok = b.sb("sb_btok", [P, NG, ST])
        state = b.sb("sb_state", [P, NS, PS])
        scaled = b.sb("sb_scaled", [P, NS, PS])
        x_ps = b.ps("sb_xps", [P, NS, PS])
        b_ps = b.ps("sb_bps", [P, NG, ST])
        s_ps = b.ps("sb_sps", [P, NS, PS])
        y_ps = b.ps("sb_yps", [P, NS, PS])
        S = {n: b.sem(f"sb_s_{n}") for n in ("const", "turn", "x", "b", "off", "st", "y", "h", "zero", "sp_ready", "dve_ready")}
        loaded = b.sems("sb_l", 2)
        block = b.block()
        y_back, e_acs, e_tot, dec = R["y_back"], R["e_acs"], R["e_tot"], R["dec"]

        def order(engine, body, reset=None):
            if reset:
                reset(0)
            for s in range(2):
                body(s, s, NT - 1 - s, s == 0)
            if reset:
                reset(1)
            with engine.Fori(1, NT // 2) as j:
                for s in range(2):
                    body(2 * j + s, s, NT - 1 - (2 * j + s), False)

        def at(buf, t, h0=None, n=None):
            tt = buf[:, t:t + 1] if isinstance(t, int) else buf[:, ds(t, 1)]
            return tt

        @block.sync
        def _(sp):
            sp.dma_start(ident[:, :], ident_dram).then_inc(S["const"], 16)

            def load(i, s, t, first):
                if not isinstance(i, int):
                    sp.wait_ge(S["off"], i - 1)
                sp.sem_inc(S["sp_ready"], 1)
                sp.dma_start(xc[:, s], xbc_c[t] if isinstance(t, int) else xbc_c[ds(t, 1)]
                             ).then_inc(loaded[s], 16)

            order(sp, load)

        def loaded_value(i, s):
            return 16 if isinstance(i, int) else 8 * (i - s) + 16

        @block.tensor
        def _(pe):
            T = nc.tensor
            pe.wait_ge(S["const"], 16)

            def body(i, s, t, first):
                pe.wait_ge(loaded[s], loaded_value(i, s))
                if not first:
                    pe.wait_ge(S["x"], i)
                    pe.wait_ge(S["b"], i)
                for c in range(4):
                    T.transpose(x_ps[:, 2 * c:2 * c + 2], xc[:, s, c * P:(c + 1) * P], ident[:, :])
                for g in range(NG):
                    m = T.transpose(b_ps[:, g], xc[:, s, (4 + g) * P:(5 + g) * P], ident[:, :])
                m.then_inc(S["turn"], 1)
                if first:
                    pe.wait_ge(S["zero"], 1)
                else:
                    pe.wait_ge(S["h"], 2 * i)
                    pe.wait_ge(S["y"], i)
                for g in range(NG):
                    m = T.matmul(y_ps[:, 4 * g:4 * g + 4], xc[:, s, (6 + g) * P:(7 + g) * P],
                                 state[:, 4 * g:4 * g + 4], start=True, stop=True)
                m.then_inc(S["off"], 1)
                pe.wait_ge(S["x"], i + 1)
                pe.wait_ge(S["b"], i + 1)
                for g in range(NG):
                    m = T.matmul(s_ps[:, 4 * g:4 * g + 4], b_tok[:, g], x_dec[:, 4 * g:4 * g + 4],
                                 start=True, stop=True)
                m.then_inc(S["st"], 1)

            def reset(k):
                if k:
                    pe.wait_ge(S["zero"], 2)

            order(pe, body, reset)

        @block.scalar
        def _(act):
            def body(i, s, t, first):
                act.wait_ge(S["turn"], i + 1)
                if not first:
                    act.wait_ge(S["st"], i)
                nc.scalar.activation(b_tok[:, :, :], b_ps[:, :, :], ACT.Copy).then_inc(S["b"], 1)

            order(act, body)

        @block.vector
        def _(dve):
            v = nc.vector

            def factor(buf, t):
                return bc(at(buf, t)[:, 0, NS:2 * NS].unsqueeze(2), [P, NS, PS])

            def body(i, s, t, first):
                dve.wait_ge(S["turn"], i + 1)
                if not first:
                    dve.wait_ge(S["st"], i)
                dve.sem_inc(S["dve_ready"], 1)
                v.tensor_tensor(x_dec[:, :, :], x_ps[:, :, :], factor(dec, t), ALU.mult).then_inc(S["x"], 1)
                dve.wait_ge(S["off"], i + 1)
                yb = y_back[:, t] if isinstance(t, int) else y_back[:, ds(t, 1)]
                yb = yb.rearrange("p (h q) -> p h q", q=PS) if isinstance(t, int) else \
                    yb.rearrange("p o (h q) -> p (o h) q", q=PS)
                v.tensor_tensor(yb, y_ps[:, :, :], factor(e_acs, t), ALU.mult).then_inc(S["y"], 1)
                v.tensor_tensor(scaled[:, :, :], state[:, :, :], factor(e_tot, t), ALU.mult).then_inc(S["h"], 1)
                dve.wait_ge(S["st"], i + 1)
                dve.wait_ge(S["h"], 2 * i + 1)
                v.tensor_tensor(state[:, :, :], scaled[:, :, :], s_ps[:, :, :], ALU.add).then_inc(S["h"], 1)

            def reset(k):
                if k:
                    dve.wait_ge(S["h"], 4)
                v.memset(state[:, :, :], 0.0).then_inc(S["zero"], 1)
                dve.wait_ge(S["zero"], k + 1)

            order(dve, body, reset)


def ssm_forward(nc, proj, xbc_c, ident_dram, small, R, mix_t):
    XW = NS * PS
    with ExitStack() as ctx:
        b = Bufs(nc, ctx)
        ident = b.sb("sf_ident", [P, P])
        wn = b.sb("sf_wn", [P, XW])
        dsk = b.sb("sf_dskip", [P, NS])
        half = b.sb("sf_half", [P, 1])
        eps = b.sb("sf_eps", [P, 1])
        z = b.sb("sf_z", [P, 2, XW])
        zs = b.sb("sf_zs", [P, XW])
        zr = b.sb("sf_zr", [P, XW])
        xc = b.sb("sf_xc", [P, 2, XBC])
        b_tok = b.sb("sf_btok", [P, NG, ST])
        x_tok = b.sb("sf_xtok", [P, NS, PS])
        x_dec = b.sb("sf_xdec", [P, NS, PS])
        x_dt = b.sb("sf_xdt", [P, 2, NS, PS])
        state = b.sb("sf_state", [P, NS, PS])
        scaled = b.sb("sf_scaled", [P, NS, PS])
        cb = b.sb("sf_cb", [P, 2, NG, 1, P])
        a_tri = b.sb("sf_atri", [P, 2, NS, P])
        diff = b.sb("sf_diff", [P, 2, NS, P])
        m_t = b.sb("sf_mt", [P, 2, NS, P])
        y = b.sb("sf_y", [P, XW])
        y2 = b.sb("sf_y2", [P, XW])
        sq = b.sb("sf_sq", [P, XW])
        ms = b.sb("sf_ms", [P, 1])
        mse = b.sb("sf_mse", [P, 1])
        rstd = b.sb("sf_rstd", [P, 1])
        yn = b.sb("sf_yn", [P, XW])
        ot = b.sb("sf_ot", [P, XW])
        ones = b.sb("sf_ones", [P, P])
        x_ps = b.ps("sf_xps", [P, NS, PS])
        m_ps = b.ps("sf_mps", [P, 4, P])
        s_ps = b.ps("sf_sps", [P, NS, PS])
        y_ps = b.ps("sf_yps", [P, NS, PS])
        d_ps = b.ps("sf_dps", [P, NS, P])
        g_ps = b.ps("sf_gps", [P, NS, PS])
        t_ps = b.ps("sf_tps", [P, 4, P])
        S = {n: b.sem(f"sf_s_{n}") for n in (
            "const", "half", "ones", "turn", "xcopy", "bcopy", "xd", "off", "st", "h", "zero", "cb", "cbm", "atri",
            "rows", "diff", "clamp", "e", "m", "diag", "y", "z", "zr", "sq", "pow", "yn", "tn", "tcopy", "xdt")}
        loaded, z_loaded = b.sems("sf_l", 2), b.sems("sf_zl", 2)
        stored = b.sem("sf_stored")
        block = b.block()
        y_back, e_acs, e_tot, dec, dt, acs, a_sb, tri = (
            R[k] for k in ("y_back", "e_acs", "e_tot", "dec", "dt", "acs", "a", "tri"))

        def order(engine, body, reset=None):
            if reset:
                reset(0)
            for s in range(2):
                body(s, s, s == 0)
            with engine.Fori(1, TP // 2) as j:
                for s in range(2):
                    body(2 * j + s, s, False)
            if reset:
                reset(1)
            for s in range(2):
                body(TP + s, s, False)

        def loaded_value(t, s):
            return 16 * (t // 2 + 1) if isinstance(t, int) else 8 * (t - s) + 16

        def row(buf, t, lo_, hi_):
            r = buf[:, t:t + 1] if isinstance(t, int) else buf[:, ds(t, 1)]
            return r[:, 0, lo_:hi_].unsqueeze(2)

        @block.sync
        def _(sp):
            for dst, src in ((ident[:, :], ident_dram), (wn[:, :], small["ssm_norm_w"].broadcast_to([P, XW])),
                             (dsk[:, :], small["ssm_D"].broadcast_to([P, NS]))):
                sp.dma_start(dst, src).then_inc(S["const"], 16)

            def load(t, s, first):
                if not (isinstance(t, int) and t < 2):
                    sp.wait_ge(S["cb"], t - 1)
                sp.dma_start(xc[:, s], xbc_c[t] if isinstance(t, int) else xbc_c[ds(t, 1)]
                             ).then_inc(loaded[s], 16)
                if not (isinstance(t, int) and t < 2):
                    sp.wait_ge(S["y"], 6 * (t - 1))
                rows = slice(t * P, (t + 1) * P) if isinstance(t, int) else ds(t * P, P)
                sp.dma_start(z[:, s], proj[rows, 1536:2048]).then_inc(z_loaded[s], 16)

            order(sp, load)

        @block.tensor
        def _(pe):
            T = nc.tensor
            pe.wait_ge(S["const"], 48)
            pe.wait_ge(S["ones"], 1)

            def body(t, s, first):
                pe.wait_ge(loaded[s], loaded_value(t, s))
                if not first:
                    pe.wait_ge(S["xcopy"], t)
                    pe.wait_ge(S["bcopy"], t)
                    pe.wait_ge(S["cbm"], 2 * t)
                for c in range(4):
                    T.transpose(x_ps[:, 2 * c:2 * c + 2], xc[:, s, c * P:(c + 1) * P], ident[:, :])
                for g in range(NG):
                    m = T.transpose(m_ps[:, g], xc[:, s, (4 + g) * P:(5 + g) * P], ident[:, :])
                m.then_inc(S["turn"], 1)
                if first:
                    pe.wait_ge(S["zero"], 1)
                else:
                    pe.wait_ge(S["h"], 2 * t)
                    pe.wait_ge(S["y"], 6 * t)
                for g in range(NG):
                    m = T.matmul(y_ps[:, 4 * g:4 * g + 4], xc[:, s, (6 + g) * P:(7 + g) * P],
                                 state[:, 4 * g:4 * g + 4], start=True, stop=True)
                m.then_inc(S["off"], 1)
                pe.wait_ge(S["bcopy"], t + 1)
                for g in range(NG):
                    m = T.matmul(m_ps[:, 2 + g], xc[:, s, (4 + g) * P:(5 + g) * P],
                                 xc[:, s, (6 + g) * P:(7 + g) * P], start=True, stop=True)
                m.then_inc(S["cb"], 1)
                pe.wait_ge(S["xd"], t + 1)
                for g in range(NG):
                    m = T.matmul(s_ps[:, 4 * g:4 * g + 4], b_tok[:, g], x_dec[:, 4 * g:4 * g + 4],
                                 start=True, stop=True)
                m.then_inc(S["st"], 1)
                for d in range(2):
                    pe.wait_ge(S["atri"], 2 * t + d + 1)
                    if not (first and d == 0):
                        pe.wait_ge(S["diff"], 2 * t + d)
                    for g in range(NG):
                        m = T.matmul(d_ps[:, 4 * g:4 * g + 4], ones[:, :], a_tri[:, d, 4 * g:4 * g + 4],
                                     start=True, stop=True)
                    m.then_inc(S["rows"], 1)
                pe.wait_ge(S["xdt"], 2 * t + 2)
                pe.wait_ge(S["m"], 2 * t + 2)
                for h in range(NS):
                    for d in range(2):
                        m = T.matmul(g_ps[:, h], m_t[:, d, h], x_dt[:, d, h], start=(d == 0), stop=(d == 1))
                m.then_inc(S["diag"], 1)
                pe.wait_ge(S["yn"], t + 1)
                if not first:
                    pe.wait_ge(S["tcopy"], t)
                for c in range(4):
                    m = T.transpose(t_ps[:, c], yn[:, c * P:(c + 1) * P], ident[:, :])
                m.then_inc(S["tn"], 1)

            def reset(k):
                if k:
                    pe.wait_ge(S["zero"], 2)

            order(pe, body, reset)

        @block.gpsimd
        def _(pool):
            g = nc.gpsimd
            g.memset(half[:, :], -0.5).then_inc(S["half"], 1)
            g.memset(eps[:, :], EPS).then_inc(S["half"], 1)
            g.memset(ones[:, :], 1.0).then_inc(S["ones"], 1)
            pool.wait_ge(S["half"], 2)

            def body(t, s, first):
                for d in range(2):
                    if not first:
                        pool.wait_ge(S["rows"], 2 * t)
                    g.tensor_tensor(a_tri[:, d], bc(row(a_sb, t, d * NS, (d + 1) * NS), [P, NS, P]),
                                    bc(tri[:, d:d + 1, :], [P, NS, P]), ALU.mult).then_inc(S["atri"], 1)
                pool.wait_ge(S["xcopy"], t + 1)
                for d in range(2):
                    if not first:
                        pool.wait_ge(S["diag"], t)
                    g.tensor_tensor(x_dt[:, d], x_tok[:, :, :], bc(row(dt, t, d * NS, (d + 1) * NS), [P, NS, PS]),
                                    ALU.mult).then_inc(S["xdt"], 1)
                pool.wait_ge(S["sq"], t + 1)
                g.tensor_tensor(mse[:, :], ms[:, :], eps[:, :], ALU.add).then_inc(S["pow"], 1)
                pool.wait_ge(S["pow"], 2 * t + 1)
                g.tensor_tensor(rstd[:, :], mse[:, :], half[:, :], ALU.pow).then_inc(S["pow"], 1)

            order(pool, body)

        @block.scalar
        def _(act):
            a = nc.scalar

            def body(t, s, first):
                act.wait_ge(S["turn"], t + 1)
                if not first:
                    act.wait_ge(S["st"], t)
                    act.wait_ge(S["y"], 6 * t)
                    act.wait_ge(S["xdt"], 2 * t)
                    act.wait_ge(S["xd"], t)
                a.activation(b_tok[:, :, :], m_ps[:, 0:2], ACT.Copy).then_inc(S["bcopy"], 1)
                a.activation(x_tok[:, :, :], x_ps[:, :, :], ACT.Copy).then_inc(S["xcopy"], 1)
                act.wait_ge(z_loaded[s], loaded_value(t, s))
                a.activation(zs[:, :], z[:, s], ACT.Exp, scale=-1.0).then_inc(S["z"], 1)
                for d in range(2):
                    act.wait_ge(S["clamp"], 2 * t + d + 1)
                    a.activation(diff[:, d], diff[:, d], ACT.Exp).then_inc(S["e"], 1)
                act.wait_ge(S["y"], 6 * t + 6)
                a.activation(sq[:, :], y[:, :], ACT.Square, scale=XW ** -0.5, accum_out=ms[:, :]).then_inc(S["sq"], 1)
                act.wait_ge(S["tn"], t + 1)
                if not first:
                    act.wait_ge(stored, 16 * t)
                a.activation(ot[:, :], t_ps[:, :, :], ACT.Copy).then_inc(S["tcopy"], 1)
                act.wait_ge(S["tcopy"], t + 1)
                dst = mix_t[t] if isinstance(t, int) else mix_t[ds(t, 1)]
                act.dma_start(dst[..., 8 * P:12 * P], ot[:, :]).then_inc(stored, 16)

            order(act, body)
            act.wait_ge(stored, 16 * NT)

        @block.vector
        def _(dve):
            v = nc.vector
            dve.wait_ge(S["const"], 48)

            def hp(ap):
                return ap.rearrange("p (h q) -> p h q", q=PS)

            def body(t, s, first):
                dve.wait_ge(S["xcopy"], t + 1)
                if not first:
                    dve.wait_ge(S["st"], t)
                v.tensor_tensor(x_dec[:, :, :], x_tok[:, :, :], bc(row(dec, t, 0, NS), [P, NS, PS]),
                                ALU.mult).then_inc(S["xd"], 1)
                dve.wait_ge(S["off"], t + 1)
                if not first:
                    dve.wait_ge(S["sq"], t)
                v.tensor_tensor(hp(y[:, :]), y_ps[:, :, :], bc(row(e_acs, t, 0, NS), [P, NS, PS]),
                                ALU.mult).then_inc(S["y"], 1)
                v.tensor_tensor(hp(y2[:, :]), x_tok[:, :, :], bc(dsk[:, :].unsqueeze(2), [P, NS, PS]),
                                ALU.mult).then_inc(S["y"], 1)
                dve.wait_ge(S["y"], 6 * t + 2)
                yb = y_back[:, t] if isinstance(t, int) else y_back[:, ds(t, 1)].rearrange("p o n -> p (o n)")
                v.tensor_tensor(y2[:, :], y2[:, :], yb, ALU.add).then_inc(S["y"], 1)
                dve.wait_ge(S["y"], 6 * t + 3)
                v.tensor_tensor(y[:, :], y[:, :], y2[:, :], ALU.add).then_inc(S["y"], 1)
                v.tensor_tensor(scaled[:, :, :], state[:, :, :], bc(row(e_tot, t, 0, NS), [P, NS, PS]),
                                ALU.mult).then_inc(S["h"], 1)
                dve.wait_ge(S["st"], t + 1)
                dve.wait_ge(S["h"], 2 * t + 1)
                v.tensor_tensor(state[:, :, :], scaled[:, :, :], s_ps[:, :, :], ALU.add).then_inc(S["h"], 1)
                dve.wait_ge(S["cb"], t + 1)
                for d in range(2):
                    if not first:
                        pass
                    v.tensor_tensor(cb[:, d, :, 0], m_ps[:, 2:4], bc(tri[:, d:d + 1, :], [P, NG, P]),
                                    ALU.mult).then_inc(S["cbm"], 1)
                for d in range(2):
                    dve.wait_ge(S["rows"], 2 * t + d + 1)
                    for g in range(NG):
                        m = v.tensor_tensor(diff[:, d, 4 * g:4 * g + 4], d_ps[:, 4 * g:4 * g + 4],
                                            bc(row(acs, t, d * NS + 4 * g, d * NS + 4 * g + 4), [P, 4, P]),
                                            ALU.subtract)
                    m.then_inc(S["diff"], 1)
                    dve.wait_ge(S["diff"], 2 * t + d + 1)
                    v.tensor_scalar(diff[:, d], diff[:, d], 0.0, None, ALU.min).then_inc(S["clamp"], 1)
                dve.wait_ge(S["cbm"], 2 * t + 2)
                for d in range(2):
                    dve.wait_ge(S["e"], 2 * t + d + 1)
                    if not first:
                        dve.wait_ge(S["diag"], t)
                    v.tensor_tensor(m_t[:, d].rearrange("p (g h) l -> p g h l", g=NG),
                                    diff[:, d].rearrange("p (g h) l -> p g h l", g=NG),
                                    bc(cb[:, d], [P, NG, NS // NG, P]), ALU.mult).then_inc(S["m"], 1)
                dve.wait_ge(S["z"], t + 1)
                v.tensor_scalar(zr[:, :], zs[:, :], 1.0, None, ALU.add).then_inc(S["zr"], 1)
                dve.wait_ge(S["zr"], 3 * t + 1)
                v.reciprocal(zr[:, :], zr[:, :]).then_inc(S["zr"], 1)
                dve.wait_ge(S["zr"], 3 * t + 2)
                v.tensor_tensor(zr[:, :], zr[:, :], z[:, s], ALU.mult).then_inc(S["zr"], 1)
                dve.wait_ge(S["diag"], t + 1)
                dve.wait_ge(S["y"], 6 * t + 4)
                v.tensor_tensor(hp(y[:, :]), hp(y[:, :]), g_ps[:, :, :], ALU.add).then_inc(S["y"], 1)
                dve.wait_ge(S["y"], 6 * t + 5)
                dve.wait_ge(S["zr"], 3 * t + 3)
                v.tensor_tensor(y[:, :], y[:, :], zr[:, :], ALU.mult).then_inc(S["y"], 1)
                dve.wait_ge(S["y"], 6 * t + 6)
                dve.wait_ge(S["pow"], 2 * t + 2)
                if not first:
                    dve.wait_ge(S["tn"], t)
                v.scalar_tensor_tensor(yn[:, :], y[:, :], rstd[:, :], wn[:, :], ALU.mult, ALU.mult
                                       ).then_inc(S["yn"], 1)

            def reset(k):
                if k:
                    dve.wait_ge(S["h"], 2 * TP)
                v.memset(state[:, :, :], 0.0).then_inc(S["zero"], 1)
                dve.wait_ge(S["zero"], k + 1)

            order(dve, body, reset)


def ssm(nc, proj, xbc_t, dt_t, ident, tri, conv_dram, small, mix_t, xbc_c):
    ssm_convolution(nc, xbc_t, conv_dram, xbc_c)
    with ExitStack() as ctx:
        b = Bufs(nc, ctx)
        R = {k: b.sb(f"ss_{k}", [P, NT, 2 * NS]) for k in ("dt", "acs", "e_acs", "e_tot", "dec", "a")}
        R["tri"] = b.sb("ss_tri", [P, 2, P])
        R["y_back"] = b.sb("ss_yback", [P, NT, NS * PS])
        ssm_steps_sizes(nc, dt_t, ident, tri, small, R)
        ssm_backward(nc, xbc_c, ident, R)
        ssm_forward(nc, proj, xbc_c, ident, small, R, mix_t)


def out_projection(nc, w_out, mix_t, x_dram, x1):
    with ExitStack() as ctx:
        b = Bufs(nc, ctx)
        raw = b.sb("wo_raw", [P, 2, D])
        w_hi = b.sb("wo_hi", [P, 2, KC, D], F32R)
        w_lo = b.sb("wo_lo", [P, 2, KC, D], F32R)
        mix = b.sb("wo_mix", [P, 2, KC, P])
        m_hi = b.sb("wo_mhi", [P, 2, KC, P], F32R)
        m_lo = b.sb("wo_mlo", [P, 2, KC, P], F32R)
        bank = b.ps("wo_bank", [P, 2, 2, PW])
        x_loaded = b.sems("wo_xl", 2)
        raw_loaded = b.sems("wo_rawl", 2)
        mix_loaded = b.sems("wo_mixl", 2)
        w_hi_done, w_split = b.sem("wo_whid"), b.sem("wo_wsplit")
        m_hi_done, m_split = b.sem("wo_mhid"), b.sem("wo_msplit")
        multiplied, added = b.sem("wo_mm"), b.sem("wo_added")
        block = b.block()

        @block.sync
        def _(sp):
            for s in range(2):
                sp.dma_start(raw[:, s], w_out[s * P:(s + 1) * P, :]).then_inc(raw_loaded[s], 16)

            def chunks(first, end):
                with sp.Fori(first, end) as j:
                    for s in range(2):
                        sp.wait_ge(w_split, 2 * j + s - 1)
                        sp.dma_start(raw[:, s], w_out[ds((2 * j + s) * P, P), :]).then_inc(raw_loaded[s], 16)

            x_v = x_dram.rearrange("(t p) d -> p t d", p=P)
            chunks(1, KC // 2)
            sp.dma_start(x1[:, 0:2, :], x_v[:, 0:2, :]).then_inc(x_loaded[0], 16)
            sp.dma_start(x1[:, 2:NT, :], x_v[:, 2:NT, :]).then_inc(x_loaded[1], 16)
            chunks(KC // 2, KC)

        @block.gpsimd
        def _(pool):
            def load(h, t, s, first=False):
                if not first:
                    pool.wait_ge(m_split, h * NT + t - 1)
                src = mix_t[t] if isinstance(t, int) else mix_t[ds(t, 1)]
                pool.dma_start(mix[:, s], src[..., h * KC * P:(h + 1) * KC * P]).then_inc(mix_loaded[s], 16)

            for s in range(2):
                load(0, s, s, True)
            with pool.Fori(1, NT // 2) as j:
                for s in range(2):
                    load(0, 2 * j + s, s)
            with pool.Fori(0, NT // 2) as j:
                for s in range(2):
                    load(1, 2 * j + s, s)

        @block.scalar
        def _(act):
            def high(j, s, first=False):
                act.wait_ge(mix_loaded[s], 16 * j + 16)
                if not first:
                    act.wait_ge(multiplied, 2 * j + s - 1)
                nc.scalar.activation(m_hi[:, s], mix[:, s], ACT.Copy).then_inc(m_hi_done, 1)

            for s in range(2):
                high(0, s, True)
            with act.Fori(1, NT) as j:
                for s in range(2):
                    high(j, s)

        @block.vector
        def _(dve):
            def weights(half, k, s):
                n = half * KC + k
                kk = slice(k, k + 1) if isinstance(k, int) else ds(k, 1)
                dve.wait_ge(raw_loaded[s], 8 * (n - s) + 16)
                nc.vector.tensor_copy(w_hi[:, half, kk], raw[:, s]).then_inc(w_hi_done, 1)
                dve.wait_ge(w_hi_done, n + 1)
                nc.vector.tensor_tensor(w_lo[:, half, kk], raw[:, s], w_hi[:, half, kk].bitcast(FP32),
                                        ALU.subtract).then_inc(w_split, 1)

            def low(n, s):
                dve.wait_ge(m_hi_done, n + 1)
                nc.vector.tensor_tensor(m_lo[:, s], mix[:, s], m_hi[:, s].bitcast(FP32),
                                        ALU.subtract).then_inc(m_split, 1)

            def add(n, t, s):
                dve.wait_ge(multiplied, n + 1)
                x = x1[:, t, :] if isinstance(t, int) else x1[:, ds(t, 1), :]
                nc.vector.tensor_tensor(x, x, bank[:, s], ALU.add).then_inc(added, 1)

            for s in range(2):
                low(s, s)
            for k in range(KC):
                weights(0, k, k % 2)
            dve.wait_ge(x_loaded[0], 16)
            for s in range(2):
                add(s, s, s)
                low(s + 2, s)
                weights(1, s, s)
            dve.wait_ge(x_loaded[1], 16)
            with dve.Fori(1, KC // 2) as j:
                for s in range(2):
                    add(2 * j + s, 2 * j + s, s)
                    low(2 * j + s + 2, s)
                    weights(1, 2 * j + s, s)
            for s in range(2):
                add(KC + s, KC + s, s)
                low(KC + s + 2, s)
            dve.wait_ge(added, NT)
            with dve.Fori(0, NT // 2 - 1) as j:
                for s in range(2):
                    add(NT + 2 * j + s, 2 * j + s, s)
                    low(NT + 2 * j + s + 2, s)
            for s in range(2):
                add(2 * NT - 2 + s, NT - 2 + s, s)

        @block.tensor
        def _(pe):
            def tile(half, n, s):
                pe.wait_ge(m_split, n + 1)
                pe.wait_ge(added, n - 1)
                for c in range(2):
                    cols = slice(c * PW, (c + 1) * PW)
                    for k in range(KC):
                        for i, (l, r) in enumerate(((m_hi, w_hi), (m_hi, w_lo), (m_lo, w_hi))):
                            m = nc.tensor.matmul(bank[:, s, c], l[:, s, k], r[:, half, k, cols],
                                                 start=(k == 0 and i == 0), stop=(k == KC - 1 and i == 2))
                m.then_inc(multiplied, 1)

            pe.wait_ge(m_split, 2)
            for k in range(KC):
                pe.wait_ge(w_split, k + 1)
                for s in range(2):
                    for c in range(2):
                        cols = slice(c * PW, (c + 1) * PW)
                        for i, (l, r) in enumerate(((m_hi, w_hi), (m_hi, w_lo), (m_lo, w_hi))):
                            m = nc.tensor.matmul(bank[:, s, c], l[:, s, k], r[:, 0, k, cols],
                                                 start=(k == 0 and i == 0), stop=(k == KC - 1 and i == 2))
                    if k == KC - 1:
                        m.then_inc(multiplied, 1)
            with pe.Fori(1, NT // 2) as j:
                for s in range(2):
                    tile(0, 2 * j + s, s)
            pe.wait_ge(w_split, 2 * KC)
            with pe.Fori(NT // 2, NT) as j:
                for s in range(2):
                    tile(1, 2 * j + s, s)


def ffn(nc, hi, lo, w_up, w_down, conv_w, conv_b, y, out):
    PAD = TOK + 3
    GAP = SEQ + 1
    with ExitStack() as ctx:
        b = Bufs(nc, ctx)
        raw_u = b.sb("ff_rawu", [P, KC, 2, P])
        raw_d = b.sb("ff_rawd", [P, D])
        u_hi = b.sb("ff_uhi", [P, 2, KC, 2, P], F32R)
        u_lo = b.sb("ff_ulo", [P, 2, KC, 2, P], F32R)
        d_hi = b.sb("ff_dhi", [P, 2, D], F32R)
        d_lo = b.sb("ff_dlo", [P, 2, D], F32R)
        taps = b.sb("ff_taps", [P, 2 * NF, 3])
        bias = b.sb("ff_bias", [P, 2 * NF])
        padded = b.sb("ff_padded", [P, PAD])
        gate = b.sb("ff_gate", [P, PAD])
        up = b.sb("ff_up", [P, PAD])
        a_hi = b.sb("ff_ahi", [P, PAD], F32R)
        a_lo = b.sb("ff_alo", [P, PAD], F32R)
        proj = b.ps("ff_proj", [P, 2, 3 * PW])
        sums = b.ps("ff_sums", [P, 2, PW])
        const_loaded = b.sem("ff_const")
        u_loaded, d_loaded = b.sem("ff_ul"), b.sem("ff_dl")
        u_hi_done, u_split = b.sem("ff_uhid"), b.sem("ff_usplit")
        d_hi_done, d_split = b.sem("ff_dhid"), b.sem("ff_dsplit")
        zeroed = b.sem("ff_zeroed")
        projected, copied = b.sem("ff_proj_s"), b.sem("ff_copied")
        conved = b.sem("ff_conv")
        gated, acted = b.sem("ff_gated"), b.sem("ff_acted")
        a_hi_done, a_lo_done = b.sem("ff_ahid"), b.sem("ff_alod")
        summed, added = b.sem("ff_summed"), b.sem("ff_added")
        stored = b.sem("ff_stored")
        block = b.block()
        G = 2 * NT
        w_up_v = w_up.rearrange("(k p) (g n) -> p k g n", p=P, g=2)

        @block.sync
        def _(sp):
            def load(i, first=False):
                if not first:
                    sp.wait_ge(u_split, i)
                for g in range(2):
                    sp.dma_start(raw_u[:, :, g], w_up_v[:, :, g, ds(i * P, P)]).then_inc(u_loaded, 16)
                if not first:
                    sp.wait_ge(d_split, i)
                sp.dma_start(raw_d[:, :], w_down[ds(i * P, P), :]).then_inc(d_loaded, 16)

            load(0, True)
            sp.dma_start(taps[:, :, :], conv_w).then_inc(const_loaded, 16)
            sp.wait_ge(const_loaded, 16)
            sp.dma_start(bias[:, :], conv_b).then_inc(const_loaded, 16)
            with sp.Fori(1, NF) as i:
                load(i)
            with sp.Fori(0, NT) as t:
                sp.wait_ge(added, (NF - 1) * G + 2 * t + 2)
                sp.dma_start(out[ds(t * P, P), :], y[:, ds(t, 1), :]).then_inc(stored, 16)
            sp.wait_ge(stored, 16 * NT)

        @block.scalar
        def _(act):
            def up_weights(i, s, first=False):
                act.wait_ge(u_loaded, 32 * i + 32)
                if not first:
                    act.wait_ge(projected, 2 * i - 2)
                nc.scalar.activation(u_hi[:, s], raw_u[:, :, :, :], ACT.Copy).then_inc(u_hi_done, 1)

            def down_weights(i, s, first=False):
                act.wait_ge(d_loaded, 16 * i + 16)
                if not first:
                    act.wait_ge(summed, G * (i - 1))
                nc.scalar.activation(d_hi[:, s], raw_d[:, :], ACT.Copy).then_inc(d_hi_done, 1)

            def copy(i, g, first=False):
                act.wait_ge(projected, 2 * i + g + 1)
                if not first:
                    act.wait_ge(conved, 3 * (2 * i + g))
                nc.scalar.activation(padded[:, 1:1 + SEQ], proj[:, g, 0:SEQ], ACT.Copy)
                nc.scalar.activation(padded[:, GAP + 1:GAP + 1 + DEC], proj[:, g, SEQ:TOK],
                                     ACT.Copy).then_inc(copied, 1)

            def hidden(i, first=False):
                act.wait_ge(conved, 6 * i + 6)
                nc.scalar.activation(gate[:, 1:GAP + 1 + DEC], gate[:, 1:GAP + 1 + DEC],
                                     ACT.Silu).then_inc(gated, 1)
                act.wait_ge(acted, i + 1)
                if not first:
                    act.wait_ge(summed, G * i)
                nc.scalar.activation(a_hi[:, 1:GAP + 1 + DEC], gate[:, 1:GAP + 1 + DEC],
                                     ACT.Copy).then_inc(a_hi_done, 1)

            act.wait_ge(zeroed, 1)
            up_weights(0, 0, True)
            down_weights(0, 0, True)
            up_weights(1, 1, True)
            copy(0, 0, True)
            copy(0, 1)
            hidden(0, True)
            down_weights(1, 1, True)
            with act.Fori(0, (NF - 2) // 2) as j:
                for s in range(2):
                    i = 2 * j + s + 1
                    up_weights(i + 1, s)
                    copy(i, 0)
                    copy(i, 1)
                    hidden(i)
                    down_weights(i + 1, s)
            copy(NF - 1, 0)
            copy(NF - 1, 1)
            hidden(NF - 1)

        @block.vector
        def _(dve):
            nc.vector.memset(padded[:, :], 0.0).then_inc(zeroed, 1)

            def up_weights(i, s):
                dve.wait_ge(u_hi_done, i + 1)
                nc.vector.tensor_tensor(u_lo[:, s], raw_u[:, :, :, :], u_hi[:, s].bitcast(FP32),
                                        ALU.subtract).then_inc(u_split, 1)

            def down_weights(i, s):
                dve.wait_ge(d_hi_done, i + 1)
                nc.vector.tensor_tensor(d_lo[:, s], raw_d[:, :], d_hi[:, s].bitcast(FP32),
                                        ALU.subtract).then_inc(d_split, 1)

            def conv(i, g, dst):
                n = 3 * (2 * i + g)
                c = i + g * NF
                mid = slice(1, GAP + 1 + DEC)
                dve.wait_ge(copied, 2 * i + g + 1)
                nc.vector.tensor_scalar(dst[:, mid], padded[:, mid], taps[:, ds(c, 1), 1],
                                        bias[:, ds(c, 1)], ALU.mult, ALU.add).then_inc(conved, 1)
                dve.wait_ge(conved, n + 1)
                nc.vector.scalar_tensor_tensor(dst[:, mid], padded[:, 0:GAP + DEC], taps[:, ds(c, 1), 0],
                                               dst[:, mid], ALU.mult, ALU.add).then_inc(conved, 1)
                dve.wait_ge(conved, n + 2)
                nc.vector.scalar_tensor_tensor(dst[:, mid], padded[:, 2:GAP + 2 + DEC],
                                               taps[:, ds(c, 1), 2], dst[:, mid],
                                               ALU.mult, ALU.add).then_inc(conved, 1)

            def hidden(i):
                mid = slice(1, GAP + 1 + DEC)
                dve.wait_ge(gated, i + 1)
                nc.vector.tensor_tensor(gate[:, mid], gate[:, mid], up[:, mid], ALU.mult).then_inc(acted, 1)
                dve.wait_ge(a_hi_done, i + 1)
                nc.vector.tensor_tensor(a_lo[:, mid], gate[:, mid], a_hi[:, mid].bitcast(FP32),
                                        ALU.subtract).then_inc(a_lo_done, 1)

            def adds(i):
                for t in range(NT):
                    for c in range(2):
                        g = 2 * t + c
                        dve.wait_ge(summed, G * i + g + 1)
                        v = y[:, t, c * PW:(c + 1) * PW]
                        nc.vector.tensor_tensor(v, v, sums[:, c], ALU.add).then_inc(added, 1)

            dve.wait_ge(const_loaded, 32)
            up_weights(0, 0)
            down_weights(0, 0)
            up_weights(1, 1)
            conv(0, 0, gate)
            conv(0, 1, up)
            hidden(0)
            down_weights(1, 1)
            with dve.Fori(0, (NF - 2) // 2) as j:
                for s in range(2):
                    i = 2 * j + s + 1
                    up_weights(i + 1, s)
                    adds(i - 1)
                    conv(i, 0, gate)
                    conv(i, 1, up)
                    hidden(i)
                    down_weights(i + 1, s)
            adds(NF - 2)
            conv(NF - 1, 0, gate)
            conv(NF - 1, 1, up)
            hidden(NF - 1)
            adds(NF - 1)

        @block.tensor
        def _(pe):
            X, U = (hi, lo), (u_hi, u_lo)

            def project(i, s, first=False):
                for g in range(2):
                    pe.wait_ge(u_split, i + 1)
                    if not first:
                        pe.wait_ge(copied, 2 * i - 1 + g)
                    for k in range(KC):
                        for r, (w, x) in enumerate(((0, 0), (0, 1), (1, 0))):
                            for t0, n in ((0, PW), (PW, PW), (2 * PW, TOK - 2 * PW)):
                                m = nc.tensor.matmul(proj[:, g, t0:t0 + n], U[w][:, s, k, g],
                                                     X[x][:, k, t0:t0 + n],
                                                     start=(k == 0 and r == 0), stop=(k == KC - 1 and r == 2))
                    m.then_inc(projected, 1)

            def down(i, s, first=False):
                pe.wait_ge(a_lo_done, i + 1)
                pe.wait_ge(d_split, i + 1)
                for t in range(NT):
                    c0 = 1 + t * P + (t >= TP)
                    for c in range(2):
                        if not (first and t == 0):
                            pe.wait_ge(added, G * i + 2 * t + c - 1)
                        cols = slice(c * PW, (c + 1) * PW)
                        for r, (a, w) in enumerate(((a_hi, d_hi), (a_hi, d_lo), (a_lo, d_hi))):
                            m = nc.tensor.matmul(sums[:, c], a[:, c0:c0 + P], w[:, s, cols],
                                                 start=(r == 0), stop=(r == 2))
                        m.then_inc(summed, 1)

            project(0, 0, True)
            project(1, 1)
            down(0, 0, True)
            with pe.Fori(1, NF // 2) as j:
                for s in range(2):
                    i = 2 * j + s
                    project(i, s)
                    down(i - 1, 1 - s)
            down(NF - 1, 1)


def encoder(nc, tokens, w_in, w_mem, w_out, w_up, w_down, norm_w, small, ident, masks, rope, tri,
            conv_w, conv_b, ssm_conv, out, scratch):
    proj, mem_proj, xbc_t, dt_t, xbc_c, mix_t = scratch
    with nc.sbuf_tensor("act_hi", [P, KC, TOK + NMT * P], F32R) as hi, \
            nc.sbuf_tensor("act_lo", [P, KC, TOK + NMT * P], F32R) as lo:
        norm_transpose(nc, "n1", NT + NMT, [(norm_w[0:1, :], 0, NT), (norm_w[1:2, :], NT, NMT)],
                       ident, hi, lo, src_dram=tokens)
        projections(nc, hi, lo, w_in, w_mem, proj, mem_proj, xbc_t, dt_t)
    attention(nc, proj, ident, masks, rope, small, mix_t)
    memory(nc, proj, mem_proj, ident, small, mix_t)
    ssm(nc, proj, xbc_t, dt_t, ident, tri, ssm_conv, small, mix_t, xbc_c)
    with nc.sbuf_tensor("x1", [P, NT, D], FP32) as x1:
        out_projection(nc, w_out, mix_t, tokens[0:TOK, :], x1)
        with nc.sbuf_tensor("h_hi", [P, KC, TOK], F32R) as hi, \
                nc.sbuf_tensor("h_lo", [P, KC, TOK], F32R) as lo:
            norm_transpose(nc, "n2", NT, [(norm_w[2:3, :], 0, NT)], ident, hi, lo, src_sb=x1)
            ffn(nc, hi, lo, w_up, w_down, conv_w, conv_b, x1, out)


def window_masks():
    q, k = np.arange(P)[:, None], np.arange(3 * P)[None] - P
    band = np.abs(k - q) <= 128
    return np.array([np.where(band & (t * P + k >= 0) & (t * P + k < n * P), 0, NEG)
                     for n in (TP, TS) for t in range(n)], np.float32)


def rope_tables():
    inv = np.float32(10000.0) ** (-np.arange(0, DH, 2, dtype=np.float32) / np.float32(DH))
    ang = np.arange(SEQ, dtype=np.float32)[:, None] * inv.astype(np.float32)[None]
    c, s = np.cos(ang), np.sin(ang)
    tab = np.stack([np.concatenate([c, c], 1), np.concatenate([-s, s], 1)])
    return tab.reshape(2, TP, P, DH).transpose(2, 0, 1, 3).astype(np.float32)


def triangles():
    i = np.arange(P)
    return np.stack([i[:, None] <= i[None], i[:, None] >= i[None]], 1).astype(np.float32)


def kernel(**inputs):
    import concourse.bacc as bacc
    from concourse.bass_utils import run_bass_kernel_spmd

    a = {k: np.asarray(v) for k, v in inputs.items()}
    w_in = a["w_in"][0]
    dt0, mq0 = 3072, 3088
    arrays = {
        "tokens": np.concatenate([a["x_prompt"][0], a["x_sample"][0], a["mem_prompt"][0], a["mem_sample"][0]]),
        "w_in": np.concatenate([w_in[:, :2048], w_in[:, mq0:], w_in[:, 2048:dt0], w_in[:, dt0:mq0]], 1),
        "w_mem": a["w_mem_kv"][0], "w_out": a["w_out"][0],
        "w_up": a["w_ffn_up"][0], "w_down": a["w_ffn_down"][0],
        "norm_w": np.concatenate([a["norm1_w"], a["mem_norm_w"], a["norm2_w"]]),
        "ident": np.eye(P, dtype=np.float32), "masks": window_masks(), "rope": rope_tables(),
        "tri": triangles(),
        "conv_w": a["ffn_conv_w"][0].reshape(3, 2 * NF, P).transpose(2, 1, 0),
        "conv_b": a["ffn_conv_b"][0].reshape(2 * NF, P).T,
        "ssm_conv": np.concatenate([a["ssm_conv_w"][0], a["ssm_conv_b"]]).reshape(6, XBC // P, P).transpose(2, 1, 0),
    }
    small = {k: a[k].reshape(1, -1) for k in (
        "q_norm_w", "k_norm_w", "attn_sink", "mq_norm_w", "mk_norm_w", "ssm_norm_w", "ssm_D",
        "ssm_dt_bias", "ssm_A_log")}
    nc = bacc.Bacc("TRN2", target_bir_lowering=False, num_devices=1)
    maps = {k: np.ascontiguousarray(v) for k, v in {**arrays, **small}.items()}
    ap = {k: nc.dram_tensor(k, v.shape, FP32, kind="ExternalInput").ap() for k, v in maps.items()}
    out = nc.dram_tensor("out", (TOK, D), FP32, kind="ExternalOutput").ap()
    scratch = [nc.dram_tensor(f"scratch_{n}", s, FP32, kind="Internal").ap() for n, s in (
        ("proj", (TOK, NPAN * PW)), ("mem", (NMT * P, 2 * PW)), ("xbc", (XBC, TOK)), ("dt", (2 * NS, TOK)),
        ("xbc_tiles", (NT, P, XBC)), ("mix", (NT, P, 16 * P)))]
    encoder(nc, *(ap[k] for k in ("tokens", "w_in", "w_mem", "w_out", "w_up", "w_down", "norm_w")),
            {k: ap[k] for k in small}, *(ap[k] for k in ("ident", "masks", "rope", "tri", "conv_w", "conv_b",
                                                          "ssm_conv")), out, scratch)
    r = run_bass_kernel_spmd(nc, [maps], core_ids=[0])
    y = r.results[0]["out"]
    return y[None, :SEQ], y[None, SEQ:]
```

```python
import concourse.bass as bass
from concourse import mybir
from contextlib import ExitStack
import numpy as np

FP32 = mybir.dt.float32
F32R = mybir.dt.float32r
ALU = mybir.AluOpType
ACT = mybir.ActivationFunctionType
AX = mybir.AxisListType

P = 128
D = 1024
KC = D // P
SEQ, DEC = 1024, 256
TP, TS = SEQ // P, DEC // P
NT = TP + TS
TOK = NT * P
NMT = 4
HQ, HKV, DH = 16, 4, 64
HM, DM = 4, 128
NS, PS, NG, ST = 8, 64, 2, 128
XBC = NS * PS + 2 * NG * ST
F = 2816
NF = F // P
EPS = 1e-6
PW = 512
CUT = 448
TOKEN_CUTS = ((0, CUT), (CUT, CUT), (2 * CUT, TOK - 2 * CUT))
NPAN = 5
NEG = -1e30
KB = NT + 3


def ds(a, n):
    return bass.ds(a, n)


class Bufs:

    def __init__(self, nc, ctx):
        self.nc, self.ctx, self.own = nc, ctx, []

    def sb(self, name, shape, dt=FP32):
        return self.ctx.enter_context(self.nc.sbuf_tensor(name, shape, dt))

    def ps(self, name, shape):
        return self.ctx.enter_context(self.nc.psum_tensor(name, shape, FP32))

    def sem(self, name):
        self.own.append(self.ctx.enter_context(self.nc.semaphore(name)))
        return self.own[-1]

    def sems(self, name, n):
        return [self.sem(f"{name}{i}") for i in range(n)]

    def block(self):
        self.ctx.callback(self.clear)
        return self.ctx.enter_context(self.nc.Block())

    def clear(self):
        with self.nc.Block() as block:
            @block.gpsimd
            def _(pool):
                for s in self.own:
                    pool.sem_clear(s)


def norm_transpose(nc, tag, tiles, weight_rows, ident_dram, hi, lo, src_dram=None, src_sb=None):
    with ExitStack() as ctx:
        b = Bufs(nc, ctx)
        ident = b.sb(f"{tag}_ident", [P, P])
        wb = b.sb(f"{tag}_w", [P, len(weight_rows), D])
        x = b.sb(f"{tag}_x", [P, tiles, D]) if src_dram is not None else None
        xn = b.sb(f"{tag}_xn", [P, 2, D])
        junk = b.sb(f"{tag}_junk", [P, 2, D])
        ms = b.sb(f"{tag}_ms", [P, tiles])
        mse = b.sb(f"{tag}_mse", [P, tiles])
        rstd = b.sb(f"{tag}_rstd", [P, tiles])
        half = b.sb(f"{tag}_half", [P, 1])
        eps = b.sb(f"{tag}_eps", [P, 1])
        xt = b.ps(f"{tag}_xt", [P, 2, KC, P])
        const_loaded = b.sem(f"{tag}_const")
        x_loaded = b.sems(f"{tag}_xl", 2)
        half_set = b.sem(f"{tag}_halfset")
        squared, mse_done, rstd_done = b.sem(f"{tag}_sq"), b.sem(f"{tag}_mse"), b.sem(f"{tag}_rs")
        normed, transposed, hi_done, lo_done = (b.sem(f"{tag}_{n}") for n in ("xn", "tr", "hi", "lo"))
        block = b.block()

        @block.sync
        def _(sp):
            if src_dram is not None:
                for s in range(2):
                    sp.dma_start(x[:, s], src_dram[s * P:(s + 1) * P, :]).then_inc(x_loaded[s], 16)
                with sp.Fori(1, tiles // 2) as j:
                    for s in range(2):
                        sp.wait_ge(x_loaded[s], 16 * j)
                        sp.dma_start(x[:, ds(2 * j + s, 1)], src_dram[ds((2 * j + s) * P, P), :]
                                     ).then_inc(x_loaded[s], 16)

        def source(t):
            rows = x if src_dram is not None else src_sb
            return rows[:, t, :] if isinstance(t, int) else rows[:, ds(t, 1), :]

        @block.scalar
        def _(act):
            def square(j, s):
                t = 2 * j + s
                if src_dram is not None:
                    act.wait_ge(x_loaded[s], 16 * j + 16)
                if not (isinstance(j, int) and j == 0):
                    act.wait_ge(squared, t - 1)
                nc.scalar.activation(junk[:, s], source(t), ACT.Square, scale=D ** -0.5,
                                     accum_out=ms[:, ds(t, 1)]).then_inc(squared, 1)

            def high(j, s):
                t = 2 * j + s
                act.wait_ge(transposed, t + 1)
                nc.scalar.activation(hi[:, :, ds(t * P, P)], xt[:, s], ACT.Copy).then_inc(hi_done, 1)

            act.dma_start(ident[:, :], ident_dram).then_inc(const_loaded, 16)
            for i, (w, _, _) in enumerate(weight_rows):
                act.dma_start(wb[:, i], w.broadcast_to([P, D])).then_inc(const_loaded, 16)
            for s in range(2):
                square(0, s)
            with act.Fori(0, tiles // 2 - 1) as j:
                for s in range(2):
                    square(j + 1, s)
                    high(j, s)
            for s in range(2):
                high(tiles // 2 - 1, s)

        @block.gpsimd
        def _(pool):
            nc.gpsimd.memset(half[:, :], -0.5).then_inc(half_set, 1)
            nc.gpsimd.memset(eps[:, :], EPS).then_inc(half_set, 1)
            pool.wait_ge(half_set, 2)
            with pool.Fori(0, tiles) as t:
                pool.wait_ge(squared, t + 1)
                nc.gpsimd.tensor_tensor(mse[:, ds(t, 1)], ms[:, ds(t, 1)], eps[:, :],
                                        ALU.add).then_inc(mse_done, 1)
                pool.wait_ge(mse_done, t + 1)
                nc.gpsimd.tensor_tensor(rstd[:, ds(t, 1)], mse[:, ds(t, 1)], half[:, :],
                                        ALU.pow).then_inc(rstd_done, 1)

        @block.vector
        def _(dve):
            def norm(t, s, weight, first=False):
                dve.wait_ge(rstd_done, t + 1)
                if not first:
                    dve.wait_ge(transposed, t - 1)
                nc.vector.scalar_tensor_tensor(xn[:, s], source(t), rstd[:, ds(t, 1)], wb[:, weight],
                                               ALU.mult, ALU.mult).then_inc(normed, 1)

            def low(t, s):
                dve.wait_ge(hi_done, t + 1)
                nc.vector.tensor_tensor(lo[:, :, ds(t * P, P)], xt[:, s],
                                        hi[:, :, ds(t * P, P)].bitcast(FP32),
                                        ALU.subtract).then_inc(lo_done, 1)

            dve.wait_ge(const_loaded, 16 * (1 + len(weight_rows)))
            for s in range(2):
                norm(s, s, 0, True)
            for i, (_, first, count) in enumerate(weight_rows):
                with dve.Fori(max(first // 2, 1), (first + count) // 2) as j:
                    for s in range(2):
                        low(2 * j + s - 2, s)
                        norm(2 * j + s, s, i)
            for s in range(2):
                low(tiles - 2 + s, s)

        @block.tensor
        def _(pe):
            pe.wait_ge(const_loaded, 16 * (1 + len(weight_rows)))

            def one(t, s, first):
                pe.wait_ge(normed, t + 1)
                if not first:
                    pe.wait_ge(lo_done, t - 1)
                for k in range(KC):
                    m = nc.tensor.transpose(xt[:, s, k], xn[:, s, k * P:(k + 1) * P], ident[:, :])
                m.then_inc(transposed, 1)

            for s in range(2):
                one(s, s, True)
            with pe.Fori(1, tiles // 2) as j:
                for s in range(2):
                    one(2 * j + s, s, False)


def projections(nc, hi, lo, w_in, w_mem, proj, mem_proj, xbc_c, small, ident_dram, tri_dram,
                conv_dram, R):
    PIECES, RAW, BANKS = 4, 2, 7
    TAPS, NCH = 5, XBC // P
    PADW, SPAN = TOK + 6, TOK + 2
    CUTS = ((0, 512, 2), (512, 512, 514), (SEQ, DEC, SEQ + 4))
    NC = len(CUTS)
    H2 = 2 * NS
    rows = KC // PIECES
    Z_PANEL = 3
    with ExitStack() as ctx:
        b = Bufs(nc, ctx)
        raw = b.sb("pj_raw", [P, RAW, rows, PW])
        w_hi = b.sb("pj_whi", [P, 2, KC, PW], F32R)
        w_lo = b.sb("pj_wlo", [P, 2, KC, PW], F32R)
        dt_raw = b.sb("pj_dtraw", [P, KC, H2])
        dt_hi = b.sb("pj_dthi", [P, KC, H2], F32R)
        dt_lo = b.sb("pj_dtlo", [P, KC, H2], F32R)
        stage = b.sb("pj_stage", [P, 2, PW])
        ident = b.sb("pj_ident", [H2, H2])
        taps = b.sb("cv_taps", [P, NCH, TAPS + 1])
        x = b.sb("cv_x", [P, PADW])
        y = b.sb("cv_y", [P, SPAN])
        ones = b.sb("sz_ones", [P, P])
        bias = b.sb("sz_bias", [P, 1, H2])
        a_log = b.sb("sz_alog", [P, 1, H2])
        a_neg = b.sb("sz_aneg", [P, 1, H2])
        v1, v2, v3, v4 = (b.sb(f"sz_v{i}", [P, NT, H2]) for i in range(1, 5))
        bank = b.ps("pj_bank", [P, BANKS, PW])
        sizes = b.ps("sz_ps", [P, 3, NT, H2])
        raw_loaded = b.sems("pj_rawl", RAW)
        dt_loaded = b.sem("pj_dtl")
        w_hi_done, w_split = b.sem("pj_whid"), b.sem("pj_split")
        multiplied = b.sem("pj_mm")
        copied = b.sem("pj_copied")
        stored = b.sems("pj_stored", 2)
        taps_loaded, zeroed, tapped = b.sem("cv_const"), b.sem("cv_zero"), b.sem("cv_tap")
        silued, row_stored = b.sem("cv_silu"), b.sem("cv_stored")
        sz_loaded, dt_projected, step, summed = b.sem("sz_l"), b.sem("sz_dt"), b.sem("sz_step"), b.sem("sz_sum")
        exps, ones_set, want_exp = b.sem("sz_exp"), b.sem("sz_ones_s"), b.sem("sz_want")
        block = b.block()
        dt, acs, e_acs, e_tot, dec = R["dt"], R["acs"], R["e_acs"], R["e_tot"], R["dec"]
        a_sb, tri = R["a"], R["tri"]

        w_mem_v = w_mem.rearrange("(k p) n -> p k n", p=P)
        w_in_v = w_in.rearrange("(k p) n -> p k n", p=P)
        XBC_COL, DT_COL = NPAN * PW, NPAN * PW + XBC
        DT0 = NCH * NC
        TOK0 = DT0 + NC
        MEM0 = TOK0 + NPAN * NT
        GROUPS = MEM0 + 2 * NMT

        @block.sync
        def _(sp):
            def load(n, src, c):
                for q in range(PIECES):
                    if not (isinstance(n, int) and n == 0 and q < RAW):
                        sp.wait_ge(w_split, PIECES * n + q - RAW + 1)
                    sp.dma_start(raw[:, q % RAW], src[:, q * rows:(q + 1) * rows, c]).then_inc(raw_loaded[q % RAW], 16)

            load(0, w_in_v, slice(XBC_COL, XBC_COL + PW))
            sp.dma_start(taps[:, :, :], conv_dram).then_inc(taps_loaded, 16)
            sp.dma_start(dt_raw[:, :, :], w_in_v[:, :, DT_COL:DT_COL + H2]).then_inc(dt_loaded, 16)
            for dst, src in ((tri[:, :, :], tri_dram), (ident[:, :], ident_dram[0:H2, 0:H2]),
                             (bias[:, 0], small["ssm_dt_bias"].broadcast_to([P, H2])),
                             (a_log[:, 0], small["ssm_A_log"].broadcast_to([P, H2]))):
                sp.dma_start(dst, src).then_inc(sz_loaded, 16)
            load(1, w_in_v, slice(XBC_COL + PW, XBC_COL + 2 * PW))
            with sp.Fori(0, NPAN) as m:
                load(m + 2, w_in_v, ds(m * PW, PW))
            for n in range(2):
                load(NPAN + 2 + n, w_mem_v, slice(n * PW, (n + 1) * PW))

        @block.vector
        def _(dve):
            v = nc.vector

            def split(n, s, free):
                if free is not None:
                    dve.wait_ge(multiplied, free)
                for q in range(PIECES):
                    dve.wait_ge(raw_loaded[q % RAW], 16 * (PIECES // RAW * n + q // RAW + 1))
                    k = slice(q * rows, (q + 1) * rows)
                    v.tensor_copy(w_hi[:, s, k], raw[:, q % RAW]).then_inc(w_hi_done, 1)
                    dve.wait_ge(w_hi_done, PIECES * n + q + 1)
                    v.tensor_tensor(w_lo[:, s, k], raw[:, q % RAW], w_hi[:, s, k].bitcast(FP32),
                                    ALU.subtract).then_inc(w_split, 1)

            def conv(c):
                dve.wait_ge(copied, NC * (c + 1))
                if c > 0:
                    dve.wait_ge(row_stored, 32 * c)
                v.tensor_scalar(y[:, :], x[:, 0:SPAN], taps[:, c:c + 1, 0], taps[:, c:c + 1, TAPS], ALU.mult,
                                ALU.add).then_inc(tapped, 1)
                for k in range(1, TAPS):
                    dve.wait_ge(tapped, TAPS * c + k)
                    v.scalar_tensor_tensor(y[:, :], x[:, k:k + SPAN], taps[:, c:c + 1, k], y[:, :],
                                           ALU.mult, ALU.add).then_inc(tapped, 1)

            n = [0]

            def then(ins):
                n[0] += 1
                ins.then_inc(step, 1)
                dve.wait_ge(step, n[0])

            v.memset(x[:, :], 0.0).then_inc(zeroed, 1)
            v.memset(ones[:, :], 1.0).then_inc(ones_set, 1)
            split(0, 0, None)
            dve.wait_ge(dt_loaded, 16)
            then(v.tensor_copy(dt_hi[:, :, :], dt_raw[:, :, :]))
            then(v.tensor_tensor(dt_lo[:, :, :], dt_raw[:, :, :], dt_hi[:, :, :].bitcast(FP32), ALU.subtract))
            split(1, 1, None)
            dve.wait_ge(taps_loaded, 16)
            for c in range(4):
                conv(c)
            split(2, 0, DT0 // 2)
            for c in range(4, NCH):
                conv(c)
            split(3, 1, DT0)
            split(4, 0, TOK0 + NT)
            dve.wait_ge(sz_loaded, 64)
            dve.wait_ge(dt_projected, 1)
            then(v.tensor_tensor(v1[:, :, :], sizes[:, 0], bc(bias[:, :, :], [P, NT, H2]), ALU.add))
            then(v.tensor_scalar(v2[:, :, :], v1[:, :, :], -1.0, None, ALU.mult))
            then(v.tensor_tensor(v3[:, :, :], v1[:, :, :], v2[:, :, :], ALU.min))
            v.tensor_scalar(v1[:, :, :], v1[:, :, :], 0.0, None, ALU.max).then_inc(want_exp, 1)
            dve.wait_ge(exps, 2)
            then(v.tensor_scalar(v2[:, :, :], v4[:, :, :], 2.0, None, ALU.add))
            then(v.reciprocal(v3[:, :, :], v2[:, :, :]))
            then(v.tensor_tensor(v4[:, :, :], v4[:, :, :], v3[:, :, :], ALU.mult))
            then(v.tensor_tensor(v2[:, :, :], v4[:, :, :], v4[:, :, :], ALU.mult))
            then(v.tensor_scalar(v3[:, :, :], v2[:, :, :], 1.0 / 17, 1.0 / 15, ALU.mult, ALU.add))
            for k in (13, 11, 9, 7, 5, 3, 1):
                then(v.tensor_tensor(v3[:, :, :], v3[:, :, :], v2[:, :, :], ALU.mult))
                then(v.tensor_scalar(v3[:, :, :], v3[:, :, :], 1.0 / k, None, ALU.add))
            then(v.tensor_tensor(v3[:, :, :], v3[:, :, :], v4[:, :, :], ALU.mult))
            dve.wait_ge(want_exp, 1)
            then(v.scalar_tensor_tensor(dt[:, :, :], v3[:, :, :], 2.0, v1[:, :, :], ALU.mult, ALU.add))
            then(v.tensor_scalar(a_neg[:, :, :], a_neg[:, :, :], -1.0, None, ALU.mult))
            v.tensor_tensor(a_sb[:, :, :], dt[:, :, :], bc(a_neg[:, :, :], [P, NT, H2]), ALU.mult
                            ).then_inc(want_exp, 1)
            split(5, 1, TOK0 + 2 * NT)
            dve.wait_ge(summed, 1)
            then(v.tensor_copy(acs[:, :, :], sizes[:, 1]))
            v.tensor_tensor(v1[:, :, :], sizes[:, 2], acs[:, :, :], ALU.subtract).then_inc(want_exp, 1)
            dve.wait_ge(exps, 5)
            v.tensor_tensor(dec[:, :, :], v2[:, :, :], dt[:, :, :], ALU.mult).then_inc(step, 1)
            for n in range(6, NPAN + 4):
                split(n, n % 2, TOK0 + NT * (n - 3))

        @block.tensor
        def _(pe):
            W = (w_hi, w_lo)
            X = (hi, lo)

            def group(g, out, left, right, panel=None):
                if g >= BANKS:
                    pe.wait_ge(copied, g - BANKS + 1)
                for k in range(KC):
                    if panel is not None and k % rows == 0:
                        pe.wait_ge(w_split, PIECES * panel + k // rows + 1)
                    for i, (a, c) in enumerate(((0, 0), (0, 1), (1, 0))):
                        m = nc.tensor.matmul(out, left(a, k), right(c, k), start=(k == 0 and i == 0),
                                             stop=(k == KC - 1 and i == 2))
                m.then_inc(multiplied, 1)

            def channel_panel(n, s):
                for m4 in range(4):
                    for i, (t0, w, _) in enumerate(CUTS):
                        g = NC * (4 * n + m4) + i
                        group(g, bank[:, g % BANKS, 0:w], lambda a, k: W[a][:, s, k, m4 * P:(m4 + 1) * P],
                              lambda c, k: X[c][:, k, t0:t0 + w], n if m4 == i == 0 else None)

            def token_panel(n, s, tiles, t0, g0):
                for t in range(tiles):
                    g = g0 + t
                    group(g, bank[:, g % BANKS], lambda a, k: X[a][:, k, (t0 + t) * P:(t0 + t + 1) * P],
                          lambda c, k: W[c][:, s, k], n if t == 0 else None)

            channel_panel(0, 0)
            channel_panel(1, 1)
            for i, (t0, w, _) in enumerate(CUTS):
                g = DT0 + i
                group(g, bank[0:H2, g % BANKS, 0:w], lambda a, k: (dt_hi, dt_lo)[a][:, k],
                      lambda c, k: X[c][:, k, t0:t0 + w])
            token_panel(2, 0, NT, 0, TOK0)
            pe.wait_ge(copied, TOK0)
            pe.wait_ge(sz_loaded, 64)
            for t in range(NT):
                at = CUTS[0][2] + t * P if t < TP else CUTS[2][2] + (t - TP) * P
                m = nc.tensor.transpose(sizes[:, 0, t], x[0:H2, at:at + P], ident[:, :])
            m.then_inc(dt_projected, 1)
            token_panel(3, 1, NT, 0, TOK0 + NT)
            pe.wait_ge(ones_set, 1)
            pe.wait_ge(want_exp, 2)
            for d in range(2):
                nc.tensor.matmul(sizes[:, 1, :, d * NS:(d + 1) * NS], tri[:, d],
                                 a_sb[:, :, d * NS:(d + 1) * NS], start=True, stop=True)
            nc.tensor.matmul(sizes[:, 2], ones[:, :], a_sb[:, :, :], start=True, stop=True
                             ).then_inc(summed, 1)
            for n in range(4, 2 + NPAN):
                token_panel(n, n % 2, NT, 0, TOK0 + NT * (n - 2))
            for n in range(2):
                token_panel(NPAN + 2 + n, (NPAN + n) % 2, NMT, NT, MEM0 + NMT * n)

        @block.scalar
        def _(act):
            a = nc.scalar

            def to_row(c, part):
                for i, (_, w, at) in enumerate(CUTS):
                    g = NC * c + i
                    act.wait_ge(multiplied, g + 1)
                    if i == 0 and c > 0:
                        act.wait_ge(tapped, TAPS * c)
                    a.activation(x[0:part, at:at + w], bank[0:part, g % BANKS, 0:w], ACT.Copy).then_inc(copied, 1)

            def channels(c):
                to_row(c, P)
                act.wait_ge(tapped, TAPS * (c + 1))
                a.activation(y[:, :], y[:, :], ACT.Silu).then_inc(silued, 1)
                act.wait_ge(silued, c + 1)
                dst = xbc_c.rearrange("t p n -> p t n")[:, :, c * P:(c + 1) * P]
                act.dma_start(dst[:, 0:TP], y[:, 0:SEQ].rearrange("p (t n) -> p t n", n=P)
                              ).then_inc(row_stored, 16)
                act.dma_start(dst[:, TP:NT], y[:, SEQ + 2:SPAN].rearrange("p (t n) -> p t n", n=P)
                              ).then_inc(row_stored, 16)

            def out(g, dst, func=ACT.Copy):
                s = (g - TOK0) % 2
                act.wait_ge(multiplied, g + 1)
                if g >= TOK0 + 2:
                    act.wait_ge(stored[s], 16 * ((g - TOK0) // 2))
                a.activation(stage[:, s], bank[:, g % BANKS], func).then_inc(copied, 1)
                act.wait_ge(copied, g + 1)
                act.dma_start(dst, stage[:, s]).then_inc(stored[s], 16)

            act.wait_ge(zeroed, 1)
            for c in range(NCH):
                channels(c)
            to_row(NCH, H2)
            for n in range(NPAN):
                for t in range(NT):
                    out(TOK0 + NT * n + t, proj[t * P:(t + 1) * P, n * PW:(n + 1) * PW],
                        ACT.Silu if n == Z_PANEL else ACT.Copy)
                    if n == 1 and t == 4:
                        act.wait_ge(sz_loaded, 64)
                        a.activation(a_neg[:, :, :], a_log[:, :, :], ACT.Exp).then_inc(exps, 1)
                        act.wait_ge(want_exp, 1)
                        a.activation(v4[:, :, :], v3[:, :, :], ACT.Exp).then_inc(exps, 1)
                    if n == 2 and t == 4:
                        act.wait_ge(want_exp, 3)
                        a.activation(e_acs[:, :, :], acs[:, :, :], ACT.Exp).then_inc(exps, 1)
                        a.activation(e_tot[:, :, :], sizes[:, 2], ACT.Exp).then_inc(exps, 1)
                        a.activation(v2[:, :, :], v1[:, :, :], ACT.Exp).then_inc(exps, 1)
            for n in range(2):
                for t in range(NMT):
                    out(MEM0 + NMT * n + t, mem_proj[t * P:(t + 1) * P, n * PW:(n + 1) * PW])
            for s in range(2):
                act.wait_ge(stored[s], 16 * (GROUPS - TOK0) // 2)
            act.wait_ge(row_stored, 32 * NCH)


def bc(ap, shape):
    return ap.broadcast_to(shape)


def attention(nc, proj, ident_dram, mask_dram, rope_dram, small, mix_t):
    q_w, k_w, sink = small["q_norm_w"], small["k_norm_w"], small["attn_sink"]
    WIN = 3 * P
    with ExitStack() as ctx:
        b = Bufs(nc, ctx)
        ident = b.sb("at_ident", [P, P])
        mask = b.sb("at_mask", [P, 2, WIN])
        rope = b.sb("at_rope", [P, 2, TP, DH])
        wrow = b.sb("at_wrow", [P, 4, DH])
        table = b.sb("at_table", [P, 4, TP, DH])
        k_raw = b.sb("at_kraw", [P, NT, HKV, DH])
        k_a = b.sb("at_ka", [P, NT, HKV, DH])
        k_two = b.sb("at_ktwo", [P, NT, HKV, 2, DH])
        k_b = k_two[:, :, :, 0]
        k_ss = b.sb("at_kss", [P, NT * HKV])
        k_mse = b.sb("at_kmse", [P, NT * HKV])
        k_rstd = b.sb("at_krstd", [P, NT * HKV])
        v_sb = b.sb("at_v", [P, KB, HKV * DH])
        kt_hi = b.sb("at_kthi", [P, HKV, KB * P], F32R)
        kt_lo = b.sb("at_ktlo", [P, HKV, KB * P], F32R)
        half = b.sb("at_half", [P, NT * HKV])
        eps = b.sb("at_eps", [P, NT * HKV])
        sinkb = b.sb("at_sink", [P, HQ])
        nsink = b.sb("at_nsink", [P, HQ])
        q_raw = b.sb("at_qraw", [P, 2, HQ, DH])
        q_sq = b.sb("at_qsq", [P, HQ, DH])
        q_c = b.sb("at_qc", [P, 2, HQ, DH])
        q_b = b.sb("at_qb", [P, HQ, DH])
        q_n = b.sb("at_qn", [P, HQ, DH])
        q_two = b.sb("at_qtwo", [P, HQ, 2, DH])
        q_ss = b.sb("at_qss", [P, 2, HQ])
        q_mse = b.sb("at_qmse", [P, 2, HQ])
        q_rstd = b.sb("at_qrstd", [P, 2, HQ])
        qt = b.sb("at_qt", [P, 2, HQ, P], F32R)
        sm = b.sb("at_sm", [P, 4, WIN])
        pr = b.sb("at_pr", [P, 4, WIN])
        pt = b.sb("at_pt", [P, 2, 3, P])
        nm = b.sb("at_nm", [P, 2, HQ])
        rowsum = b.sb("at_rowsum", [P, 2, HQ])
        t1 = b.sb("at_t1", [P, HQ])
        es = b.sb("at_es", [P, HQ])
        den = b.sb("at_den", [P, HQ])
        rec = b.sb("at_rec", [P, HQ])
        o_sb = b.sb("at_o", [P, HQ, DH])
        ot = b.sb("at_ot", [P, KC * P])
        s_ps = b.ps("at_sps", [P, 2, PW])
        t_ps = b.ps("at_tps", [P, 2, 4, P])
        o_ps = b.ps("at_ops", [P, HQ, DH])
        x_ps = b.ps("at_xps", [P, 2, 4, P])
        names = ("const", "kvl", "vl", "ksq", "kred", "krs", "kprep", "ktwice", "kt", "khi", "klo", "half", "table",
                 "qss", "qred", "qpow", "qmse", "qrot", "qn", "qhi", "qlo", "s", "m", "e", "t", "pt", "v",
                 "t1", "es", "den", "oscaled", "x", "xcopy", "ready")
        S = {n: b.sem(f"at_s_{n}") for n in names}
        q_loaded, m_loaded = b.sems("at_ql", 2), b.sems("at_ml", 2)
        stored = b.sem("at_stored")
        block = b.block()

        def blk(t):
            return (t if t < TP else t + 1) if isinstance(t, int) else t

        def key_bank(t):
            return t_ps[:, t % 4] if t % 4 < 2 else s_ps[:, t % 4 - 2].rearrange("p (h n) -> p h n", n=P)

        def tile_loop(engine, body):
            for s in range(2):
                body(s, s)
            with engine.Fori(1, TP // 2) as j:
                for s in range(2):
                    body(2 * j + s, s)
            for s in range(2):
                body(TP + s, s)

        @block.sync
        def _(sp):
            kv = proj.rearrange("(t p) n -> p t n", p=P)
            loads = [(ident[:, :], ident_dram), (rope[:, :, :, :], rope_dram),
                     (wrow[:, 0], q_w.broadcast_to([P, DH])), (wrow[:, 2], k_w.broadcast_to([P, DH])),
                     (wrow[:, 1, 0:32], q_w[:, 32:64].broadcast_to([P, 32])),
                     (wrow[:, 1, 32:64], q_w[:, 0:32].broadcast_to([P, 32])),
                     (wrow[:, 3, 0:32], k_w[:, 32:64].broadcast_to([P, 32])),
                     (wrow[:, 3, 32:64], k_w[:, 0:32].broadcast_to([P, 32])),
                     (sinkb[:, :], sink.broadcast_to([P, HQ]))]
            sp.dma_start(k_raw[:, :, :, :], kv[:, :, 1024:1280]).then_inc(S["kvl"], 16)
            for dst, src in loads:
                sp.dma_start(dst, src).then_inc(S["const"], 16)
            sp.dma_start(v_sb[:, 1:1 + TP, :], kv[:, 0:TP, 1280:1536]).then_inc(S["vl"], 16)
            sp.dma_start(v_sb[:, TP + 2:TP + 2 + TS, :], kv[:, TP:NT, 1280:1536]).then_inc(S["vl"], 16)

            def load(t, s):
                if not (isinstance(t, int) and t < 2):
                    sp.wait_ge(S["qrot"], t - 1)
                    sp.wait_ge(S["qss"], t - 1)
                rows = slice(t * P, (t + 1) * P) if isinstance(t, int) else ds(t * P, P)
                sp.dma_start(q_raw[:, s], proj[rows, 0:1024]).then_inc(q_loaded[s], 16)
                if not (isinstance(t, int) and t < 2):
                    sp.wait_ge(S["m"], HQ * (t - 1))
                sp.dma_start(mask[:, s], mask_dram[t] if isinstance(t, int) else mask_dram[ds(t, 1)]
                             ).then_inc(m_loaded[s], 16)

            tile_loop(sp, load)

        @block.gpsimd
        def _(pool):
            g = nc.gpsimd
            g.memset(half[:, :], -0.5).then_inc(S["half"], 1)
            g.memset(eps[:, :], EPS).then_inc(S["half"], 1)
            pool.wait_ge(S["half"], 2)
            pool.wait_ge(S["kred"], 1)
            g.tensor_tensor(k_mse[:, :], k_ss[:, :], eps[:, :], ALU.add).then_inc(S["krs"], 1)
            pool.wait_ge(S["krs"], 1)
            g.tensor_tensor(k_rstd[:, :], k_mse[:, :], half[:, :], ALU.pow).then_inc(S["krs"], 1)
            pool.wait_ge(S["table"], 4)

            def queries(t, s):
                j = t if isinstance(t, int) else (t - s)
                pos = (t % TP) if isinstance(t, int) else t
                first = isinstance(t, int) and t < 2
                pool.wait_ge(q_loaded[s], (16 * (t // 2 + 1)) if isinstance(t, int) else 8 * (t - s) + 16)
                if not (isinstance(t, int) and t == 0):
                    pool.wait_ge(S["qlo"], t)
                tab = [table[:, i, pos:pos + 1, :] if isinstance(pos, int) else table[:, i, ds(pos, 1), :]
                       for i in range(2)]
                g.tensor_tensor(q_c[:, s], q_raw[:, s], bc(tab[0], [P, HQ, DH]), ALU.mult).then_inc(S["qpow"], 1)
                for lo_, hi_ in ((0, 32), (32, 64)):
                    g.tensor_tensor(q_b[:, :, lo_:lo_ + 32], q_raw[:, s, :, 32 - lo_:64 - lo_],
                                    bc(tab[1][:, :, lo_:hi_], [P, HQ, 32]), ALU.mult).then_inc(S["qpow"], 1)
                pool.wait_ge(S["qpow"], 3 * t + 3)
                g.tensor_tensor(q_c[:, s], q_c[:, s], q_b[:, :, :], ALU.add).then_inc(S["qrot"], 1)
                pool.wait_ge(S["qred"], t + 1)
                g.tensor_tensor(q_mse[:, s], q_ss[:, s], eps[:, 0:HQ], ALU.add).then_inc(S["qmse"], 1)
                pool.wait_ge(S["qmse"], 2 * t + 1)
                g.tensor_tensor(q_rstd[:, s], q_mse[:, s], half[:, 0:HQ], ALU.pow).then_inc(S["qmse"], 1)
                pool.wait_ge(S["qmse"], 2 * t + 2)
                g.tensor_tensor(q_n[:, :, :], q_c[:, s], bc(q_rstd[:, s].unsqueeze(2), [P, HQ, DH]),
                                ALU.mult).then_inc(S["qn"], 1)
                pool.wait_ge(S["qhi"], t + 1)
                g.tensor_tensor(q_two[:, :, 1].bitcast(F32R), q_n[:, :, :], q_two[:, :, 0],
                                ALU.subtract).then_inc(S["qlo"], 1)

            tile_loop(pool, queries)

        def q_loaded_value(t, s):
            return 16 * (t // 2 + 1) if isinstance(t, int) else 8 * (t - s) + 16

        def units_before(t):
            return 4 if isinstance(t, int) and t == 0 else 6 * t + 2

        def o_unit_no(t, c):
            return 6 * t + 3 + c

        def q_unit_no(t, c):
            return 5 + c if isinstance(t, int) and t == 0 else 6 * t + 5 + c

        def square(act, t, s):
            act.wait_ge(q_loaded[s], q_loaded_value(t, s))
            if not (isinstance(t, int) and t == 0):
                act.wait_ge(S["qred"], t)
            nc.scalar.activation(q_sq[:, :, :], q_raw[:, s], ACT.Square, scale=DH ** -0.5).then_inc(S["qss"], 1)

        def high(act, t):
            act.wait_ge(S["qn"], t + 1)
            if not (isinstance(t, int) and t == 0):
                act.wait_ge(S["x"], units_before(t - 1))
            nc.scalar.activation(q_two[:, :, 0].bitcast(F32R), q_n[:, :, :], ACT.Copy).then_inc(S["qhi"], 1)

        def q_evac(act, s, c, n):
            act.wait_ge(S["x"], n)
            nc.scalar.activation(qt[:, s, 4 * c:4 * c + 4], x_ps[:, c % 2], ACT.Copy).then_inc(S["xcopy"], 1)

        @block.scalar
        def _(act):
            act.wait_ge(S["kvl"], 16)
            nc.scalar.activation(k_a[:, :, :, :], k_raw[:, :, :, :], ACT.Square, scale=DH ** -0.5).then_inc(S["ksq"], 1)
            square(act, 0, 0)
            act.wait_ge(S["kprep"], 8)
            nc.scalar.activation(k_two[:, :, :, 1], k_two[:, :, :, 0], ACT.Copy).then_inc(S["ktwice"], 1)
            high(act, 0)
            for t in range(NT):
                act.wait_ge(S["kt"], t + 1)
                nc.scalar.activation(kt_hi[:, :, (blk(t) + 1) * P:(blk(t) + 2) * P], key_bank(t), ACT.Copy
                                     ).then_inc(S["khi"], 1)
            for c in range(4):
                q_evac(act, 0, c, c + 1)

            def tile(t, s):
                last = isinstance(t, int) and t == NT - 1
                zero = isinstance(t, int) and t == 0
                for h in range(HQ):
                    n = HQ * t + h
                    act.wait_ge(S["m"], n + 1)
                    if not (zero and h < 4):
                        act.wait_ge(S["t"], n - 3)
                    nc.scalar.activation(pr[:, h % 4], sm[:, h % 4], ACT.Exp, bias=nm[:, s, h:h + 1],
                                         scale=-1.0, accum_out=rowsum[:, s, h:h + 1]).then_inc(S["e"], 1)
                    if h == 0 and not last:
                        square(act, t + 1, 1 - s)
                    if h == 1 and not zero:
                        sink_exp(t - 1, 1)
                    if h == 10:
                        sink_exp(t, 0)
                    if h in (7, 8) and not zero:
                        output_evac(t - 1, h - 7, o_unit_no(t, h - 7))
                    if h == 4 and not last:
                        high(act, t + 1)
                    if 11 <= h < 15 and not last:
                        q_evac(act, 1 - s, h - 11, q_unit_no(t, h - 11))

            def sink_exp(t, c):
                act.wait_ge(S["t1"], 2 * t + c + 1)
                if not (isinstance(t, int) and t == 0):
                    act.wait_ge(S["den"], 4 * (t - 1) + 2 * c + 1)
                nc.scalar.activation(es[:, 8 * c:8 * c + 8], t1[:, 8 * c:8 * c + 8], ACT.Exp).then_inc(S["es"], 1)

            def output_evac(t, c, u):
                act.wait_ge(S["x"], u)
                if c == 0 and not (isinstance(t, int) and t == 0):
                    act.wait_ge(stored, 16 * t)
                nc.scalar.activation(ot[:, 4 * c * P:4 * (c + 1) * P], x_ps[:, c], ACT.Copy).then_inc(S["xcopy"], 1)
                if c == 1:
                    act.wait_ge(S["xcopy"], u)
                    dst = mix_t[t] if isinstance(t, int) else mix_t[ds(t, 1)]
                    act.dma_start(dst[..., 0:KC * P], ot[:, :]).then_inc(stored, 16)

            tile_loop(act, tile)
            sink_exp(NT - 1, 1)
            for c in range(2):
                output_evac(NT - 1, c, units_before(NT - 1) + 3 + c)
            act.wait_ge(stored, 16 * NT)

        @block.vector
        def _(dve):
            v = nc.vector
            for z in (0, TP + 1, KB - 1):
                v.memset(v_sb[:, z], 0.0)
                v.memset(kt_hi[:, :, z * P:(z + 1) * P].bitcast(FP32), 0.0)
                v.memset(kt_lo[:, :, z * P:(z + 1) * P].bitcast(FP32), 0.0)

            def reduce(t, s):
                dve.wait_ge(S["qss"], t + 1)
                if not (isinstance(t, int) and t < 2):
                    dve.wait_ge(S["qmse"], 2 * (t - 1))
                v.reduce_sum(q_ss[:, s], q_sq[:, :, :], AX.X).then_inc(S["qred"], 1)

            dve.wait_ge(S["ksq"], 1)
            v.reduce_sum(k_ss[:, :], k_a[:, :, :, :], AX.X).then_inc(S["kred"], 1)
            dve.wait_ge(S["const"], 16 * 9)
            for i in range(4):
                v.tensor_tensor(table[:, i], rope[:, i % 2], bc(wrow[:, i:i + 1, :], [P, TP, DH]),
                                ALU.mult).then_inc(S["table"], 1)
            v.tensor_scalar(nsink[:, :], sinkb[:, :], -1.0, None, ALU.mult).then_inc(S["table"], 1)
            reduce(0, 0)
            dve.wait_ge(S["table"], 5)
            dve.wait_ge(S["kred"], 1)
            n = 0
            for t0, m in ((0, TP), (TP, TS)):
                c = table[:, 2, 0:m].unsqueeze(2)
                sn = table[:, 3, 0:m].unsqueeze(2)
                v.tensor_tensor(k_a[:, t0:t0 + m], k_raw[:, t0:t0 + m], bc(c, [P, m, HKV, DH]),
                                ALU.mult).then_inc(S["kprep"], 1)
                for a in (0, 32):
                    v.tensor_tensor(k_b[:, t0:t0 + m, :, a:a + 32], k_raw[:, t0:t0 + m, :, 32 - a:64 - a],
                                    bc(sn[:, :, :, a:a + 32], [P, m, HKV, 32]),
                                    ALU.mult).then_inc(S["kprep"], 1)
            dve.wait_ge(S["kprep"], 6)
            v.tensor_tensor(k_a[:, :, :, :], k_a[:, :, :, :], k_b[:, :, :, :], ALU.add).then_inc(S["kprep"], 1)
            dve.wait_ge(S["kprep"], 7)
            dve.wait_ge(S["krs"], 2)
            kr = k_rstd[:, :].rearrange("p (t h) -> p t h", h=HKV).unsqueeze(3)
            v.tensor_tensor(k_two[:, :, :, 0], k_a[:, :, :, :], bc(kr, [P, NT, HKV, DH]),
                            ALU.mult).then_inc(S["kprep"], 1)

            for t in range(NT):
                cols = slice((blk(t) + 1) * P, (blk(t) + 2) * P)
                dve.wait_ge(S["khi"], t + 1)
                v.tensor_tensor(kt_lo[:, :, cols], key_bank(t), kt_hi[:, :, cols].bitcast(FP32),
                                ALU.subtract).then_inc(S["klo"], 1)

            def finish(t, s, c):
                n = 4 * t + 2 * c
                heads = slice(8 * c, 8 * c + 8)
                dve.wait_ge(S["es"], 2 * t + c + 1)
                v.tensor_tensor(den[:, heads], rowsum[:, s, heads], es[:, heads], ALU.add).then_inc(S["den"], 1)
                dve.wait_ge(S["den"], n + 1)
                v.reciprocal(rec[:, heads], den[:, heads]).then_inc(S["den"], 1)
                dve.wait_ge(S["den"], n + 2)
                dve.wait_ge(S["v"], HQ * t + 8 * c + 8)
                if not (isinstance(t, int) and t == 0):
                    dve.wait_ge(S["x"], o_unit_no(t, c))
                v.tensor_tensor(o_sb[:, heads], o_ps[:, heads], bc(rec[:, heads].unsqueeze(2), [P, 8, DH]),
                                ALU.mult).then_inc(S["oscaled"], 1)

            def sink_term(t, s, c):
                heads = slice(8 * c, 8 * c + 8)
                dve.wait_ge(S["m"], HQ * t + 8 * c + 8)
                if not (isinstance(t, int) and t == 0):
                    dve.wait_ge(S["es"], 2 * t + c - 1)
                v.tensor_tensor(t1[:, heads], nm[:, s, heads], sinkb[:, heads], ALU.add).then_inc(S["t1"], 1)

            def copy_pt(n, h):
                dve.wait_ge(S["t"], n + 1)
                if not (isinstance(n, int) and n < 2):
                    dve.wait_ge(S["v"], n - 1)
                v.tensor_copy(pt[:, h % 2], t_ps[:, h % 2, 0:3]).then_inc(S["pt"], 1)

            def tile(t, s):
                last = isinstance(t, int) and t == NT - 1
                zero = isinstance(t, int) and t == 0
                dve.wait_ge(m_loaded[s], q_loaded_value(t, s))
                for h in range(HQ):
                    n = HQ * t + h
                    if h == 0 and not zero:
                        sink_term(t - 1, 1 - s, 1)
                    if h == 9:
                        sink_term(t, s, 0)
                    if not (zero and h < 3):
                        copy_pt(n - 3, h + 1)
                    dve.wait_ge(S["s"], n + 1)
                    if not (zero and h < 4):
                        dve.wait_ge(S["e"], n - 3)
                    dve.sem_inc(S["ready"], 1)
                    v.tensor_tensor_reduce(out=sm[:, h % 4], in0=s_ps[:, h % 2, 0:WIN], in1=mask[:, s],
                                           scale=-(DH ** -0.5), scalar=nsink[:, h:h + 1], op0=ALU.add,
                                           op1=ALU.min, accum_out=nm[:, s, h:h + 1]).then_inc(S["m"], 1)
                    if h == 4 and not zero:
                        finish(t - 1, 1 - s, 1)
                    if h == 12:
                        finish(t, s, 0)
                    if h == 1 and not last:
                        reduce(t + 1, 1 - s)

            tile_loop(dve, tile)
            for n in range(HQ * NT - 3, HQ * NT):
                copy_pt(n, n % 2)
            sink_term(NT - 1, 1, 1)
            finish(NT - 1, 1, 1)

        @block.tensor
        def _(pe):
            T = nc.tensor
            pe.wait_ge(S["const"], 16 * 9)
            pe.wait_ge(S["ktwice"], 1)

            for t in range(NT):
                if t >= 4:
                    pe.wait_ge(S["klo"], t - 3)
                for j in range(HKV):
                    m = T.transpose(key_bank(t)[:, j], k_two[:, t, j], ident[:, :])
                m.then_inc(S["kt"], 1)
            pe.wait_ge(S["klo"], NT)

            def q_unit(c, n):
                if not (isinstance(n, int) and n <= 2):
                    pe.wait_ge(S["xcopy"], n - 2)
                for h in range(4):
                    m = T.transpose(x_ps[:, c % 2, h], q_two[:, 4 * c + h], ident[:, :])
                m.then_inc(S["x"], 1)

            pe.wait_ge(S["vl"], 32)
            pe.wait_ge(S["qlo"], 1)
            for c in range(4):
                q_unit(c, c + 1)

            def o_unit(t, c, u):
                pe.wait_ge(S["oscaled"], 2 * t + c + 1)
                pe.wait_ge(S["xcopy"], u - 2)
                for k in range(4):
                    i = 4 * c + k
                    m = T.transpose(x_ps[:, c, k], o_sb[:, 2 * i:2 * i + 2], ident[:, :])
                m.then_inc(S["x"], 1)

            def weights_t(n, h):
                pe.wait_ge(S["e"], n + 1)
                if not (isinstance(n, int) and n < 2):
                    pe.wait_ge(S["pt"], n - 1)
                for k in range(3):
                    m = T.transpose(t_ps[:, h % 2, k], pr[:, h % 4, k * P:(k + 1) * P], ident[:, :])
                m.then_inc(S["t"], 1)

            def values(n, t, h):
                pe.wait_ge(S["pt"], n + 1)
                if h % 8 == 0 and not (isinstance(t, int) and t == 0):
                    pe.wait_ge(S["oscaled"], 2 * t - 1 + h // 8)
                g = (h // 4) * DH
                for k in range(3):
                    kb = blk(t) + k
                    rhs = v_sb[:, kb, g:g + DH] if isinstance(kb, int) else v_sb[:, ds(kb, 1), g:g + DH]
                    m = T.matmul(o_ps[:, h], pt[:, h % 2, k], rhs, start=(k == 0), stop=(k == 2))
                m.then_inc(S["v"], 1)

            def tile(t, s):
                last = isinstance(t, int) and t == NT - 1
                zero = isinstance(t, int) and t == 0
                pe.wait_ge(S["xcopy"], units_before(t))
                for h in range(HQ):
                    n = HQ * t + h
                    if not (zero and h < 2):
                        pe.wait_ge(S["m"], n - 1)
                    k0 = blk(t) * P
                    cols = slice(k0, k0 + WIN) if isinstance(k0, int) else ds(k0, WIN)
                    T.matmul(s_ps[:, h % 2, 0:WIN], qt[:, s, h], kt_hi[:, h // 4, cols], start=True, stop=False)
                    T.matmul(s_ps[:, h % 2, 0:WIN], qt[:, s, h], kt_lo[:, h // 4, cols], start=False,
                             stop=True).then_inc(S["s"], 1)
                    if not (zero and h < 4):
                        if h >= 4:
                            values(n - 4, t, h - 4)
                        else:
                            values(n - 4, t - 1, h + HQ - 4)
                    if not (zero and h < 2):
                        weights_t(n - 2, (h + 2) % 4)
                    if h in (6, 7) and not zero:
                        o_unit(t - 1, h - 6, o_unit_no(t, h - 6))
                    if 10 <= h < 14 and not last:
                        if h == 10:
                            pe.wait_ge(S["qlo"], t + 2)
                        q_unit(h - 10, q_unit_no(t, h - 10))

            tile_loop(pe, tile)
            weights_t(HQ * NT - 2, 2)
            values(HQ * NT - 4, NT - 1, HQ - 4)
            weights_t(HQ * NT - 1, 3)
            for h in range(HQ - 3, HQ):
                values(HQ * (NT - 1) + h, NT - 1, h)
            for c in range(2):
                o_unit(NT - 1, c, units_before(NT - 1) + 3 + c)


def memory(nc, proj, mem_proj, ident_dram, small, mix_t):
    MT = NMT // 2
    NK = MT * P
    SC = DM ** -0.5
    with ExitStack() as ctx:
        b = Bufs(nc, ctx)
        ident = b.sb("me_ident", [P, P])
        wq = b.sb("me_wq", [P, 1, DM])
        wk = b.sb("me_wk", [P, 1, DM])
        half = b.sb("me_half", [P, NMT * HM])
        eps = b.sb("me_eps", [P, NMT * HM])
        k_raw = b.sb("me_kraw", [P, NMT, HM, DM])
        k_sq = b.sb("me_ksq", [P, NMT, HM, DM])
        k_n = b.sb("me_kn", [P, NMT, HM, DM])
        k_ss = b.sb("me_kss", [P, NMT * HM])
        k_mse = b.sb("me_kmse", [P, NMT * HM])
        k_rstd = b.sb("me_krstd", [P, NMT * HM])
        v_sb = b.sb("me_v", [P, NMT, HM, DM])
        kt = b.sb("me_kt", [P, HM, NMT * P])
        q_raw = b.sb("me_qraw", [P, 2, HM, DM])
        q_sq = b.sb("me_qsq", [P, HM, DM])
        q_w = b.sb("me_qw", [P, HM, DM])
        q_n = b.sb("me_qn", [P, HM, DM])
        q_ss = b.sb("me_qss", [P, HM])
        q_mse = b.sb("me_qmse", [P, HM])
        q_rstd = b.sb("me_qrstd", [P, HM])
        qt = b.sb("me_qt", [P, HM, P])
        mx = b.sb("me_mx", [P, HM])
        nm = b.sb("me_nm", [P, HM])
        rowsum = b.sb("me_rowsum", [P, 2, HM])
        rec = b.sb("me_rec", [P, HM])
        pr = b.sb("me_pr", [P, HM, NK])
        pt = b.sb("me_pt", [P, 2, HM, MT, P])
        o_sb = b.sb("me_o", [P, HM, DM])
        ot = b.sb("me_ot", [P, HM * P])
        s_ps = b.ps("me_sps", [P, HM, NK])
        t_ps = b.ps("me_tps", [P, HM, MT, P])
        q_ps = b.ps("me_qps", [P, HM, P])
        o_ps = b.ps("me_ops", [P, HM, DM])
        ot_ps = b.ps("me_otps", [P, HM, P])
        S = {n: b.sem(f"me_s_{n}") for n in (
            "const", "kv", "v", "ksq", "kred", "kpow", "kn", "kt", "kcopy", "half",
            "sq", "red", "pow", "qw", "qn", "qt", "qcopy", "s", "mx", "nm", "e", "t", "tcopy", "o", "rec",
            "oscaled", "ot", "otcopy")}
        q_loaded = b.sems("me_ql", 2)
        stored = b.sem("me_stored")
        block = b.block()

        def steps(engine, body, first=0, last=NT):
            for t in range(first, 4):
                body(t, t % 2)
            with engine.Fori(2, TP // 2) as j:
                for s in range(2):
                    body(2 * j + s, s)
            for t in range(TP, last):
                body(t, t % 2)

        def is0(t, n=0):
            return isinstance(t, int) and t <= n

        @block.sync
        def _(sp):
            kv = mem_proj.rearrange("(t p) n -> p t n", p=P)
            sp.dma_start(k_raw[:, :, :, :], kv[:, :, 0:512]).then_inc(S["kv"], 16)
            for dst, src in ((ident[:, :], ident_dram), (wq[:, 0], small["mq_norm_w"].broadcast_to([P, DM])),
                             (wk[:, 0], small["mk_norm_w"].broadcast_to([P, DM]))):
                sp.dma_start(dst, src).then_inc(S["const"], 16)
            sp.dma_start(v_sb[:, :, :, :], kv[:, :, 512:1024]).then_inc(S["v"], 16)

            def load(t, s):
                if not is0(t, 1):
                    sp.wait_ge(S["sq"], t - 1)
                    sp.wait_ge(S["qw"], t - 1)
                rows = slice(t * P, (t + 1) * P) if isinstance(t, int) else ds(t * P, P)
                sp.dma_start(q_raw[:, s], proj[rows, 2048:2560]).then_inc(q_loaded[s], 16)

            steps(sp, load)

        def is_last(t, n):
            return isinstance(t, int) and t >= NT - n

        def loaded(t, s):
            return 16 * (t // 2 + 1) if isinstance(t, int) else 8 * (t - s) + 16

        @block.gpsimd
        def _(pool):
            g = nc.gpsimd
            g.memset(half[:, :], -0.5).then_inc(S["half"], 1)
            g.memset(eps[:, :], EPS).then_inc(S["half"], 1)
            pool.wait_ge(S["half"], 2)
            pool.wait_ge(S["kred"], 1)
            g.tensor_tensor(k_mse[:, :], k_ss[:, :], eps[:, :], ALU.add).then_inc(S["kpow"], 1)
            pool.wait_ge(S["kpow"], 1)
            g.tensor_tensor(k_rstd[:, :], k_mse[:, :], half[:, :], ALU.pow).then_inc(S["kpow"], 1)
            pool.wait_ge(S["const"], 48)

            def queries(t, s):
                pool.wait_ge(q_loaded[s], loaded(t, s))
                if not is0(t):
                    pool.wait_ge(S["qn"], t)
                g.tensor_tensor(q_w[:, :, :], q_raw[:, s], bc(wq[:, :, :], [P, HM, DM]), ALU.mult
                                ).then_inc(S["qw"], 1)
                pool.wait_ge(S["red"], t + 1)
                g.tensor_tensor(q_mse[:, :], q_ss[:, :], eps[:, 0:HM], ALU.add).then_inc(S["pow"], 1)
                pool.wait_ge(S["pow"], 2 * t + 1)
                g.tensor_tensor(q_rstd[:, :], q_mse[:, :], half[:, 0:HM], ALU.pow).then_inc(S["pow"], 1)

            steps(pool, queries)

        @block.scalar
        def _(act):
            a = nc.scalar
            act.wait_ge(S["kv"], 16)
            a.activation(k_sq[:, :, :, :], k_raw[:, :, :, :], ACT.Square, scale=SC).then_inc(S["ksq"], 1)
            for i in range(2):
                for m in range(2):
                    act.wait_ge(S["kt"], 2 * i + m + 1)
                    k = 2 * i + m
                    a.activation(kt[:, :, k * P:(k + 1) * P], (t_ps[:, 0:2] if m == 0 else t_ps[:, 2:4]
                                 ).rearrange("p a b c -> p (a b) c"), ACT.Copy).then_inc(S["kcopy"], 1)

            def square(t, s):
                act.wait_ge(q_loaded[s], loaded(t, s))
                if not is0(t):
                    act.wait_ge(S["red"], t)
                a.activation(q_sq[:, :, :], q_raw[:, s], ACT.Square, scale=SC).then_inc(S["sq"], 1)

            def q_copy(t):
                act.wait_ge(S["qt"], t + 1)
                if not is0(t):
                    act.wait_ge(S["s"], 2 * t)
                a.activation(qt[:, :, :], q_ps[:, :, :], ACT.Copy).then_inc(S["qcopy"], 1)

            square(0, 0)
            q_copy(0)
            square(1, 1)

            def tile(t, s):
                if not is_last(t, 2):
                    square(t + 2, s)
                if not is0(t, 1):
                    act.wait_ge(S["rec"], t - 1)
                for c in range(2):
                    act.wait_ge(S["nm"], 2 * t + c + 1)
                    if not is0(t):
                        act.wait_ge(S["t"], 2 * t + c - 1)
                    for h in (2 * c, 2 * c + 1):
                        m = a.activation(pr[:, h], s_ps[:, h], ACT.Exp, bias=nm[:, h:h + 1], scale=SC,
                                         accum_out=rowsum[:, s, h:h + 1])
                    m.then_inc(S["e"], 1)
                if not is_last(t, 1):
                    q_copy(t + 1)
                if not is0(t, 2):
                    store(t - 3)

            def store(t):
                act.wait_ge(S["ot"], t + 1)
                if not is0(t):
                    act.wait_ge(stored, 16 * t)
                a.activation(ot[:, :], ot_ps[:, :, :], ACT.Copy).then_inc(S["otcopy"], 1)
                act.wait_ge(S["otcopy"], t + 1)
                dst = mix_t[t] if isinstance(t, int) else mix_t[ds(t, 1)]
                act.dma_start(dst[..., 12 * P:16 * P], ot[:, :]).then_inc(stored, 16)

            steps(act, tile)
            for t in range(NT - 3, NT):
                store(t)
            act.wait_ge(stored, 16 * NT)

        @block.vector
        def _(dve):
            v = nc.vector
            dve.wait_ge(S["ksq"], 1)
            v.reduce_sum(k_ss[:, :], k_sq[:, :, :, :], AX.X).then_inc(S["kred"], 1)
            dve.wait_ge(S["const"], 48)
            dve.wait_ge(S["kv"], 16)
            v.tensor_tensor(k_n[:, :, :, :], k_raw[:, :, :, :], bc(wk[:, :, :].unsqueeze(1), [P, NMT, HM, DM]),
                            ALU.mult).then_inc(S["kn"], 1)
            dve.wait_ge(S["kpow"], 2)
            dve.wait_ge(S["kn"], 1)
            kr = k_rstd[:, :].rearrange("p (t h) -> p t h", h=HM).unsqueeze(3)
            v.tensor_tensor(k_n[:, :, :, :], k_n[:, :, :, :], bc(kr, [P, NMT, HM, DM]), ALU.mult
                            ).then_inc(S["kn"], 1)

            def queries(t):
                dve.wait_ge(S["sq"], t + 1)
                if not is0(t):
                    dve.wait_ge(S["pow"], 2 * t)
                v.reduce_sum(q_ss[:, :], q_sq[:, :, :], AX.X).then_inc(S["red"], 1)
                dve.wait_ge(S["pow"], 2 * t + 2)
                dve.wait_ge(S["qw"], t + 1)
                if not is0(t):
                    dve.wait_ge(S["qt"], t)
                v.tensor_tensor(q_n[:, :, :], q_w[:, :, :], bc(q_rstd[:, :].unsqueeze(2), [P, HM, DM]),
                                ALU.mult).then_inc(S["qn"], 1)

            queries(0)
            queries(1)

            def invert(t, s):
                if not is0(t):
                    dve.wait_ge(S["oscaled"], t)
                dve.wait_ge(S["e"], 2 * t + 2)
                v.reciprocal(rec[:, :], rowsum[:, s]).then_inc(S["rec"], 1)

            def scale(t):
                dve.wait_ge(S["rec"], t + 1)
                dve.wait_ge(S["o"], t + 1)
                if not is0(t):
                    dve.wait_ge(S["ot"], t)
                v.tensor_tensor(o_sb[:, :, :], o_ps[:, :, :], bc(rec[:, :].unsqueeze(2), [P, HM, DM]),
                                ALU.mult).then_inc(S["oscaled"], 1)

            def tile(t, s):
                if not is0(t, 1):
                    invert(t - 2, s)
                for c in range(2):
                    two = slice(2 * c, 2 * c + 2)
                    dve.wait_ge(S["s"], 2 * t + c + 1)
                    if not is0(t):
                        dve.wait_ge(S["nm"], 2 * t + c - 1)
                    v.reduce_max(mx[:, two], s_ps[:, two, :], AX.X).then_inc(S["mx"], 1)
                    dve.wait_ge(S["mx"], 2 * t + c + 1)
                    if not is0(t):
                        dve.wait_ge(S["e"], 2 * t + c - 1)
                    v.tensor_scalar(nm[:, two], mx[:, two], -SC, None, ALU.mult).then_inc(S["nm"], 1)
                if not is0(t, 1):
                    scale(t - 2)
                if not is_last(t, 2):
                    queries(t + 2)
                if not is0(t, 1):
                    dve.wait_ge(S["o"], t - 1)
                for c in range(2):
                    dve.wait_ge(S["t"], 2 * t + c + 1)
                    v.tensor_copy(pt[:, s, 2 * c:2 * c + 2], t_ps[:, 2 * c:2 * c + 2]).then_inc(S["tcopy"], 1)

            steps(dve, tile)
            for t in (NT - 2, NT - 1):
                invert(t, t % 2)
                scale(t)

        @block.tensor
        def _(pe):
            T = nc.tensor
            pe.wait_ge(S["const"], 48)
            pe.wait_ge(S["kn"], 2)
            for k in range(NMT):
                if k >= 2:
                    pe.wait_ge(S["kcopy"], k - 1)
                for h in range(HM):
                    m = T.transpose(t_ps[:, 2 * (k % 2) + h // 2, h % 2], k_n[:, k, h], ident[:, :])
                m.then_inc(S["kt"], 1)
            pe.wait_ge(S["kcopy"], NMT)
            pe.wait_ge(S["v"], 16)

            def q_t(t):
                pe.wait_ge(S["qn"], t + 1)
                if not is0(t):
                    pe.wait_ge(S["qcopy"], t)
                for h in range(HM):
                    m = T.transpose(q_ps[:, h], q_n[:, h], ident[:, :])
                m.then_inc(S["qt"], 1)

            def scores(t, sequence, c):
                pe.wait_ge(S["qcopy"], t + 1)
                if not is0(t):
                    pe.wait_ge(S["e"], 2 * t + c - 1)
                c0 = sequence * NK
                for h in (2 * c, 2 * c + 1):
                    m = T.matmul(s_ps[:, h], qt[:, h], kt[:, h, c0:c0 + NK], start=True, stop=True)
                m.then_inc(S["s"], 1)

            def o_t(t):
                pe.wait_ge(S["oscaled"], t + 1)
                if not is0(t):
                    pe.wait_ge(S["otcopy"], t)
                for h in range(HM):
                    m = T.transpose(ot_ps[:, h], o_sb[:, h], ident[:, :])
                m.then_inc(S["ot"], 1)

            def seq(t):
                return int(isinstance(t, int) and t >= TP)

            def output(t, s, sequence):
                pe.wait_ge(S["tcopy"], 2 * t + 2)
                if not is0(t):
                    pe.wait_ge(S["oscaled"], t)
                for h in range(HM):
                    for k in range(MT):
                        m = T.matmul(o_ps[:, h], pt[:, s, h, k], v_sb[:, MT * sequence + k, h],
                                     start=(k == 0), stop=(k == MT - 1))
                m.then_inc(S["o"], 1)

            q_t(0)
            for c in range(2):
                scores(0, 0, c)

            def tile(t, s, last_of_prompt=False):
                if not is_last(t, 1):
                    q_t(t + 1)
                for c in range(2):
                    pe.wait_ge(S["e"], 2 * t + c + 1)
                    if not is0(t):
                        pe.wait_ge(S["tcopy"], 2 * t + c - 1)
                    for h in (2 * c, 2 * c + 1):
                        for k in range(MT):
                            m = T.transpose(t_ps[:, h, k], pr[:, h, k * P:(k + 1) * P], ident[:, :])
                    m.then_inc(S["t"], 1)
                if not is_last(t, 1):
                    for c in range(2):
                        scores(t + 1, 1 if last_of_prompt else seq(t), c)
                if not is0(t):
                    output(t - 1, 1 - s, int(isinstance(t, int) and t > TP))
                if not is0(t, 1):
                    o_t(t - 2)

            for t in range(2):
                tile(t, t)
            with pe.Fori(1, TP // 2 - 1) as j:
                for s in range(2):
                    tile(2 * j + s, s)
            for t in range(TP - 2, NT):
                tile(t, t % 2, t == TP - 1)
            output(NT - 1, 1, 1)
            o_t(NT - 2)
            o_t(NT - 1)


def ssm_backward(nc, xbc_c, ident_dram, R):
    XW = NS * PS
    with ExitStack() as ctx:
        b = Bufs(nc, ctx)
        ident = b.sb("sb_ident", [P, P])
        xc = b.sb("sb_xc", [P, 2, XBC])
        x_dec = b.sb("sb_xdec", [P, NS, PS])
        b_tok = b.sb("sb_btok", [P, NG, ST])
        state = b.sb("sb_state", [P, NS, PS])
        scaled = b.sb("sb_scaled", [P, NS, PS])
        x_ps = b.ps("sb_xps", [P, NS, PS])
        b_ps = b.ps("sb_bps", [P, NG, ST])
        s_ps = b.ps("sb_sps", [P, NS, PS])
        y_ps = b.ps("sb_yps", [P, NS, PS])
        S = {n: b.sem(f"sb_s_{n}") for n in ("const", "turn", "x", "b", "off", "st", "y", "h", "zero", "sp_ready", "dve_ready")}
        loaded = b.sems("sb_l", 2)
        block = b.block()
        y_back, e_acs, e_tot, dec = R["y_back"], R["e_acs"], R["e_tot"], R["dec"]

        def order(engine, body, reset=None):
            if reset:
                reset(0)
            for s in range(2):
                body(s, s, NT - 1 - s, s == 0)
            if reset:
                reset(1)
            with engine.Fori(1, NT // 2) as j:
                for s in range(2):
                    body(2 * j + s, s, NT - 1 - (2 * j + s), False)

        def at(buf, t, h0=None, n=None):
            tt = buf[:, t:t + 1] if isinstance(t, int) else buf[:, ds(t, 1)]
            return tt

        @block.sync
        def _(sp):
            sp.dma_start(ident[:, :], ident_dram).then_inc(S["const"], 16)

            def load(i, s, t, first):
                if not isinstance(i, int):
                    sp.wait_ge(S["off"], i - 1)
                sp.sem_inc(S["sp_ready"], 1)
                sp.dma_start(xc[:, s], xbc_c[t] if isinstance(t, int) else xbc_c[ds(t, 1)]
                             ).then_inc(loaded[s], 16)

            order(sp, load)

        def loaded_value(i, s):
            return 16 if isinstance(i, int) else 8 * (i - s) + 16

        @block.tensor
        def _(pe):
            T = nc.tensor
            pe.wait_ge(S["const"], 16)

            def body(i, s, t, first):
                pe.wait_ge(loaded[s], loaded_value(i, s))
                if not first:
                    pe.wait_ge(S["x"], i)
                    pe.wait_ge(S["b"], i)
                for c in range(4):
                    T.transpose(x_ps[:, 2 * c:2 * c + 2], xc[:, s, c * P:(c + 1) * P], ident[:, :])
                for g in range(NG):
                    m = T.transpose(b_ps[:, g], xc[:, s, (4 + g) * P:(5 + g) * P], ident[:, :])
                m.then_inc(S["turn"], 1)
                if first:
                    pe.wait_ge(S["zero"], 1)
                else:
                    pe.wait_ge(S["h"], 2 * i)
                    pe.wait_ge(S["y"], i)
                for g in range(NG):
                    m = T.matmul(y_ps[:, 4 * g:4 * g + 4], xc[:, s, (6 + g) * P:(7 + g) * P],
                                 state[:, 4 * g:4 * g + 4], start=True, stop=True)
                m.then_inc(S["off"], 1)
                pe.wait_ge(S["x"], i + 1)
                pe.wait_ge(S["b"], i + 1)
                for g in range(NG):
                    m = T.matmul(s_ps[:, 4 * g:4 * g + 4], b_tok[:, g], x_dec[:, 4 * g:4 * g + 4],
                                 start=True, stop=True)
                m.then_inc(S["st"], 1)

            def reset(k):
                if k:
                    pe.wait_ge(S["zero"], 2)

            order(pe, body, reset)

        @block.scalar
        def _(act):
            def body(i, s, t, first):
                act.wait_ge(S["turn"], i + 1)
                if not first:
                    act.wait_ge(S["st"], i)
                nc.scalar.activation(b_tok[:, :, :], b_ps[:, :, :], ACT.Copy).then_inc(S["b"], 1)

            order(act, body)

        @block.vector
        def _(dve):
            v = nc.vector

            def factor(buf, t):
                return bc(at(buf, t)[:, 0, NS:2 * NS].unsqueeze(2), [P, NS, PS])

            def body(i, s, t, first):
                dve.wait_ge(S["turn"], i + 1)
                if not first:
                    dve.wait_ge(S["st"], i)
                dve.sem_inc(S["dve_ready"], 1)
                v.tensor_tensor(x_dec[:, :, :], x_ps[:, :, :], factor(dec, t), ALU.mult).then_inc(S["x"], 1)
                dve.wait_ge(S["off"], i + 1)
                yb = y_back[:, t] if isinstance(t, int) else y_back[:, ds(t, 1)]
                yb = yb.rearrange("p (h q) -> p h q", q=PS) if isinstance(t, int) else \
                    yb.rearrange("p o (h q) -> p (o h) q", q=PS)
                v.tensor_tensor(yb, y_ps[:, :, :], factor(e_acs, t), ALU.mult).then_inc(S["y"], 1)
                v.tensor_tensor(scaled[:, :, :], state[:, :, :], factor(e_tot, t), ALU.mult).then_inc(S["h"], 1)
                dve.wait_ge(S["st"], i + 1)
                dve.wait_ge(S["h"], 2 * i + 1)
                v.tensor_tensor(state[:, :, :], scaled[:, :, :], s_ps[:, :, :], ALU.add).then_inc(S["h"], 1)

            def reset(k):
                if k:
                    dve.wait_ge(S["h"], 4)
                v.memset(state[:, :, :], 0.0).then_inc(S["zero"], 1)
                dve.wait_ge(S["zero"], k + 1)

            order(dve, body, reset)


def ssm_forward(nc, proj, xbc_c, ident_dram, small, R, mix_t):
    XW = NS * PS
    with ExitStack() as ctx:
        b = Bufs(nc, ctx)
        ident = b.sb("sf_ident", [P, P])
        wn = b.sb("sf_wn", [P, XW])
        dsk = b.sb("sf_dskip", [P, NS])
        half = b.sb("sf_half", [P, 1])
        eps = b.sb("sf_eps", [P, 1])
        z = b.sb("sf_z", [P, 2, XW])
        xc = b.sb("sf_xc", [P, 2, XBC])
        b_tok = b.sb("sf_btok", [P, NG, ST])
        x_tok = b.sb("sf_xtok", [P, NS, PS])
        x_dec = b.sb("sf_xdec", [P, NS, PS])
        x_dt = b.sb("sf_xdt", [P, 2, NS, PS])
        state = b.sb("sf_state", [P, NS, PS])
        scaled = b.sb("sf_scaled", [P, NS, PS])
        cb = b.sb("sf_cb", [P, 2, NG, 1, P])
        a_tri = b.sb("sf_atri", [P, 2, NS, P])
        acs_t = b.sb("sf_acst", [P, 2, 2 * NS])
        drop = b.sb("sf_drop", [P, 2, NS, P])
        m_t = b.sb("sf_mt", [P, 2, NS, P])
        y = b.sb("sf_y", [P, 2, XW])
        y2 = b.sb("sf_y2", [P, XW])
        sq = b.sb("sf_sq", [P, XW])
        ms = b.sb("sf_ms", [P, 1])
        mse = b.sb("sf_mse", [P, 1])
        rstd = b.sb("sf_rstd", [P, 1])
        yn = b.sb("sf_yn", [P, 2, XW])
        ot = b.sb("sf_ot", [P, XW])
        ones = b.sb("sf_ones", [P, P])
        x_ps = b.ps("sf_xps", [P, NS, PS])
        m_ps = b.ps("sf_mps", [P, 4, P])
        s_ps = b.ps("sf_sps", [P, NS, PS])
        y_ps = b.ps("sf_yps", [P, NS, PS])
        d_ps = b.ps("sf_dps", [P, NS, P])
        g_ps = b.ps("sf_gps", [P, NS, PS])
        t_ps = b.ps("sf_tps", [P, 4, P])
        S = {n: b.sem(f"sf_s_{n}") for n in (
            "const", "half", "ones", "turn", "xcopy", "bcopy", "xd", "off", "st", "h", "zero", "cb", "cbm", "atri",
            "rows", "acs", "drop", "e", "m", "diag", "y", "gated", "sq", "pow", "yn", "tn", "tcopy", "xdt")}
        loaded, z_loaded = b.sems("sf_l", 2), b.sems("sf_zl", 2)
        stored = b.sem("sf_stored")
        block = b.block()
        y_back, e_acs, e_tot, dec, dt, acs, a_sb, tri = (
            R[k] for k in ("y_back", "e_acs", "e_tot", "dec", "dt", "acs", "a", "tri"))

        def order(engine, body, reset=None):
            if reset:
                reset(0)
            for s in range(2):
                body(s, s)
            with engine.Fori(1, TP // 2) as j:
                for s in range(2):
                    body(2 * j + s, s)
            if reset:
                reset(1)
            for s in range(2):
                body(TP + s, s)

        def before(t, n):
            return isinstance(t, int) and t < n

        def loaded_value(t, s):
            return 16 * (t // 2 + 1) if isinstance(t, int) else 8 * (t - s) + 16

        def row(buf, t, lo_, hi_):
            r = buf[:, t:t + 1] if isinstance(t, int) else buf[:, ds(t, 1)]
            return r[:, 0, lo_:hi_].unsqueeze(2)

        @block.sync
        def _(sp):
            for dst, src in ((ident[:, :], ident_dram), (wn[:, :], small["ssm_norm_w"].broadcast_to([P, XW])),
                             (dsk[:, :], small["ssm_D"].broadcast_to([P, NS]))):
                sp.dma_start(dst, src).then_inc(S["const"], 16)

            def load(t, s):
                if not before(t, 2):
                    sp.wait_ge(S["cb"], t - 1)
                sp.dma_start(xc[:, s], xbc_c[t] if isinstance(t, int) else xbc_c[ds(t, 1)]
                             ).then_inc(loaded[s], 16)
                if not before(t, 2):
                    sp.wait_ge(S["gated"], 2 * (t - 1))
                rows = slice(t * P, (t + 1) * P) if isinstance(t, int) else ds(t * P, P)
                sp.dma_start(z[:, s], proj[rows, 1536:2048]).then_inc(z_loaded[s], 16)

            order(sp, load)

        @block.tensor
        def _(pe):
            T = nc.tensor
            pe.wait_ge(S["const"], 48)
            pe.wait_ge(S["ones"], 1)

            def within(t, first=False):
                pe.wait_ge(S["xdt"], 2 * t + 2)
                pe.wait_ge(S["m"], 2 * t + 2)
                if not first:
                    pe.wait_ge(S["gated"], 2 * t - 1)
                for h in range(NS):
                    for d in range(2):
                        m = T.matmul(g_ps[:, h], m_t[:, d, h], x_dt[:, d, h], start=(d == 0), stop=(d == 1))
                m.then_inc(S["diag"], 1)

            def turn_back(t, s, first=False):
                pe.wait_ge(S["yn"], t + 1)
                if not first:
                    pe.wait_ge(S["tcopy"], t)
                for c in range(4):
                    m = T.transpose(t_ps[:, c], yn[:, s, c * P:(c + 1) * P], ident[:, :])
                m.then_inc(S["tn"], 1)

            def body(t, s):
                first = before(t, 1)
                pe.wait_ge(loaded[s], loaded_value(t, s))
                if not first:
                    pe.wait_ge(S["xcopy"], t)
                    pe.wait_ge(S["bcopy"], t)
                    pe.wait_ge(S["cbm"], 2 * t)
                for c in range(4):
                    T.transpose(x_ps[:, 2 * c:2 * c + 2], xc[:, s, c * P:(c + 1) * P], ident[:, :])
                for g in range(NG):
                    m = T.transpose(m_ps[:, g], xc[:, s, (4 + g) * P:(5 + g) * P], ident[:, :])
                m.then_inc(S["turn"], 1)
                for d in range(2):
                    pe.wait_ge(S["atri"], 2 * t + d + 1)
                    if not (first and d == 0):
                        pe.wait_ge(S["drop"], 2 * t + d)
                    for g in range(NG):
                        m = T.matmul(d_ps[:, 4 * g:4 * g + 4], ones[:, :], a_tri[:, d, 4 * g:4 * g + 4],
                                     start=True, stop=True)
                    m.then_inc(S["rows"], 1)
                    if d == 0:
                        if first:
                            pe.wait_ge(S["zero"], 1)
                        else:
                            pe.wait_ge(S["h"], 2 * t)
                            pe.wait_ge(S["y"], 4 * t - 3)
                        for g in range(NG):
                            m = T.matmul(y_ps[:, 4 * g:4 * g + 4], xc[:, s, (6 + g) * P:(7 + g) * P],
                                         state[:, 4 * g:4 * g + 4], start=True, stop=True)
                        m.then_inc(S["off"], 1)
                        pe.wait_ge(S["bcopy"], t + 1)
                        for g in range(NG):
                            m = T.matmul(m_ps[:, 2 + g], xc[:, s, (4 + g) * P:(5 + g) * P],
                                         xc[:, s, (6 + g) * P:(7 + g) * P], start=True, stop=True)
                        m.then_inc(S["cb"], 1)
                        if not first:
                            within(t - 1, before(t, 2))
                        pe.wait_ge(S["xd"], t + 1)
                        for g in range(NG):
                            m = T.matmul(s_ps[:, 4 * g:4 * g + 4], b_tok[:, g], x_dec[:, 4 * g:4 * g + 4],
                                         start=True, stop=True)
                        m.then_inc(S["st"], 1)
                if not before(t, 2):
                    turn_back(t - 2, s, before(t, 3))

            def reset(k):
                if k:
                    pe.wait_ge(S["zero"], 2)

            order(pe, body, reset)
            within(NT - 1)
            turn_back(NT - 2, 0)
            turn_back(NT - 1, 1)

        @block.gpsimd
        def _(pool):
            g = nc.gpsimd
            g.memset(ones[:, :], 1.0).then_inc(S["ones"], 1)
            g.memset(half[:, :], -0.5).then_inc(S["half"], 1)
            g.memset(eps[:, :], EPS).then_inc(S["half"], 1)
            pool.wait_ge(S["half"], 2)

            def triangle_of(t, d, first=False):
                if not first:
                    pool.wait_ge(S["rows"], 2 * t + d - 1)
                g.tensor_tensor(a_tri[:, d], bc(row(a_sb, t, d * NS, (d + 1) * NS), [P, NS, P]),
                                bc(tri[:, d:d + 1, :], [P, NS, P]), ALU.mult).then_inc(S["atri"], 1)

            def rstd_of(t, first=False):
                pool.wait_ge(S["sq"], t + 1)
                g.tensor_tensor(mse[:, :], ms[:, :], eps[:, :], ALU.add).then_inc(S["pow"], 1)
                pool.wait_ge(S["pow"], 2 * t + 1)
                if not first:
                    pool.wait_ge(S["yn"], t)
                g.tensor_tensor(rstd[:, :], mse[:, :], half[:, :], ALU.pow).then_inc(S["pow"], 1)

            def body(t, s):
                pool.wait_ge(S["xcopy"], t + 1)
                for d in range(2):
                    if not before(t, 1):
                        pool.wait_ge(S["diag"], t)
                    g.tensor_tensor(x_dt[:, d], x_tok[:, :, :], bc(row(dt, t, d * NS, (d + 1) * NS), [P, NS, PS]),
                                    ALU.mult).then_inc(S["xdt"], 1)
                end = isinstance(t, int) and t == NT - 1
                if not end:
                    triangle_of(t + 1, 0)
                if not before(t, 1):
                    rstd_of(t - 1, before(t, 2))
                if not end:
                    triangle_of(t + 1, 1)

            for d in range(2):
                triangle_of(0, d, True)
            order(pool, body)
            rstd_of(NT - 1)

        @block.scalar
        def _(act):
            a = nc.scalar

            def squares(t, s, first=False):
                act.wait_ge(S["gated"], 2 * t + 2)
                if not first:
                    act.wait_ge(S["pow"], 2 * t - 1)
                    act.wait_ge(S["sq"], t)
                a.activation(sq[:, :], y[:, s], ACT.Square, scale=XW ** -0.5, accum_out=ms[:, :]
                             ).then_inc(S["sq"], 1)

            def store(t, first=False):
                act.wait_ge(S["tn"], t + 1)
                if not first:
                    act.wait_ge(stored, 16 * t)
                a.activation(ot[:, :], t_ps[:, :, :], ACT.Copy).then_inc(S["tcopy"], 1)
                act.wait_ge(S["tcopy"], t + 1)
                dst = mix_t[t] if isinstance(t, int) else mix_t[ds(t, 1)]
                act.dma_start(dst[..., 8 * P:12 * P], ot[:, :]).then_inc(stored, 16)

            def body(t, s):
                act.wait_ge(S["turn"], t + 1)
                if not before(t, 1):
                    act.wait_ge(S["st"], t)
                    act.wait_ge(S["y"], 4 * t - 2)
                    act.wait_ge(S["xdt"], 2 * t)
                    act.wait_ge(S["xd"], t)
                a.activation(b_tok[:, :, :], m_ps[:, 0:2], ACT.Copy).then_inc(S["bcopy"], 1)
                a.activation(x_tok[:, :, :], x_ps[:, :, :], ACT.Copy).then_inc(S["xcopy"], 1)
                act.wait_ge(S["acs"], t + 1)
                for d in range(2):
                    act.wait_ge(S["rows"], 2 * t + d + 1)
                    if not before(t, 1):
                        act.wait_ge(S["m"], 2 * t - 1 + d)
                    for h in range(NS):
                        m = a.activation(drop[:, d, h], d_ps[:, h], ACT.Relu, scale=-1.0,
                                         bias=acs_t[:, s, d * NS + h:d * NS + h + 1])
                    m.then_inc(S["drop"], 1)
                    if d == 1 and not before(t, 1):
                        squares(t - 1, 1 - s, before(t, 2))
                    act.wait_ge(S["drop"], 2 * t + d + 1)
                    a.activation(drop[:, d], drop[:, d], ACT.Exp, scale=-1.0).then_inc(S["e"], 1)
                if not before(t, 2):
                    store(t - 2, before(t, 3))

            order(act, body)
            squares(NT - 1, 1)
            store(NT - 2)
            store(NT - 1)
            act.wait_ge(stored, 16 * NT)

        @block.vector
        def _(dve):
            v = nc.vector
            dve.wait_ge(S["const"], 48)

            def hp(ap):
                return ap.rearrange("p (h q) -> p h q", q=PS)

            def gate(t, s):
                dve.wait_ge(S["diag"], t + 1)
                dve.wait_ge(S["y"], 4 * t + 4)
                v.tensor_tensor(hp(y[:, s]), hp(y[:, s]), g_ps[:, :, :], ALU.add).then_inc(S["gated"], 1)
                dve.wait_ge(S["gated"], 2 * t + 1)
                dve.wait_ge(z_loaded[s], loaded_value(t, s))
                v.tensor_tensor(y[:, s], y[:, s], z[:, s], ALU.mult).then_inc(S["gated"], 1)

            def norm(t, s, first=False):
                dve.wait_ge(S["pow"], 2 * t + 2)
                if not first:
                    dve.wait_ge(S["tn"], t - 1)
                v.scalar_tensor_tensor(yn[:, s], y[:, s], rstd[:, :], wn[:, :], ALU.mult, ALU.mult
                                       ).then_inc(S["yn"], 1)

            def body(t, s):
                if not before(t, 2):
                    dve.wait_ge(S["drop"], 2 * t - 2)
                at = acs[:, t:t + 1] if isinstance(t, int) else acs[:, ds(t, 1)]
                v.tensor_copy(acs_t[:, s:s + 1], at).then_inc(S["acs"], 1)
                dve.wait_ge(S["xcopy"], t + 1)
                if not before(t, 1):
                    dve.wait_ge(S["st"], t)
                v.tensor_tensor(x_dec[:, :, :], x_tok[:, :, :], bc(row(dec, t, 0, NS), [P, NS, PS]),
                                ALU.mult).then_inc(S["xd"], 1)
                dve.wait_ge(S["off"], t + 1)
                if not before(t, 2):
                    dve.wait_ge(S["sq"], t - 1)
                    dve.wait_ge(S["yn"], t - 1)
                v.tensor_tensor(hp(y[:, s]), y_ps[:, :, :], bc(row(e_acs, t, 0, NS), [P, NS, PS]),
                                ALU.mult).then_inc(S["y"], 1)
                if not before(t, 1):
                    dve.wait_ge(S["y"], 4 * t)
                v.tensor_tensor(hp(y2[:, :]), x_tok[:, :, :], bc(dsk[:, :].unsqueeze(2), [P, NS, PS]),
                                ALU.mult).then_inc(S["y"], 1)
                dve.wait_ge(S["cb"], t + 1)
                if not before(t, 1):
                    dve.wait_ge(S["m"], 2 * t)
                for d in range(2):
                    v.tensor_tensor(cb[:, d, :, 0], m_ps[:, 2:4], bc(tri[:, d:d + 1, :], [P, NG, P]),
                                    ALU.mult).then_inc(S["cbm"], 1)
                dve.wait_ge(S["y"], 4 * t + 2)
                yb = y_back[:, t] if isinstance(t, int) else y_back[:, ds(t, 1)].rearrange("p o n -> p (o n)")
                v.tensor_tensor(y2[:, :], y2[:, :], yb, ALU.add).then_inc(S["y"], 1)
                if not before(t, 1):
                    dve.wait_ge(S["h"], 2 * t)
                v.tensor_tensor(scaled[:, :, :], state[:, :, :], bc(row(e_tot, t, 0, NS), [P, NS, PS]),
                                ALU.mult).then_inc(S["h"], 1)
                dve.wait_ge(S["y"], 4 * t + 3)
                v.tensor_tensor(y[:, s], y[:, s], y2[:, :], ALU.add).then_inc(S["y"], 1)
                if not before(t, 1):
                    gate(t - 1, 1 - s)
                dve.wait_ge(S["st"], t + 1)
                dve.wait_ge(S["h"], 2 * t + 1)
                v.tensor_tensor(state[:, :, :], scaled[:, :, :], s_ps[:, :, :], ALU.add).then_inc(S["h"], 1)
                dve.wait_ge(S["cbm"], 2 * t + 2)
                for d in range(2):
                    dve.wait_ge(S["e"], 2 * t + d + 1)
                    if not before(t, 1):
                        dve.wait_ge(S["diag"], t)
                    v.tensor_tensor(m_t[:, d].rearrange("p (g h) l -> p g h l", g=NG),
                                    drop[:, d].rearrange("p (g h) l -> p g h l", g=NG),
                                    bc(cb[:, d], [P, NG, NS // NG, P]), ALU.mult).then_inc(S["m"], 1)
                if not before(t, 1):
                    norm(t - 1, 1 - s, before(t, 3))

            def reset(k):
                if k:
                    dve.wait_ge(S["h"], 2 * TP)
                v.memset(state[:, :, :], 0.0).then_inc(S["zero"], 1)
                dve.wait_ge(S["zero"], k + 1)

            order(dve, body, reset)
            gate(NT - 1, 1)
            norm(NT - 1, 1)


def ssm(nc, proj, ident, small, R, mix_t, xbc_c):
    with ExitStack() as ctx:
        R = {**R, "y_back": Bufs(nc, ctx).sb("ss_yback", [P, NT, NS * PS])}
        ssm_backward(nc, xbc_c, ident, R)
        ssm_forward(nc, proj, xbc_c, ident, small, R, mix_t)


def out_projection(nc, w_out, mix_t, x_dram, x1):
    with ExitStack() as ctx:
        b = Bufs(nc, ctx)
        raw = b.sb("wo_raw", [P, 2, D])
        w_hi = b.sb("wo_hi", [P, 2, KC, D], F32R)
        w_lo = b.sb("wo_lo", [P, 2, KC, D], F32R)
        mix = b.sb("wo_mix", [P, 2, KC, P])
        m_hi = b.sb("wo_mhi", [P, 2, KC, P], F32R)
        m_lo = b.sb("wo_mlo", [P, 2, KC, P], F32R)
        bank = b.ps("wo_bank", [P, 2, 2, PW])
        x_loaded = b.sems("wo_xl", 2)
        raw_loaded = b.sems("wo_rawl", 2)
        mix_loaded = b.sems("wo_mixl", 2)
        w_hi_done, w_split = b.sem("wo_whid"), b.sem("wo_wsplit")
        m_hi_done, m_split = b.sem("wo_mhid"), b.sem("wo_msplit")
        multiplied, added = b.sem("wo_mm"), b.sem("wo_added")
        block = b.block()

        @block.sync
        def _(sp):
            for s in range(2):
                sp.dma_start(raw[:, s], w_out[s * P:(s + 1) * P, :]).then_inc(raw_loaded[s], 16)

            def chunks(first, end):
                with sp.Fori(first, end) as j:
                    for s in range(2):
                        sp.wait_ge(w_split, 2 * j + s - 1)
                        sp.dma_start(raw[:, s], w_out[ds((2 * j + s) * P, P), :]).then_inc(raw_loaded[s], 16)

            x_v = x_dram.rearrange("(t p) d -> p t d", p=P)
            chunks(1, KC // 2)
            sp.dma_start(x1[:, 0:2, :], x_v[:, 0:2, :]).then_inc(x_loaded[0], 16)
            sp.dma_start(x1[:, 2:NT, :], x_v[:, 2:NT, :]).then_inc(x_loaded[1], 16)
            chunks(KC // 2, KC)

        @block.gpsimd
        def _(pool):
            def load(h, t, s, first=False):
                if not first:
                    pool.wait_ge(m_split, h * NT + t - 1)
                src = mix_t[t] if isinstance(t, int) else mix_t[ds(t, 1)]
                pool.dma_start(mix[:, s], src[..., h * KC * P:(h + 1) * KC * P]).then_inc(mix_loaded[s], 16)

            for s in range(2):
                load(0, s, s, True)
            with pool.Fori(1, NT // 2) as j:
                for s in range(2):
                    load(0, 2 * j + s, s)
            with pool.Fori(0, NT // 2) as j:
                for s in range(2):
                    load(1, 2 * j + s, s)

        @block.scalar
        def _(act):
            def high(j, s, first=False):
                act.wait_ge(mix_loaded[s], 16 * j + 16)
                if not first:
                    act.wait_ge(multiplied, 2 * j + s - 1)
                nc.scalar.activation(m_hi[:, s], mix[:, s], ACT.Copy).then_inc(m_hi_done, 1)

            for s in range(2):
                high(0, s, True)
            with act.Fori(1, NT) as j:
                for s in range(2):
                    high(j, s)

        @block.vector
        def _(dve):
            def weights(half, k, s):
                n = half * KC + k
                kk = slice(k, k + 1) if isinstance(k, int) else ds(k, 1)
                dve.wait_ge(raw_loaded[s], 8 * (n - s) + 16)
                nc.vector.tensor_copy(w_hi[:, half, kk], raw[:, s]).then_inc(w_hi_done, 1)
                dve.wait_ge(w_hi_done, n + 1)
                nc.vector.tensor_tensor(w_lo[:, half, kk], raw[:, s], w_hi[:, half, kk].bitcast(FP32),
                                        ALU.subtract).then_inc(w_split, 1)

            def low(n, s):
                dve.wait_ge(m_hi_done, n + 1)
                nc.vector.tensor_tensor(m_lo[:, s], mix[:, s], m_hi[:, s].bitcast(FP32),
                                        ALU.subtract).then_inc(m_split, 1)

            def add(n, t, s):
                dve.wait_ge(multiplied, n + 1)
                x = x1[:, t, :] if isinstance(t, int) else x1[:, ds(t, 1), :]
                nc.vector.tensor_tensor(x, x, bank[:, s], ALU.add).then_inc(added, 1)

            for s in range(2):
                low(s, s)
            for k in range(KC):
                weights(0, k, k % 2)
            dve.wait_ge(x_loaded[0], 16)
            for s in range(2):
                add(s, s, s)
                low(s + 2, s)
                weights(1, s, s)
            dve.wait_ge(x_loaded[1], 16)
            with dve.Fori(1, KC // 2) as j:
                for s in range(2):
                    add(2 * j + s, 2 * j + s, s)
                    low(2 * j + s + 2, s)
                    weights(1, 2 * j + s, s)
            for s in range(2):
                add(KC + s, KC + s, s)
                low(KC + s + 2, s)
            dve.wait_ge(added, NT)
            with dve.Fori(0, NT // 2 - 1) as j:
                for s in range(2):
                    add(NT + 2 * j + s, 2 * j + s, s)
                    low(NT + 2 * j + s + 2, s)
            for s in range(2):
                add(2 * NT - 2 + s, NT - 2 + s, s)

        @block.tensor
        def _(pe):
            def tile(half, n, s):
                pe.wait_ge(m_split, n + 1)
                pe.wait_ge(added, n - 1)
                for c in range(2):
                    cols = slice(c * PW, (c + 1) * PW)
                    for k in range(KC):
                        for i, (l, r) in enumerate(((m_hi, w_hi), (m_hi, w_lo), (m_lo, w_hi))):
                            m = nc.tensor.matmul(bank[:, s, c], l[:, s, k], r[:, half, k, cols],
                                                 start=(k == 0 and i == 0), stop=(k == KC - 1 and i == 2))
                m.then_inc(multiplied, 1)

            pe.wait_ge(m_split, 2)
            for k in range(KC):
                pe.wait_ge(w_split, k + 1)
                for s in range(2):
                    for c in range(2):
                        cols = slice(c * PW, (c + 1) * PW)
                        for i, (l, r) in enumerate(((m_hi, w_hi), (m_hi, w_lo), (m_lo, w_hi))):
                            m = nc.tensor.matmul(bank[:, s, c], l[:, s, k], r[:, 0, k, cols],
                                                 start=(k == 0 and i == 0), stop=(k == KC - 1 and i == 2))
                    if k == KC - 1:
                        m.then_inc(multiplied, 1)
            with pe.Fori(1, NT // 2) as j:
                for s in range(2):
                    tile(0, 2 * j + s, s)
            pe.wait_ge(w_split, 2 * KC)
            with pe.Fori(NT // 2, NT) as j:
                for s in range(2):
                    tile(1, 2 * j + s, s)


def ffn(nc, hi, lo, w_up, w_down, conv_w, conv_b, y, out):
    PAD = TOK + 3
    GAP = SEQ + 1
    with ExitStack() as ctx:
        b = Bufs(nc, ctx)
        raw_u = b.sb("ff_rawu", [P, KC, 2, P])
        raw_d = b.sb("ff_rawd", [P, D])
        u_hi = b.sb("ff_uhi", [P, 2, KC, 2, P], F32R)
        u_lo = b.sb("ff_ulo", [P, 2, KC, 2, P], F32R)
        d_hi = b.sb("ff_dhi", [P, 2, D], F32R)
        d_lo = b.sb("ff_dlo", [P, 2, D], F32R)
        taps = b.sb("ff_taps", [P, 2 * NF, 3])
        bias = b.sb("ff_bias", [P, 2 * NF])
        padded = b.sb("ff_padded", [P, PAD])
        gate = b.sb("ff_gate", [P, PAD])
        up = b.sb("ff_up", [P, PAD])
        a_hi = b.sb("ff_ahi", [P, PAD], F32R)
        a_lo = b.sb("ff_alo", [P, PAD], F32R)
        proj = b.ps("ff_proj", [P, 2, 3 * PW])
        sums = b.ps("ff_sums", [P, 2, PW])
        const_loaded = b.sem("ff_const")
        u_loaded, d_loaded = b.sem("ff_ul"), b.sem("ff_dl")
        u_hi_done, u_split = b.sem("ff_uhid"), b.sem("ff_usplit")
        d_hi_done, d_split = b.sem("ff_dhid"), b.sem("ff_dsplit")
        zeroed = b.sem("ff_zeroed")
        projected, copied = b.sem("ff_proj_s"), b.sem("ff_copied")
        conved = b.sem("ff_conv")
        gated, acted = b.sem("ff_gated"), b.sem("ff_acted")
        a_hi_done, a_lo_done = b.sem("ff_ahid"), b.sem("ff_alod")
        summed, added = b.sem("ff_summed"), b.sem("ff_added")
        stored = b.sem("ff_stored")
        block = b.block()
        G = 2 * NT
        RING = 5

        def ring(g):
            k = g % RING
            return proj[:, 0, k * PW:(k + 1) * PW] if k < 3 else sums[:, k - 3]

        w_up_v = w_up.rearrange("(k p) (g n) -> p k g n", p=P, g=2)

        @block.sync
        def _(sp):
            def load(i, first=False):
                if not first:
                    sp.wait_ge(u_split, i)
                for g in range(2):
                    sp.dma_start(raw_u[:, :, g], w_up_v[:, :, g, ds(i * P, P)]).then_inc(u_loaded, 16)
                if not first:
                    sp.wait_ge(d_split, i)
                sp.dma_start(raw_d[:, :], w_down[ds(i * P, P), :]).then_inc(d_loaded, 16)

            load(0, True)
            sp.dma_start(taps[:, :, :], conv_w).then_inc(const_loaded, 16)
            sp.wait_ge(const_loaded, 16)
            sp.dma_start(bias[:, :], conv_b).then_inc(const_loaded, 16)
            with sp.Fori(1, NF) as i:
                load(i)
            with sp.Fori(0, NT) as t:
                sp.wait_ge(added, (NF - 1) * G + 2 * t + 2)
                sp.dma_start(out[ds(t * P, P), :], y[:, ds(t, 1), :]).then_inc(stored, 16)
            sp.wait_ge(stored, 16 * NT)

        @block.scalar
        def _(act):
            def up_weights(i, s, first=False):
                act.wait_ge(u_loaded, 32 * i + 32)
                if not first:
                    act.wait_ge(projected, 2 * i - 2)
                nc.scalar.activation(u_hi[:, s], raw_u[:, :, :, :], ACT.Copy).then_inc(u_hi_done, 1)

            def down_weights(i, s, first=False):
                act.wait_ge(d_loaded, 16 * i + 16)
                if not first:
                    act.wait_ge(summed, G * (i - 1))
                nc.scalar.activation(d_hi[:, s], raw_d[:, :], ACT.Copy).then_inc(d_hi_done, 1)

            def copy(i, g, first=False):
                act.wait_ge(projected, 2 * i + g + 1)
                if not first:
                    act.wait_ge(conved, 3 * (2 * i + g))
                nc.scalar.activation(padded[:, 1:1 + SEQ], proj[:, g, 0:SEQ], ACT.Copy)
                nc.scalar.activation(padded[:, GAP + 1:GAP + 1 + DEC], proj[:, g, SEQ:TOK],
                                     ACT.Copy).then_inc(copied, 1)

            def hidden(i, first=False):
                act.wait_ge(conved, 6 * i + 6)
                nc.scalar.activation(gate[:, 1:GAP + 1 + DEC], gate[:, 1:GAP + 1 + DEC],
                                     ACT.Silu).then_inc(gated, 1)
                act.wait_ge(acted, i + 1)
                if not first:
                    act.wait_ge(summed, G * i)
                nc.scalar.activation(a_hi[:, 1:GAP + 1 + DEC], gate[:, 1:GAP + 1 + DEC],
                                     ACT.Copy).then_inc(a_hi_done, 1)

            act.wait_ge(zeroed, 1)
            up_weights(0, 0, True)
            down_weights(0, 0, True)
            up_weights(1, 1, True)
            copy(0, 0, True)
            copy(0, 1)
            hidden(0, True)
            down_weights(1, 1, True)
            with act.Fori(0, (NF - 2) // 2) as j:
                for s in range(2):
                    i = 2 * j + s + 1
                    up_weights(i + 1, s)
                    copy(i, 0)
                    copy(i, 1)
                    hidden(i)
                    down_weights(i + 1, s)
            copy(NF - 1, 0)
            copy(NF - 1, 1)
            hidden(NF - 1)

        @block.vector
        def _(dve):
            nc.vector.memset(padded[:, :], 0.0).then_inc(zeroed, 1)

            def up_weights(i, s):
                dve.wait_ge(u_hi_done, i + 1)
                nc.vector.tensor_tensor(u_lo[:, s], raw_u[:, :, :, :], u_hi[:, s].bitcast(FP32),
                                        ALU.subtract).then_inc(u_split, 1)

            def down_weights(i, s):
                dve.wait_ge(d_hi_done, i + 1)
                nc.vector.tensor_tensor(d_lo[:, s], raw_d[:, :], d_hi[:, s].bitcast(FP32),
                                        ALU.subtract).then_inc(d_split, 1)

            def conv(i, g, dst):
                n = 3 * (2 * i + g)
                c = i + g * NF
                mid = slice(1, GAP + 1 + DEC)
                dve.wait_ge(copied, 2 * i + g + 1)
                if g == 0 and not (isinstance(i, int) and i == 0):
                    dve.wait_ge(a_lo_done, i)
                nc.vector.tensor_scalar(dst[:, mid], padded[:, mid], taps[:, ds(c, 1), 1],
                                        bias[:, ds(c, 1)], ALU.mult, ALU.add).then_inc(conved, 1)
                dve.wait_ge(conved, n + 1)
                nc.vector.scalar_tensor_tensor(dst[:, mid], padded[:, 0:GAP + DEC], taps[:, ds(c, 1), 0],
                                               dst[:, mid], ALU.mult, ALU.add).then_inc(conved, 1)
                dve.wait_ge(conved, n + 2)
                nc.vector.scalar_tensor_tensor(dst[:, mid], padded[:, 2:GAP + 2 + DEC],
                                               taps[:, ds(c, 1), 2], dst[:, mid],
                                               ALU.mult, ALU.add).then_inc(conved, 1)

            def hidden(i):
                mid = slice(1, GAP + 1 + DEC)
                dve.wait_ge(gated, i + 1)
                nc.vector.tensor_tensor(gate[:, mid], gate[:, mid], up[:, mid], ALU.mult).then_inc(acted, 1)
                dve.wait_ge(a_hi_done, i + 1)
                nc.vector.tensor_tensor(a_lo[:, mid], gate[:, mid], a_hi[:, mid].bitcast(FP32),
                                        ALU.subtract).then_inc(a_lo_done, 1)

            def adds(i):
                for t in range(NT):
                    for c in range(2):
                        g = 2 * t + c
                        dve.wait_ge(summed, G * i + g + 1)
                        v = y[:, t, c * PW:(c + 1) * PW]
                        nc.vector.tensor_tensor(v, v, ring(g), ALU.add).then_inc(added, 1)

            dve.wait_ge(const_loaded, 32)
            up_weights(0, 0)
            down_weights(0, 0)
            up_weights(1, 1)
            conv(0, 0, gate)
            conv(0, 1, up)
            hidden(0)
            down_weights(1, 1)
            with dve.Fori(0, (NF - 2) // 2) as j:
                for s in range(2):
                    i = 2 * j + s + 1
                    up_weights(i + 1, s)
                    conv(i, 0, gate)
                    adds(i - 1)
                    conv(i, 1, up)
                    hidden(i)
                    down_weights(i + 1, s)
            conv(NF - 1, 0, gate)
            adds(NF - 2)
            conv(NF - 1, 1, up)
            hidden(NF - 1)
            adds(NF - 1)

        @block.tensor
        def _(pe):
            X, U = (hi, lo), (u_hi, u_lo)

            def project(i, s, first=False):
                for g in range(2):
                    pe.wait_ge(u_split, i + 1)
                    if not first:
                        pe.wait_ge(copied, 2 * i - 1 + g)
                    if g == 0 and not (isinstance(i, int) and i < 2):
                        pe.wait_ge(added, G * (i - 1) - 2)
                    for k in range(KC):
                        for r, (w, x) in enumerate(((0, 0), (0, 1), (1, 0))):
                            for t0, n in ((0, PW), (PW, PW), (2 * PW, TOK - 2 * PW)):
                                m = nc.tensor.matmul(proj[:, g, t0:t0 + n], U[w][:, s, k, g],
                                                     X[x][:, k, t0:t0 + n],
                                                     start=(k == 0 and r == 0), stop=(k == KC - 1 and r == 2))
                    m.then_inc(projected, 1)

            def down(i, s, first=False, last=False):
                pe.wait_ge(a_lo_done, i + 1)
                pe.wait_ge(d_split, i + 1)
                if not last:
                    pe.wait_ge(copied, 2 * i + 3)
                for t in range(NT):
                    c0 = 1 + t * P + (t >= TP)
                    for c in range(2):
                        g = 2 * t + c
                        if not (first and g < RING):
                            pe.wait_ge(added, G * i + g + 1 - RING)
                        cols = slice(c * PW, (c + 1) * PW)
                        for r, (a, w) in enumerate(((a_hi, d_hi), (a_hi, d_lo), (a_lo, d_hi))):
                            m = nc.tensor.matmul(ring(g), a[:, c0:c0 + P], w[:, s, cols],
                                                 start=(r == 0), stop=(r == 2))
                        m.then_inc(summed, 1)

            project(0, 0, True)
            project(1, 1)
            down(0, 0, True)
            with pe.Fori(1, NF // 2) as j:
                for s in range(2):
                    i = 2 * j + s
                    project(i, s)
                    down(i - 1, 1 - s)
            down(NF - 1, 1, last=True)


def encoder(nc, tokens, w_in, w_mem, w_out, w_up, w_down, norm_w, small, ident, masks, rope, tri,
            conv_w, conv_b, ssm_conv, out, scratch):
    proj, mem_proj, xbc_c, mix_t = scratch
    with ExitStack() as ctx:
        b = Bufs(nc, ctx)
        R = {k: b.sb(f"ss_{k}", [P, NT, 2 * NS]) for k in ("dt", "acs", "e_acs", "e_tot", "dec", "a")}
        R["tri"] = b.sb("ss_tri", [P, 2, P])
        with nc.sbuf_tensor("act_hi", [P, KC, TOK + NMT * P], F32R) as hi, \
                nc.sbuf_tensor("act_lo", [P, KC, TOK + NMT * P], F32R) as lo:
            norm_transpose(nc, "n1", NT + NMT, [(norm_w[0:1, :], 0, NT), (norm_w[1:2, :], NT, NMT)],
                           ident, hi, lo, src_dram=tokens)
            projections(nc, hi, lo, w_in, w_mem, proj, mem_proj, xbc_c, small, ident, tri, ssm_conv,
                        R)
        ssm(nc, proj, ident, small, R, mix_t, xbc_c)
    attention(nc, proj, ident, masks, rope, small, mix_t)
    memory(nc, proj, mem_proj, ident, small, mix_t)
    with nc.sbuf_tensor("x1", [P, NT, D], FP32) as x1:
        out_projection(nc, w_out, mix_t, tokens[0:TOK, :], x1)
        with nc.sbuf_tensor("h_hi", [P, KC, TOK], F32R) as hi, \
                nc.sbuf_tensor("h_lo", [P, KC, TOK], F32R) as lo:
            norm_transpose(nc, "n2", NT, [(norm_w[2:3, :], 0, NT)], ident, hi, lo, src_sb=x1)
            ffn(nc, hi, lo, w_up, w_down, conv_w, conv_b, x1, out)


def window_masks():
    q, k = np.arange(P)[:, None], np.arange(3 * P)[None] - P
    band = np.abs(k - q) <= 128
    return np.array([np.where(band & (t * P + k >= 0) & (t * P + k < n * P), 0, NEG)
                     for n in (TP, TS) for t in range(n)], np.float32)


def rope_tables():
    inv = np.float32(10000.0) ** (-np.arange(0, DH, 2, dtype=np.float32) / np.float32(DH))
    ang = np.arange(SEQ, dtype=np.float32)[:, None] * inv.astype(np.float32)[None]
    c, s = np.cos(ang), np.sin(ang)
    tab = np.stack([np.concatenate([c, c], 1), np.concatenate([-s, s], 1)])
    return tab.reshape(2, TP, P, DH).transpose(2, 0, 1, 3).astype(np.float32)


def triangles():
    i = np.arange(P)
    return np.stack([i[:, None] <= i[None], i[:, None] >= i[None]], 1).astype(np.float32)


def kernel(**inputs):
    import concourse.bacc as bacc
    from concourse.bass_utils import run_bass_kernel_spmd

    a = {k: np.asarray(v) for k, v in inputs.items()}
    w_in = a["w_in"][0]
    dt0, mq0 = 3072, 3088
    arrays = {
        "tokens": np.concatenate([a["x_prompt"][0], a["x_sample"][0], a["mem_prompt"][0], a["mem_sample"][0]]),
        "w_in": np.concatenate([w_in[:, :2048], w_in[:, mq0:], w_in[:, 2048:dt0], w_in[:, dt0:mq0]], 1),
        "w_mem": a["w_mem_kv"][0], "w_out": a["w_out"][0],
        "w_up": a["w_ffn_up"][0], "w_down": a["w_ffn_down"][0],
        "norm_w": np.concatenate([a["norm1_w"], a["mem_norm_w"], a["norm2_w"]]),
        "ident": np.eye(P, dtype=np.float32), "masks": window_masks(), "rope": rope_tables(),
        "tri": triangles(),
        "conv_w": a["ffn_conv_w"][0].reshape(3, 2 * NF, P).transpose(2, 1, 0),
        "conv_b": a["ffn_conv_b"][0].reshape(2 * NF, P).T,
        "ssm_conv": np.concatenate([a["ssm_conv_w"][0], a["ssm_conv_b"]]).reshape(6, XBC // P, P).transpose(2, 1, 0),
    }
    small = {k: a[k].reshape(1, -1) for k in (
        "q_norm_w", "k_norm_w", "attn_sink", "mq_norm_w", "mk_norm_w", "ssm_norm_w", "ssm_D",
        "ssm_dt_bias", "ssm_A_log")}
    nc = bacc.Bacc("TRN2", target_bir_lowering=False, num_devices=1)
    maps = {k: np.ascontiguousarray(v) for k, v in {**arrays, **small}.items()}
    ap = {k: nc.dram_tensor(k, v.shape, FP32, kind="ExternalInput").ap() for k, v in maps.items()}
    out = nc.dram_tensor("out", (TOK, D), FP32, kind="ExternalOutput").ap()
    scratch = [nc.dram_tensor(f"scratch_{n}", s, FP32, kind="Internal").ap() for n, s in (
        ("proj", (TOK, NPAN * PW)), ("mem", (NMT * P, 2 * PW)), ("xbc_tiles", (NT, P, XBC)), ("mix", (NT, P, 16 * P)))]
    encoder(nc, *(ap[k] for k in ("tokens", "w_in", "w_mem", "w_out", "w_up", "w_down", "norm_w")),
            {k: ap[k] for k in small}, *(ap[k] for k in ("ident", "masks", "rope", "tri", "conv_w", "conv_b",
                                                          "ssm_conv")), out, scratch)
    r = run_bass_kernel_spmd(nc, [maps], core_ids=[0])
    y = r.results[0]["out"]
    return y[None, :SEQ], y[None, SEQ:]
```

```python
import concourse.bass as bass
from concourse import mybir
from contextlib import ExitStack
import numpy as np

FP32 = mybir.dt.float32
F32R = mybir.dt.float32r
ALU = mybir.AluOpType
ACT = mybir.ActivationFunctionType
AX = mybir.AxisListType

P = 128
D = 1024
KC = D // P
SEQ, DEC = 1024, 256
TP, TS = SEQ // P, DEC // P
NT = TP + TS
TOK = NT * P
NMT = 4
HQ, HKV, DH = 16, 4, 64
HM, DM = 4, 128
NS, PS, NG, ST = 8, 64, 2, 128
XBC = NS * PS + 2 * NG * ST
F = 2816
NF = F // P
EPS = 1e-6
PW = 512
CUT = 448
TOKEN_CUTS = ((0, CUT), (CUT, CUT), (2 * CUT, TOK - 2 * CUT))
NPAN = 5
NEG = -1e30
KB = NT + 3


def ds(a, n):
    return bass.ds(a, n)


def bc(ap, shape):
    return ap.broadcast_to(shape)


class Bufs:

    previous = None

    def __init__(self, nc, ctx):
        self.nc, self.ctx, self.own, self.held = nc, ctx, [], ExitStack()

    def sb(self, name, shape, dt=FP32):
        return self.ctx.enter_context(self.nc.sbuf_tensor(name, shape, dt))

    def ps(self, name, shape):
        return self.ctx.enter_context(self.nc.psum_tensor(name, shape, FP32))

    def sem(self, name):
        self.own.append(self.held.enter_context(self.nc.semaphore(name)))
        return self.own[-1]

    def sems(self, name, n):
        return [self.sem(f"{name}{i}") for i in range(n)]

    def block(self):
        self.ctx.callback(self.finish)
        return self.ctx.enter_context(self.nc.Block())

    def finish(self):
        if Bufs.previous is not None:
            Bufs.previous.held.close()
        Bufs.previous = self

    @staticmethod
    def clear_previous(pool):
        if Bufs.previous is not None:
            for s in Bufs.previous.own:
                pool.sem_clear(s)

    @staticmethod
    def clear_last(nc):
        with nc.Block() as block:
            @block.gpsimd
            def _(pool):
                Bufs.clear_previous(pool)
        Bufs.previous.held.close()
        Bufs.previous = None


def norm_transpose(nc, tag, tiles, weight_rows, ident_dram, hi, lo, src):
    with ExitStack() as ctx:
        b = Bufs(nc, ctx)
        ident = b.sb(f"{tag}_ident", [P, P])
        wb = b.sb(f"{tag}_w", [P, len(weight_rows), D])
        x = b.sb(f"{tag}_x", [P, tiles, D])
        xn = b.sb(f"{tag}_xn", [P, 2, D])
        junk = b.sb(f"{tag}_junk", [P, 2, D])
        ms = b.sb(f"{tag}_ms", [P, tiles])
        mse = b.sb(f"{tag}_mse", [P, tiles])
        rstd = b.sb(f"{tag}_rstd", [P, tiles])
        half = b.sb(f"{tag}_half", [P, 1])
        eps = b.sb(f"{tag}_eps", [P, 1])
        xt = b.ps(f"{tag}_xt", [P, 2, KC, P])
        const_loaded = b.sem(f"{tag}_const")
        x_loaded = b.sems(f"{tag}_xl", 2)
        half_set = b.sem(f"{tag}_halfset")
        squared, mse_done, rstd_done = b.sem(f"{tag}_sq"), b.sem(f"{tag}_mse"), b.sem(f"{tag}_rs")
        normed, transposed, hi_done, lo_done = (b.sem(f"{tag}_{n}") for n in ("xn", "tr", "hi", "lo"))
        block = b.block()

        @block.sync
        def _(sp):
            for s in range(2):
                sp.dma_start(x[:, s], src[s * P:(s + 1) * P, :]).then_inc(x_loaded[s], 16)
            with sp.Fori(1, tiles // 2) as j:
                for s in range(2):
                    sp.wait_ge(x_loaded[s], 16 * j)
                    sp.dma_start(x[:, ds(2 * j + s, 1)], src[ds((2 * j + s) * P, P), :]
                                 ).then_inc(x_loaded[s], 16)

        def source(t):
            return x[:, t, :] if isinstance(t, int) else x[:, ds(t, 1), :]

        @block.scalar
        def _(act):
            def square(j, s):
                t = 2 * j + s
                act.wait_ge(x_loaded[s], 16 * j + 16)
                if not (isinstance(j, int) and j == 0):
                    act.wait_ge(squared, t - 1)
                nc.scalar.activation(junk[:, s], source(t), ACT.Square, scale=D ** -0.5,
                                     accum_out=ms[:, ds(t, 1)]).then_inc(squared, 1)

            def high(j, s):
                t = 2 * j + s
                act.wait_ge(transposed, t + 1)
                nc.scalar.activation(hi[:, :, ds(t * P, P)], xt[:, s], ACT.Copy).then_inc(hi_done, 1)

            act.dma_start(ident[:, :], ident_dram).then_inc(const_loaded, 16)
            for i, (w, _, _) in enumerate(weight_rows):
                act.dma_start(wb[:, i], w.broadcast_to([P, D])).then_inc(const_loaded, 16)
            for s in range(2):
                square(0, s)
            with act.Fori(0, tiles // 2 - 1) as j:
                for s in range(2):
                    square(j + 1, s)
                    high(j, s)
            for s in range(2):
                high(tiles // 2 - 1, s)

        @block.gpsimd
        def _(pool):
            b.clear_previous(pool)
            nc.gpsimd.memset(half[:, :], -0.5).then_inc(half_set, 1)
            nc.gpsimd.memset(eps[:, :], EPS).then_inc(half_set, 1)
            pool.wait_ge(half_set, 2)
            with pool.Fori(0, tiles) as t:
                pool.wait_ge(squared, t + 1)
                nc.gpsimd.tensor_tensor(mse[:, ds(t, 1)], ms[:, ds(t, 1)], eps[:, :],
                                        ALU.add).then_inc(mse_done, 1)
                pool.wait_ge(mse_done, t + 1)
                nc.gpsimd.tensor_tensor(rstd[:, ds(t, 1)], mse[:, ds(t, 1)], half[:, :],
                                        ALU.pow).then_inc(rstd_done, 1)

        @block.vector
        def _(dve):
            def norm(t, s, weight, first=False):
                dve.wait_ge(rstd_done, t + 1)
                if not first:
                    dve.wait_ge(transposed, t - 1)
                nc.vector.scalar_tensor_tensor(xn[:, s], source(t), rstd[:, ds(t, 1)], wb[:, weight],
                                               ALU.mult, ALU.mult).then_inc(normed, 1)

            def low(t, s):
                dve.wait_ge(hi_done, t + 1)
                nc.vector.tensor_tensor(lo[:, :, ds(t * P, P)], xt[:, s],
                                        hi[:, :, ds(t * P, P)].bitcast(FP32),
                                        ALU.subtract).then_inc(lo_done, 1)

            dve.wait_ge(const_loaded, 16 * (1 + len(weight_rows)))
            for s in range(2):
                norm(s, s, 0, True)
            for i, (_, first, count) in enumerate(weight_rows):
                with dve.Fori(max(first // 2, 1), (first + count) // 2) as j:
                    for s in range(2):
                        norm(2 * j + s, s, i)
                        low(2 * j + s - 2, s)
            for s in range(2):
                low(tiles - 2 + s, s)

        @block.tensor
        def _(pe):
            pe.wait_ge(const_loaded, 16 * (1 + len(weight_rows)))

            def one(t, s, first):
                pe.wait_ge(normed, t + 1)
                if not first:
                    pe.wait_ge(lo_done, t - 1)
                for k in range(KC):
                    m = nc.tensor.transpose(xt[:, s, k], xn[:, s, k * P:(k + 1) * P], ident[:, :])
                m.then_inc(transposed, 1)

            for s in range(2):
                one(s, s, True)
            with pe.Fori(1, tiles // 2) as j:
                for s in range(2):
                    one(2 * j + s, s, False)


def projections(nc, hi, lo, w_in, w_mem, proj, mem_proj, xbc_c, small, ident_dram, tri_dram,
                conv_dram, R):
    PIECES, RAW, BANKS = 4, 2, 7
    TAPS, NCH = 5, XBC // P
    PADW, SPAN = TOK + 6, TOK + 2
    CUTS = ((0, 512, 2), (512, 512, 514), (SEQ, DEC, SEQ + 4))
    NC = len(CUTS)
    H2 = 2 * NS
    rows = KC // PIECES
    Z_PANEL = 3
    with ExitStack() as ctx:
        b = Bufs(nc, ctx)
        raw = b.sb("pj_raw", [P, RAW, rows, PW])
        w_hi = b.sb("pj_whi", [P, 2, KC, PW], F32R)
        w_lo = b.sb("pj_wlo", [P, 2, KC, PW], F32R)
        dt_raw = b.sb("pj_dtraw", [P, KC, H2])
        dt_hi = b.sb("pj_dthi", [P, KC, H2], F32R)
        dt_lo = b.sb("pj_dtlo", [P, KC, H2], F32R)
        stage = b.sb("pj_stage", [P, 2, PW])
        ident = b.sb("pj_ident", [H2, H2])
        taps = b.sb("cv_taps", [P, NCH, TAPS + 1])
        x = b.sb("cv_x", [P, PADW])
        y = b.sb("cv_y", [P, SPAN])
        ones = b.sb("sz_ones", [P, P])
        bias = b.sb("sz_bias", [P, 1, H2])
        a_log = b.sb("sz_alog", [P, 1, H2])
        a_neg = b.sb("sz_aneg", [P, 1, H2])
        v1, v2, v3, v4 = (b.sb(f"sz_v{i}", [P, NT, H2]) for i in range(1, 5))
        bank = b.ps("pj_bank", [P, BANKS, PW])
        sizes = b.ps("sz_ps", [P, 3, NT, H2])
        raw_loaded = b.sems("pj_rawl", RAW)
        dt_loaded = b.sem("pj_dtl")
        w_hi_done, w_split = b.sem("pj_whid"), b.sem("pj_split")
        multiplied = b.sem("pj_mm")
        copied = b.sem("pj_copied")
        stored = b.sems("pj_stored", 2)
        taps_loaded, zeroed, tapped = b.sem("cv_const"), b.sem("cv_zero"), b.sem("cv_tap")
        silued, row_stored = b.sem("cv_silu"), b.sem("cv_stored")
        sz_loaded, dt_projected, step, summed = b.sem("sz_l"), b.sem("sz_dt"), b.sem("sz_step"), b.sem("sz_sum")
        exps, ones_set, want_exp = b.sem("sz_exp"), b.sem("sz_ones_s"), b.sem("sz_want")
        block = b.block()
        dt, acs, e_acs, e_tot, dec = R["dt"], R["acs"], R["e_acs"], R["e_tot"], R["dec"]
        a_sb, tri = R["a"], R["tri"]

        w_mem_v = w_mem.rearrange("(k p) n -> p k n", p=P)
        w_in_v = w_in.rearrange("(k p) n -> p k n", p=P)
        XBC_COL, DT_COL = NPAN * PW, NPAN * PW + XBC
        DT0 = NCH * NC
        TOK0 = DT0 + NC
        MEM0 = TOK0 + NPAN * NT
        GROUPS = MEM0 + 2 * NMT

        @block.sync
        def _(sp):
            def load(n, src, c):
                for q in range(PIECES):
                    if not (isinstance(n, int) and n == 0 and q < RAW):
                        sp.wait_ge(w_split, PIECES * n + q - RAW + 1)
                    sp.dma_start(raw[:, q % RAW], src[:, q * rows:(q + 1) * rows, c]).then_inc(raw_loaded[q % RAW], 16)

            load(0, w_in_v, slice(XBC_COL, XBC_COL + PW))
            sp.dma_start(taps[:, :, :], conv_dram).then_inc(taps_loaded, 16)
            sp.dma_start(dt_raw[:, :, :], w_in_v[:, :, DT_COL:DT_COL + H2]).then_inc(dt_loaded, 16)
            for dst, src in ((tri[:, :, :], tri_dram), (ident[:, :], ident_dram[0:H2, 0:H2]),
                             (bias[:, 0], small["ssm_dt_bias"].broadcast_to([P, H2])),
                             (a_log[:, 0], small["ssm_A_log"].broadcast_to([P, H2]))):
                sp.dma_start(dst, src).then_inc(sz_loaded, 16)
            load(1, w_in_v, slice(XBC_COL + PW, XBC_COL + 2 * PW))
            with sp.Fori(0, NPAN) as m:
                load(m + 2, w_in_v, ds(m * PW, PW))
            for n in range(2):
                load(NPAN + 2 + n, w_mem_v, slice(n * PW, (n + 1) * PW))

        @block.vector
        def _(dve):
            v = nc.vector

            def split(n, s, free):
                if free is not None:
                    dve.wait_ge(multiplied, free)
                for q in range(PIECES):
                    dve.wait_ge(raw_loaded[q % RAW], 16 * (PIECES // RAW * n + q // RAW + 1))
                    k = slice(q * rows, (q + 1) * rows)
                    v.tensor_copy(w_hi[:, s, k], raw[:, q % RAW]).then_inc(w_hi_done, 1)
                    dve.wait_ge(w_hi_done, PIECES * n + q + 1)
                    v.tensor_tensor(w_lo[:, s, k], raw[:, q % RAW], w_hi[:, s, k].bitcast(FP32),
                                    ALU.subtract).then_inc(w_split, 1)

            def conv(c):
                dve.wait_ge(copied, NC * (c + 1))
                if c > 0:
                    dve.wait_ge(row_stored, 32 * c)
                v.tensor_scalar(y[:, :], x[:, 0:SPAN], taps[:, c:c + 1, 0], taps[:, c:c + 1, TAPS], ALU.mult,
                                ALU.add).then_inc(tapped, 1)
                for k in range(1, TAPS):
                    dve.wait_ge(tapped, TAPS * c + k)
                    v.scalar_tensor_tensor(y[:, :], x[:, k:k + SPAN], taps[:, c:c + 1, k], y[:, :],
                                           ALU.mult, ALU.add).then_inc(tapped, 1)

            n = [0]

            def then(ins):
                n[0] += 1
                ins.then_inc(step, 1)
                dve.wait_ge(step, n[0])

            v.memset(x[:, :], 0.0).then_inc(zeroed, 1)
            v.memset(ones[:, :], 1.0).then_inc(ones_set, 1)
            split(0, 0, None)
            dve.wait_ge(dt_loaded, 16)
            then(v.tensor_copy(dt_hi[:, :, :], dt_raw[:, :, :]))
            then(v.tensor_tensor(dt_lo[:, :, :], dt_raw[:, :, :], dt_hi[:, :, :].bitcast(FP32), ALU.subtract))
            split(1, 1, None)
            dve.wait_ge(taps_loaded, 16)
            for c in range(4):
                conv(c)
            split(2, 0, DT0 // 2)
            for c in range(4, NCH):
                conv(c)
            split(3, 1, DT0)
            split(4, 0, TOK0 + NT)
            dve.wait_ge(sz_loaded, 64)
            dve.wait_ge(dt_projected, 1)
            then(v.tensor_tensor(v1[:, :, :], sizes[:, 0], bc(bias[:, :, :], [P, NT, H2]), ALU.add))
            then(v.tensor_scalar(v2[:, :, :], v1[:, :, :], -1.0, None, ALU.mult))
            then(v.tensor_tensor(v3[:, :, :], v1[:, :, :], v2[:, :, :], ALU.min))
            v.tensor_scalar(v1[:, :, :], v1[:, :, :], 0.0, None, ALU.max).then_inc(want_exp, 1)
            dve.wait_ge(exps, 2)
            then(v.tensor_scalar(v2[:, :, :], v4[:, :, :], 2.0, None, ALU.add))
            then(v.reciprocal(v3[:, :, :], v2[:, :, :]))
            then(v.tensor_tensor(v4[:, :, :], v4[:, :, :], v3[:, :, :], ALU.mult))
            then(v.tensor_tensor(v2[:, :, :], v4[:, :, :], v4[:, :, :], ALU.mult))
            then(v.tensor_scalar(v3[:, :, :], v2[:, :, :], 1.0 / 17, 1.0 / 15, ALU.mult, ALU.add))
            for k in (13, 11, 9, 7, 5, 3, 1):
                then(v.tensor_tensor(v3[:, :, :], v3[:, :, :], v2[:, :, :], ALU.mult))
                then(v.tensor_scalar(v3[:, :, :], v3[:, :, :], 1.0 / k, None, ALU.add))
            then(v.tensor_tensor(v3[:, :, :], v3[:, :, :], v4[:, :, :], ALU.mult))
            dve.wait_ge(want_exp, 1)
            then(v.scalar_tensor_tensor(dt[:, :, :], v3[:, :, :], 2.0, v1[:, :, :], ALU.mult, ALU.add))
            then(v.tensor_scalar(a_neg[:, :, :], a_neg[:, :, :], -1.0, None, ALU.mult))
            v.tensor_tensor(a_sb[:, :, :], dt[:, :, :], bc(a_neg[:, :, :], [P, NT, H2]), ALU.mult
                            ).then_inc(want_exp, 1)
            split(5, 1, TOK0 + 2 * NT)
            dve.wait_ge(summed, 1)
            then(v.tensor_copy(acs[:, :, :], sizes[:, 1]))
            v.tensor_tensor(v1[:, :, :], sizes[:, 2], acs[:, :, :], ALU.subtract).then_inc(want_exp, 1)
            dve.wait_ge(exps, 5)
            v.tensor_tensor(dec[:, :, :], v2[:, :, :], dt[:, :, :], ALU.mult).then_inc(step, 1)
            for n in range(6, NPAN + 4):
                split(n, n % 2, TOK0 + NT * (n - 3))

        @block.tensor
        def _(pe):
            W = (w_hi, w_lo)
            X = (hi, lo)

            def group(g, out, left, right, panel=None):
                if g >= BANKS:
                    pe.wait_ge(copied, g - BANKS + 1)
                for k in range(KC):
                    if panel is not None and k % rows == 0:
                        pe.wait_ge(w_split, PIECES * panel + k // rows + 1)
                    for i, (a, c) in enumerate(((0, 0), (0, 1), (1, 0))):
                        m = nc.tensor.matmul(out, left(a, k), right(c, k), start=(k == 0 and i == 0),
                                             stop=(k == KC - 1 and i == 2))
                m.then_inc(multiplied, 1)

            def channel_panel(n, s):
                for m4 in range(4):
                    for i, (t0, w, _) in enumerate(CUTS):
                        g = NC * (4 * n + m4) + i
                        group(g, bank[:, g % BANKS, 0:w], lambda a, k: W[a][:, s, k, m4 * P:(m4 + 1) * P],
                              lambda c, k: X[c][:, k, t0:t0 + w], n if m4 == i == 0 else None)

            def token_panel(n, s, tiles, t0, g0):
                for t in range(tiles):
                    g = g0 + t
                    group(g, bank[:, g % BANKS], lambda a, k: X[a][:, k, (t0 + t) * P:(t0 + t + 1) * P],
                          lambda c, k: W[c][:, s, k], n if t == 0 else None)

            channel_panel(0, 0)
            channel_panel(1, 1)
            for i, (t0, w, _) in enumerate(CUTS):
                g = DT0 + i
                group(g, bank[0:H2, g % BANKS, 0:w], lambda a, k: (dt_hi, dt_lo)[a][:, k],
                      lambda c, k: X[c][:, k, t0:t0 + w])
            token_panel(2, 0, NT, 0, TOK0)
            pe.wait_ge(copied, TOK0)
            pe.wait_ge(sz_loaded, 64)
            for t in range(NT):
                at = CUTS[0][2] + t * P if t < TP else CUTS[2][2] + (t - TP) * P
                m = nc.tensor.transpose(sizes[:, 0, t], x[0:H2, at:at + P], ident[:, :])
            m.then_inc(dt_projected, 1)
            token_panel(3, 1, NT, 0, TOK0 + NT)
            pe.wait_ge(ones_set, 1)
            pe.wait_ge(want_exp, 2)
            for d in range(2):
                nc.tensor.matmul(sizes[:, 1, :, d * NS:(d + 1) * NS], tri[:, d],
                                 a_sb[:, :, d * NS:(d + 1) * NS], start=True, stop=True)
            nc.tensor.matmul(sizes[:, 2], ones[:, :], a_sb[:, :, :], start=True, stop=True
                             ).then_inc(summed, 1)
            for n in range(4, 2 + NPAN):
                token_panel(n, n % 2, NT, 0, TOK0 + NT * (n - 2))
            for n in range(2):
                token_panel(NPAN + 2 + n, (NPAN + n) % 2, NMT, NT, MEM0 + NMT * n)

        @block.gpsimd
        def _(pool):
            b.clear_previous(pool)

        @block.scalar
        def _(act):
            a = nc.scalar

            def to_row(c, part):
                for i, (_, w, at) in enumerate(CUTS):
                    g = NC * c + i
                    act.wait_ge(multiplied, g + 1)
                    if i == 0 and c > 0:
                        act.wait_ge(tapped, TAPS * c)
                    a.activation(x[0:part, at:at + w], bank[0:part, g % BANKS, 0:w], ACT.Copy).then_inc(copied, 1)

            def channels(c):
                to_row(c, P)
                act.wait_ge(tapped, TAPS * (c + 1))
                a.activation(y[:, :], y[:, :], ACT.Silu).then_inc(silued, 1)
                act.wait_ge(silued, c + 1)
                dst = xbc_c.rearrange("t p n -> p t n")[:, :, c * P:(c + 1) * P]
                act.dma_start(dst[:, 0:TP], y[:, 0:SEQ].rearrange("p (t n) -> p t n", n=P)
                              ).then_inc(row_stored, 16)
                act.dma_start(dst[:, TP:NT], y[:, SEQ + 2:SPAN].rearrange("p (t n) -> p t n", n=P)
                              ).then_inc(row_stored, 16)

            def out(g, dst, func=ACT.Copy):
                s = (g - TOK0) % 2
                act.wait_ge(multiplied, g + 1)
                if g >= TOK0 + 2:
                    act.wait_ge(stored[s], 16 * ((g - TOK0) // 2))
                a.activation(stage[:, s], bank[:, g % BANKS], func).then_inc(copied, 1)
                act.wait_ge(copied, g + 1)
                act.dma_start(dst, stage[:, s]).then_inc(stored[s], 16)

            act.wait_ge(zeroed, 1)
            for c in range(NCH):
                channels(c)
            to_row(NCH, H2)
            for n in range(NPAN):
                for t in range(NT):
                    out(TOK0 + NT * n + t, proj[t * P:(t + 1) * P, n * PW:(n + 1) * PW],
                        ACT.Silu if n == Z_PANEL else ACT.Copy)
                    if n == 1 and t == 4:
                        act.wait_ge(sz_loaded, 64)
                        a.activation(a_neg[:, :, :], a_log[:, :, :], ACT.Exp).then_inc(exps, 1)
                        act.wait_ge(want_exp, 1)
                        a.activation(v4[:, :, :], v3[:, :, :], ACT.Exp).then_inc(exps, 1)
                    if n == 2 and t == 4:
                        act.wait_ge(want_exp, 3)
                        a.activation(e_acs[:, :, :], acs[:, :, :], ACT.Exp).then_inc(exps, 1)
                        a.activation(e_tot[:, :, :], sizes[:, 2], ACT.Exp).then_inc(exps, 1)
                        a.activation(v2[:, :, :], v1[:, :, :], ACT.Exp).then_inc(exps, 1)
            for n in range(2):
                for t in range(NMT):
                    out(MEM0 + NMT * n + t, mem_proj[t * P:(t + 1) * P, n * PW:(n + 1) * PW])
            for s in range(2):
                act.wait_ge(stored[s], 16 * (GROUPS - TOK0) // 2)
            act.wait_ge(row_stored, 32 * NCH)


def attention(nc, proj, ident_dram, mask_dram, rope_dram, small, mix_t):
    q_w, k_w, sink = small["q_norm_w"], small["k_norm_w"], small["attn_sink"]
    WIN = 3 * P
    KEY_PARTS = ((0, 2), (2, 4), (6, NT - 6))
    with ExitStack() as ctx:
        b = Bufs(nc, ctx)
        ident = b.sb("at_ident", [P, P])
        mask = b.sb("at_mask", [P, 2, WIN])
        rope = b.sb("at_rope", [P, 2, TP, DH])
        wrow = b.sb("at_wrow", [P, 4, DH])
        table = b.sb("at_table", [P, 4, TP, DH])
        k_raw = b.sb("at_kraw", [P, NT, HKV, DH])
        k_a = b.sb("at_ka", [P, NT, HKV, DH])
        k_two = b.sb("at_ktwo", [P, NT, HKV, 2, DH])
        k_b = k_two[:, :, :, 0]
        k_ss = b.sb("at_kss", [P, NT * HKV])
        k_mse = b.sb("at_kmse", [P, NT * HKV])
        k_rstd = b.sb("at_krstd", [P, NT * HKV])
        v_sb = b.sb("at_v", [P, KB, HKV * DH])
        kt_hi = b.sb("at_kthi", [P, HKV, KB * P], F32R)
        kt_lo = b.sb("at_ktlo", [P, HKV, KB * P], F32R)
        half = b.sb("at_half", [P, NT * HKV])
        eps = b.sb("at_eps", [P, NT * HKV])
        sinkb = b.sb("at_sink", [P, HQ])
        nsink = b.sb("at_nsink", [P, HQ])
        q_raw = b.sb("at_qraw", [P, 2, HQ, DH])
        q_sq = b.sb("at_qsq", [P, HQ, DH])
        q_c = b.sb("at_qc", [P, 2, HQ, DH])
        q_b = b.sb("at_qb", [P, HQ, DH])
        q_n = b.sb("at_qn", [P, HQ, DH])
        q_two = b.sb("at_qtwo", [P, HQ, 2, DH])
        q_ss = b.sb("at_qss", [P, 2, HQ])
        q_mse = b.sb("at_qmse", [P, 2, HQ])
        q_rstd = b.sb("at_qrstd", [P, 2, HQ])
        qt = b.sb("at_qt", [P, 2, HQ, P], F32R)
        sm = b.sb("at_sm", [P, 4, WIN])
        pr = b.sb("at_pr", [P, 4, WIN])
        pt = b.sb("at_pt", [P, 2, 3, P])
        nm = b.sb("at_nm", [P, 2, HQ])
        rowsum = b.sb("at_rowsum", [P, 2, HQ])
        t1 = b.sb("at_t1", [P, HQ])
        es = b.sb("at_es", [P, HQ])
        den = b.sb("at_den", [P, HQ])
        rec = b.sb("at_rec", [P, HQ])
        o_sb = b.sb("at_o", [P, HQ, DH])
        ot = b.sb("at_ot", [P, KC * P])
        s_ps = b.ps("at_sps", [P, 2, PW])
        t_ps = b.ps("at_tps", [P, 2, 4, P])
        o_ps = b.ps("at_ops", [P, HQ, DH])
        x_ps = b.ps("at_xps", [P, 2, 4, P])
        names = ("const", "kvl", "vl", "ksq", "kred", "krs", "kprep", "ktwice", "kt", "khi", "klo", "half", "table",
                 "qss", "qred", "qpow", "qmse", "qrot", "qn", "qhi", "qlo", "s", "m", "e", "t", "pt", "v",
                 "t1", "es", "den", "oscaled", "x", "xcopy", "ready")
        S = {n: b.sem(f"at_s_{n}") for n in names}
        q_loaded, m_loaded = b.sems("at_ql", 2), b.sems("at_ml", 2)
        stored = b.sem("at_stored")
        block = b.block()

        def blk(t):
            return (t if t < TP else t + 1) if isinstance(t, int) else t

        def key_bank(t):
            return t_ps[:, t % 4] if t % 4 < 2 else s_ps[:, t % 4 - 2].rearrange("p (h n) -> p h n", n=P)

        def tile_loop(engine, body):
            for s in range(2):
                body(s, s)
            with engine.Fori(1, TP // 2) as j:
                for s in range(2):
                    body(2 * j + s, s)
            for s in range(2):
                body(TP + s, s)

        @block.sync
        def _(sp):
            kv = proj.rearrange("(t p) n -> p t n", p=P)
            loads = [(ident[:, :], ident_dram), (rope[:, :, :, :], rope_dram),
                     (wrow[:, 0], q_w.broadcast_to([P, DH])), (wrow[:, 2], k_w.broadcast_to([P, DH])),
                     (wrow[:, 1, 0:32], q_w[:, 32:64].broadcast_to([P, 32])),
                     (wrow[:, 1, 32:64], q_w[:, 0:32].broadcast_to([P, 32])),
                     (wrow[:, 3, 0:32], k_w[:, 32:64].broadcast_to([P, 32])),
                     (wrow[:, 3, 32:64], k_w[:, 0:32].broadcast_to([P, 32])),
                     (sinkb[:, :], sink.broadcast_to([P, HQ]))]
            sp.dma_start(k_raw[:, :, :, :], kv[:, :, 1024:1280]).then_inc(S["kvl"], 16)
            for dst, src in loads:
                sp.dma_start(dst, src).then_inc(S["const"], 16)
            sp.dma_start(v_sb[:, 1:1 + TP, :], kv[:, 0:TP, 1280:1536]).then_inc(S["vl"], 16)
            sp.dma_start(v_sb[:, TP + 2:TP + 2 + TS, :], kv[:, TP:NT, 1280:1536]).then_inc(S["vl"], 16)

            def load(t, s):
                if not (isinstance(t, int) and t < 2):
                    sp.wait_ge(S["qrot"], t - 1)
                    sp.wait_ge(S["qss"], t - 1)
                rows = slice(t * P, (t + 1) * P) if isinstance(t, int) else ds(t * P, P)
                sp.dma_start(q_raw[:, s], proj[rows, 0:1024]).then_inc(q_loaded[s], 16)
                if not (isinstance(t, int) and t < 2):
                    sp.wait_ge(S["m"], HQ * (t - 1))
                sp.dma_start(mask[:, s], mask_dram[t] if isinstance(t, int) else mask_dram[ds(t, 1)]
                             ).then_inc(m_loaded[s], 16)

            tile_loop(sp, load)

        @block.gpsimd
        def _(pool):
            b.clear_previous(pool)
            g = nc.gpsimd
            g.memset(half[:, :], -0.5).then_inc(S["half"], 1)
            g.memset(eps[:, :], EPS).then_inc(S["half"], 1)
            pool.wait_ge(S["half"], 2)
            pool.wait_ge(S["kred"], 1)
            g.tensor_tensor(k_mse[:, :], k_ss[:, :], eps[:, :], ALU.add).then_inc(S["krs"], 1)
            pool.wait_ge(S["krs"], 1)
            g.tensor_tensor(k_rstd[:, :], k_mse[:, :], half[:, :], ALU.pow).then_inc(S["krs"], 1)
            pool.wait_ge(S["table"], 4)

            def queries(t, s):
                j = t if isinstance(t, int) else (t - s)
                pos = (t % TP) if isinstance(t, int) else t
                first = isinstance(t, int) and t < 2
                pool.wait_ge(q_loaded[s], (16 * (t // 2 + 1)) if isinstance(t, int) else 8 * (t - s) + 16)
                if not (isinstance(t, int) and t == 0):
                    pool.wait_ge(S["qlo"], t)
                tab = [table[:, i, pos:pos + 1, :] if isinstance(pos, int) else table[:, i, ds(pos, 1), :]
                       for i in range(2)]
                g.tensor_tensor(q_c[:, s], q_raw[:, s], bc(tab[0], [P, HQ, DH]), ALU.mult).then_inc(S["qpow"], 1)
                for lo_, hi_ in ((0, 32), (32, 64)):
                    g.tensor_tensor(q_b[:, :, lo_:lo_ + 32], q_raw[:, s, :, 32 - lo_:64 - lo_],
                                    bc(tab[1][:, :, lo_:hi_], [P, HQ, 32]), ALU.mult).then_inc(S["qpow"], 1)
                pool.wait_ge(S["qpow"], 3 * t + 3)
                g.tensor_tensor(q_c[:, s], q_c[:, s], q_b[:, :, :], ALU.add).then_inc(S["qrot"], 1)
                pool.wait_ge(S["qred"], t + 1)
                g.tensor_tensor(q_mse[:, s], q_ss[:, s], eps[:, 0:HQ], ALU.add).then_inc(S["qmse"], 1)
                pool.wait_ge(S["qmse"], 2 * t + 1)
                g.tensor_tensor(q_rstd[:, s], q_mse[:, s], half[:, 0:HQ], ALU.pow).then_inc(S["qmse"], 1)
                pool.wait_ge(S["qmse"], 2 * t + 2)
                g.tensor_tensor(q_n[:, :, :], q_c[:, s], bc(q_rstd[:, s].unsqueeze(2), [P, HQ, DH]),
                                ALU.mult).then_inc(S["qn"], 1)
                pool.wait_ge(S["qhi"], t + 1)
                g.tensor_tensor(q_two[:, :, 1].bitcast(F32R), q_n[:, :, :], q_two[:, :, 0],
                                ALU.subtract).then_inc(S["qlo"], 1)

            tile_loop(pool, queries)

        def q_loaded_value(t, s):
            return 16 * (t // 2 + 1) if isinstance(t, int) else 8 * (t - s) + 16

        def units_before(t):
            return 4 if isinstance(t, int) and t == 0 else 6 * t + 2

        def o_unit_no(t, c):
            return 6 * t + 3 + c

        def q_unit_no(t, c):
            return 5 + c if isinstance(t, int) and t == 0 else 6 * t + 5 + c

        def square(act, t, s):
            act.wait_ge(q_loaded[s], q_loaded_value(t, s))
            if not (isinstance(t, int) and t == 0):
                act.wait_ge(S["qred"], t)
            nc.scalar.activation(q_sq[:, :, :], q_raw[:, s], ACT.Square, scale=DH ** -0.5).then_inc(S["qss"], 1)

        def high(act, t):
            act.wait_ge(S["qn"], t + 1)
            if not (isinstance(t, int) and t == 0):
                act.wait_ge(S["x"], units_before(t - 1))
            nc.scalar.activation(q_two[:, :, 0].bitcast(F32R), q_n[:, :, :], ACT.Copy).then_inc(S["qhi"], 1)

        def q_evac(act, s, c, n):
            act.wait_ge(S["x"], n)
            nc.scalar.activation(qt[:, s, 4 * c:4 * c + 4], x_ps[:, c % 2], ACT.Copy).then_inc(S["xcopy"], 1)

        @block.scalar
        def _(act):
            act.wait_ge(S["kvl"], 16)
            nc.scalar.activation(k_a[:, :, :, :], k_raw[:, :, :, :], ACT.Square, scale=DH ** -0.5).then_inc(S["ksq"], 1)
            square(act, 0, 0)
            for i, (t0, m) in enumerate(KEY_PARTS):
                act.wait_ge(S["kprep"], 8 + i)
                nc.scalar.activation(k_two[:, t0:t0 + m, :, 1], k_two[:, t0:t0 + m, :, 0], ACT.Copy
                                     ).then_inc(S["ktwice"], 1)
            for t in range(NT):
                if t == 6:
                    high(act, 0)
                act.wait_ge(S["kt"], t + 1)
                nc.scalar.activation(kt_hi[:, :, (blk(t) + 1) * P:(blk(t) + 2) * P], key_bank(t), ACT.Copy
                                     ).then_inc(S["khi"], 1)
            for c in range(4):
                q_evac(act, 0, c, c + 1)

            def tile(t, s):
                last = isinstance(t, int) and t == NT - 1
                zero = isinstance(t, int) and t == 0
                for h in range(HQ):
                    n = HQ * t + h
                    act.wait_ge(S["m"], n + 1)
                    if not (zero and h < 4):
                        act.wait_ge(S["t"], n - 3)
                    nc.scalar.activation(pr[:, h % 4], sm[:, h % 4], ACT.Exp, bias=nm[:, s, h:h + 1],
                                         scale=-1.0, accum_out=rowsum[:, s, h:h + 1]).then_inc(S["e"], 1)
                    if h == 0 and not last:
                        square(act, t + 1, 1 - s)
                    if h == 1 and not zero:
                        sink_exp(t - 1, 1)
                    if h == 10:
                        sink_exp(t, 0)
                    if h in (7, 8) and not zero:
                        output_evac(t - 1, h - 7, o_unit_no(t, h - 7))
                    if h == 4 and not last:
                        high(act, t + 1)
                    if 11 <= h < 15 and not last:
                        q_evac(act, 1 - s, h - 11, q_unit_no(t, h - 11))

            def sink_exp(t, c):
                act.wait_ge(S["t1"], 2 * t + c + 1)
                if not (isinstance(t, int) and t == 0):
                    act.wait_ge(S["den"], 4 * (t - 1) + 2 * c + 1)
                nc.scalar.activation(es[:, 8 * c:8 * c + 8], t1[:, 8 * c:8 * c + 8], ACT.Exp).then_inc(S["es"], 1)

            def output_evac(t, c, u):
                act.wait_ge(S["x"], u)
                if c == 0 and not (isinstance(t, int) and t == 0):
                    act.wait_ge(stored, 16 * t)
                nc.scalar.activation(ot[:, 4 * c * P:4 * (c + 1) * P], x_ps[:, c], ACT.Copy).then_inc(S["xcopy"], 1)
                if c == 1:
                    act.wait_ge(S["xcopy"], u)
                    dst = mix_t[t] if isinstance(t, int) else mix_t[ds(t, 1)]
                    act.dma_start(dst[..., 0:KC * P], ot[:, :]).then_inc(stored, 16)

            tile_loop(act, tile)
            sink_exp(NT - 1, 1)
            for c in range(2):
                output_evac(NT - 1, c, units_before(NT - 1) + 3 + c)
            act.wait_ge(stored, 16 * NT)

        @block.vector
        def _(dve):
            v = nc.vector
            for z in (0, TP + 1, KB - 1):
                v.memset(v_sb[:, z], 0.0)
                v.memset(kt_hi[:, :, z * P:(z + 1) * P].bitcast(FP32), 0.0)
                v.memset(kt_lo[:, :, z * P:(z + 1) * P].bitcast(FP32), 0.0)

            def reduce(t, s):
                dve.wait_ge(S["qss"], t + 1)
                if not (isinstance(t, int) and t < 2):
                    dve.wait_ge(S["qmse"], 2 * (t - 1))
                v.reduce_sum(q_ss[:, s], q_sq[:, :, :], AX.X).then_inc(S["qred"], 1)

            dve.wait_ge(S["ksq"], 1)
            v.reduce_sum(k_ss[:, :], k_a[:, :, :, :], AX.X).then_inc(S["kred"], 1)
            dve.wait_ge(S["const"], 16 * 9)
            for i in range(4):
                v.tensor_tensor(table[:, i], rope[:, i % 2], bc(wrow[:, i:i + 1, :], [P, TP, DH]),
                                ALU.mult).then_inc(S["table"], 1)
            v.tensor_scalar(nsink[:, :], sinkb[:, :], -1.0, None, ALU.mult).then_inc(S["table"], 1)
            dve.wait_ge(S["table"], 5)
            dve.wait_ge(S["kred"], 1)
            for t0, m in ((0, TP), (TP, TS)):
                c = table[:, 2, 0:m].unsqueeze(2)
                sn = table[:, 3, 0:m].unsqueeze(2)
                v.tensor_tensor(k_a[:, t0:t0 + m], k_raw[:, t0:t0 + m], bc(c, [P, m, HKV, DH]),
                                ALU.mult).then_inc(S["kprep"], 1)
                for a in (0, 32):
                    v.tensor_tensor(k_b[:, t0:t0 + m, :, a:a + 32], k_raw[:, t0:t0 + m, :, 32 - a:64 - a],
                                    bc(sn[:, :, :, a:a + 32], [P, m, HKV, 32]),
                                    ALU.mult).then_inc(S["kprep"], 1)
            reduce(0, 0)
            dve.wait_ge(S["kprep"], 6)
            v.tensor_tensor(k_a[:, :, :, :], k_a[:, :, :, :], k_b[:, :, :, :], ALU.add).then_inc(S["kprep"], 1)
            dve.wait_ge(S["kprep"], 7)
            dve.wait_ge(S["krs"], 2)
            kr = k_rstd[:, :].rearrange("p (t h) -> p t h", h=HKV).unsqueeze(3)
            for t0, m in KEY_PARTS:
                v.tensor_tensor(k_two[:, t0:t0 + m, :, 0], k_a[:, t0:t0 + m], bc(kr[:, t0:t0 + m], [P, m, HKV, DH]),
                                ALU.mult).then_inc(S["kprep"], 1)

            for t in range(NT):
                cols = slice((blk(t) + 1) * P, (blk(t) + 2) * P)
                dve.wait_ge(S["khi"], t + 1)
                v.tensor_tensor(kt_lo[:, :, cols], key_bank(t), kt_hi[:, :, cols].bitcast(FP32),
                                ALU.subtract).then_inc(S["klo"], 1)

            def finish(t, s, c):
                n = 4 * t + 2 * c
                heads = slice(8 * c, 8 * c + 8)
                dve.wait_ge(S["es"], 2 * t + c + 1)
                v.tensor_tensor(den[:, heads], rowsum[:, s, heads], es[:, heads], ALU.add).then_inc(S["den"], 1)
                dve.wait_ge(S["den"], n + 1)
                v.reciprocal(rec[:, heads], den[:, heads]).then_inc(S["den"], 1)
                dve.wait_ge(S["den"], n + 2)
                dve.wait_ge(S["v"], HQ * t + 8 * c + 8)
                if not (isinstance(t, int) and t == 0):
                    dve.wait_ge(S["x"], o_unit_no(t, c))
                v.tensor_tensor(o_sb[:, heads], o_ps[:, heads], bc(rec[:, heads].unsqueeze(2), [P, 8, DH]),
                                ALU.mult).then_inc(S["oscaled"], 1)

            def sink_term(t, s, c):
                heads = slice(8 * c, 8 * c + 8)
                dve.wait_ge(S["m"], HQ * t + 8 * c + 8)
                if not (isinstance(t, int) and t == 0):
                    dve.wait_ge(S["es"], 2 * t + c - 1)
                v.tensor_tensor(t1[:, heads], nm[:, s, heads], sinkb[:, heads], ALU.add).then_inc(S["t1"], 1)

            def copy_pt(n, h):
                dve.wait_ge(S["t"], n + 1)
                if not (isinstance(n, int) and n < 2):
                    dve.wait_ge(S["v"], n - 1)
                v.tensor_copy(pt[:, h % 2], t_ps[:, h % 2, 0:3]).then_inc(S["pt"], 1)

            def tile(t, s):
                last = isinstance(t, int) and t == NT - 1
                zero = isinstance(t, int) and t == 0
                dve.wait_ge(m_loaded[s], q_loaded_value(t, s))
                for h in range(HQ):
                    n = HQ * t + h
                    if h == 0 and not zero:
                        sink_term(t - 1, 1 - s, 1)
                    if h == 9:
                        sink_term(t, s, 0)
                    if not (zero and h < 3):
                        copy_pt(n - 3, h + 1)
                    dve.wait_ge(S["s"], n + 1)
                    if not (zero and h < 4):
                        dve.wait_ge(S["e"], n - 3)
                    dve.sem_inc(S["ready"], 1)
                    v.tensor_tensor_reduce(out=sm[:, h % 4], in0=s_ps[:, h % 2, 0:WIN], in1=mask[:, s],
                                           scale=-(DH ** -0.5), scalar=nsink[:, h:h + 1], op0=ALU.add,
                                           op1=ALU.min, accum_out=nm[:, s, h:h + 1]).then_inc(S["m"], 1)
                    if h == 4 and not zero:
                        finish(t - 1, 1 - s, 1)
                    if h == 12:
                        finish(t, s, 0)
                    if h == 1 and not last:
                        reduce(t + 1, 1 - s)

            tile_loop(dve, tile)
            for n in range(HQ * NT - 3, HQ * NT):
                copy_pt(n, n % 2)
            sink_term(NT - 1, 1, 1)
            finish(NT - 1, 1, 1)

        @block.tensor
        def _(pe):
            T = nc.tensor
            pe.wait_ge(S["const"], 16 * 9)
            for t in range(NT):
                pe.wait_ge(S["ktwice"], 1 + sum(t >= t0 for t0, _ in KEY_PARTS[1:]))
                if t >= 4:
                    pe.wait_ge(S["klo"], t - 3)
                for j in range(HKV):
                    m = T.transpose(key_bank(t)[:, j], k_two[:, t, j], ident[:, :])
                m.then_inc(S["kt"], 1)
            pe.wait_ge(S["klo"], NT)

            def q_unit(c, n):
                if not (isinstance(n, int) and n <= 2):
                    pe.wait_ge(S["xcopy"], n - 2)
                for h in range(4):
                    m = T.transpose(x_ps[:, c % 2, h], q_two[:, 4 * c + h], ident[:, :])
                m.then_inc(S["x"], 1)

            pe.wait_ge(S["vl"], 32)
            pe.wait_ge(S["qlo"], 1)
            for c in range(4):
                q_unit(c, c + 1)

            def o_unit(t, c, u):
                pe.wait_ge(S["oscaled"], 2 * t + c + 1)
                pe.wait_ge(S["xcopy"], u - 2)
                for k in range(4):
                    i = 4 * c + k
                    m = T.transpose(x_ps[:, c, k], o_sb[:, 2 * i:2 * i + 2], ident[:, :])
                m.then_inc(S["x"], 1)

            def weights_t(n, h):
                pe.wait_ge(S["e"], n + 1)
                if not (isinstance(n, int) and n < 2):
                    pe.wait_ge(S["pt"], n - 1)
                for k in range(3):
                    m = T.transpose(t_ps[:, h % 2, k], pr[:, h % 4, k * P:(k + 1) * P], ident[:, :])
                m.then_inc(S["t"], 1)

            def values(n, t, h):
                pe.wait_ge(S["pt"], n + 1)
                if h % 8 == 0 and not (isinstance(t, int) and t == 0):
                    pe.wait_ge(S["oscaled"], 2 * t - 1 + h // 8)
                g = (h // 4) * DH
                for k in range(3):
                    kb = blk(t) + k
                    rhs = v_sb[:, kb, g:g + DH] if isinstance(kb, int) else v_sb[:, ds(kb, 1), g:g + DH]
                    m = T.matmul(o_ps[:, h], pt[:, h % 2, k], rhs, start=(k == 0), stop=(k == 2))
                m.then_inc(S["v"], 1)

            def tile(t, s):
                last = isinstance(t, int) and t == NT - 1
                zero = isinstance(t, int) and t == 0
                pe.wait_ge(S["xcopy"], units_before(t))
                for h in range(HQ):
                    n = HQ * t + h
                    if not (zero and h < 2):
                        pe.wait_ge(S["m"], n - 1)
                    k0 = blk(t) * P
                    cols = slice(k0, k0 + WIN) if isinstance(k0, int) else ds(k0, WIN)
                    T.matmul(s_ps[:, h % 2, 0:WIN], qt[:, s, h], kt_hi[:, h // 4, cols], start=True, stop=False)
                    T.matmul(s_ps[:, h % 2, 0:WIN], qt[:, s, h], kt_lo[:, h // 4, cols], start=False,
                             stop=True).then_inc(S["s"], 1)
                    if not (zero and h < 4):
                        if h >= 4:
                            values(n - 4, t, h - 4)
                        else:
                            values(n - 4, t - 1, h + HQ - 4)
                    if not (zero and h < 2):
                        weights_t(n - 2, (h + 2) % 4)
                    if h in (6, 7) and not zero:
                        o_unit(t - 1, h - 6, o_unit_no(t, h - 6))
                    if 10 <= h < 14 and not last:
                        if h == 10:
                            pe.wait_ge(S["qlo"], t + 2)
                        q_unit(h - 10, q_unit_no(t, h - 10))

            tile_loop(pe, tile)
            weights_t(HQ * NT - 2, 2)
            values(HQ * NT - 4, NT - 1, HQ - 4)
            weights_t(HQ * NT - 1, 3)
            for h in range(HQ - 3, HQ):
                values(HQ * (NT - 1) + h, NT - 1, h)
            for c in range(2):
                o_unit(NT - 1, c, units_before(NT - 1) + 3 + c)


def memory(nc, proj, mem_proj, ident_dram, small, mix_t):
    MT = NMT // 2
    NK = MT * P
    SC = DM ** -0.5
    with ExitStack() as ctx:
        b = Bufs(nc, ctx)
        ident = b.sb("me_ident", [P, P])
        wq = b.sb("me_wq", [P, 1, DM])
        wk = b.sb("me_wk", [P, 1, DM])
        half = b.sb("me_half", [P, NMT * HM])
        eps = b.sb("me_eps", [P, NMT * HM])
        k_raw = b.sb("me_kraw", [P, NMT, HM, DM])
        k_sq = b.sb("me_ksq", [P, NMT, HM, DM])
        k_n = b.sb("me_kn", [P, NMT, HM, DM])
        k_ss = b.sb("me_kss", [P, NMT * HM])
        k_mse = b.sb("me_kmse", [P, NMT * HM])
        k_rstd = b.sb("me_krstd", [P, NMT * HM])
        v_sb = b.sb("me_v", [P, NMT, HM, DM])
        kt = b.sb("me_kt", [P, HM, NMT * P])
        q_raw = b.sb("me_qraw", [P, 2, HM, DM])
        q_sq = b.sb("me_qsq", [P, HM, DM])
        q_w = b.sb("me_qw", [P, HM, DM])
        q_n = b.sb("me_qn", [P, HM, DM])
        q_ss = b.sb("me_qss", [P, HM])
        q_mse = b.sb("me_qmse", [P, HM])
        q_rstd = b.sb("me_qrstd", [P, HM])
        qt = b.sb("me_qt", [P, HM, P])
        mx = b.sb("me_mx", [P, HM])
        nm = b.sb("me_nm", [P, HM])
        rowsum = b.sb("me_rowsum", [P, 2, HM])
        rec = b.sb("me_rec", [P, HM])
        pr = b.sb("me_pr", [P, HM, NK])
        pt = b.sb("me_pt", [P, 2, HM, MT, P])
        o_sb = b.sb("me_o", [P, HM, DM])
        ot = b.sb("me_ot", [P, HM * P])
        s_ps = b.ps("me_sps", [P, HM, NK])
        t_ps = b.ps("me_tps", [P, HM, MT, P])
        q_ps = b.ps("me_qps", [P, HM, P])
        o_ps = b.ps("me_ops", [P, HM, DM])
        ot_ps = b.ps("me_otps", [P, HM, P])
        S = {n: b.sem(f"me_s_{n}") for n in (
            "const", "v", "ksq", "kred", "kpow", "kn", "kt", "kcopy", "half",
            "sq", "red", "pow", "qw", "qn", "qt", "qcopy", "s", "mx", "nm", "e", "t", "tcopy", "o", "rec",
            "oscaled", "ot", "otcopy")}
        q_loaded, k_loaded = b.sems("me_ql", 2), b.sems("me_kl", 2)
        stored = b.sem("me_stored")
        block = b.block()

        def steps(engine, body, first=0, last=NT):
            for t in range(first, 4):
                body(t, t % 2)
            with engine.Fori(2, TP // 2) as j:
                for s in range(2):
                    body(2 * j + s, s)
            for t in range(TP, last):
                body(t, t % 2)

        def is0(t, n=0):
            return isinstance(t, int) and t <= n

        @block.sync
        def _(sp):
            kv = mem_proj.rearrange("(t p) n -> p t n", p=P)
            for i in range(2):
                sp.dma_start(k_raw[:, MT * i:MT * (i + 1)], kv[:, MT * i:MT * (i + 1), 0:512]).then_inc(k_loaded[i], 16)
            for dst, src in ((ident[:, :], ident_dram), (wq[:, 0], small["mq_norm_w"].broadcast_to([P, DM])),
                             (wk[:, 0], small["mk_norm_w"].broadcast_to([P, DM]))):
                sp.dma_start(dst, src).then_inc(S["const"], 16)
            sp.dma_start(v_sb[:, :, :, :], kv[:, :, 512:1024]).then_inc(S["v"], 16)

            def load(t, s):
                if not is0(t, 1):
                    sp.wait_ge(S["sq"], t - 1)
                    sp.wait_ge(S["qw"], t - 1)
                rows = slice(t * P, (t + 1) * P) if isinstance(t, int) else ds(t * P, P)
                sp.dma_start(q_raw[:, s], proj[rows, 2048:2560]).then_inc(q_loaded[s], 16)

            steps(sp, load)

        def is_last(t, n):
            return isinstance(t, int) and t >= NT - n

        def loaded(t, s):
            return 16 * (t // 2 + 1) if isinstance(t, int) else 8 * (t - s) + 16

        @block.gpsimd
        def _(pool):
            b.clear_previous(pool)
            g = nc.gpsimd
            g.memset(half[:, :], -0.5).then_inc(S["half"], 1)
            g.memset(eps[:, :], EPS).then_inc(S["half"], 1)
            pool.wait_ge(S["half"], 2)
            for i in range(2):
                c = slice(MT * HM * i, MT * HM * (i + 1))
                pool.wait_ge(S["kred"], i + 1)
                g.tensor_tensor(k_mse[:, c], k_ss[:, c], eps[:, c], ALU.add).then_inc(S["kpow"], 1)
                pool.wait_ge(S["kpow"], 2 * i + 1)
                g.tensor_tensor(k_rstd[:, c], k_mse[:, c], half[:, c], ALU.pow).then_inc(S["kpow"], 1)
            pool.wait_ge(S["const"], 48)

            def queries(t, s):
                pool.wait_ge(q_loaded[s], loaded(t, s))
                if not is0(t):
                    pool.wait_ge(S["qn"], t)
                g.tensor_tensor(q_w[:, :, :], q_raw[:, s], bc(wq[:, :, :], [P, HM, DM]), ALU.mult
                                ).then_inc(S["qw"], 1)
                pool.wait_ge(S["red"], t + 1)
                g.tensor_tensor(q_mse[:, :], q_ss[:, :], eps[:, 0:HM], ALU.add).then_inc(S["pow"], 1)
                pool.wait_ge(S["pow"], 2 * t + 1)
                g.tensor_tensor(q_rstd[:, :], q_mse[:, :], half[:, 0:HM], ALU.pow).then_inc(S["pow"], 1)

            steps(pool, queries)

        @block.scalar
        def _(act):
            a = nc.scalar
            for i in range(2):
                act.wait_ge(k_loaded[i], 16)
                a.activation(k_sq[:, MT * i:MT * (i + 1)], k_raw[:, MT * i:MT * (i + 1)], ACT.Square, scale=SC
                             ).then_inc(S["ksq"], 1)
            for i in range(2):
                for m in range(2):
                    act.wait_ge(S["kt"], 2 * i + m + 1)
                    k = 2 * i + m
                    a.activation(kt[:, :, k * P:(k + 1) * P], (t_ps[:, 0:2] if m == 0 else t_ps[:, 2:4]
                                 ).rearrange("p a b c -> p (a b) c"), ACT.Copy).then_inc(S["kcopy"], 1)

            def square(t, s):
                act.wait_ge(q_loaded[s], loaded(t, s))
                if not is0(t):
                    act.wait_ge(S["red"], t)
                a.activation(q_sq[:, :, :], q_raw[:, s], ACT.Square, scale=SC).then_inc(S["sq"], 1)

            def q_copy(t):
                act.wait_ge(S["qt"], t + 1)
                if not is0(t):
                    act.wait_ge(S["s"], 2 * t)
                a.activation(qt[:, :, :], q_ps[:, :, :], ACT.Copy).then_inc(S["qcopy"], 1)

            square(0, 0)
            q_copy(0)
            square(1, 1)

            def tile(t, s):
                if not is_last(t, 2):
                    square(t + 2, s)
                if not is0(t, 1):
                    act.wait_ge(S["rec"], t - 1)
                for c in range(2):
                    act.wait_ge(S["nm"], 2 * t + c + 1)
                    if not is0(t):
                        act.wait_ge(S["t"], 2 * t + c - 1)
                    for h in (2 * c, 2 * c + 1):
                        m = a.activation(pr[:, h], s_ps[:, h], ACT.Exp, bias=nm[:, h:h + 1], scale=SC,
                                         accum_out=rowsum[:, s, h:h + 1])
                    m.then_inc(S["e"], 1)
                if not is_last(t, 1):
                    q_copy(t + 1)
                if not is0(t, 2):
                    store(t - 3)

            def store(t):
                act.wait_ge(S["ot"], t + 1)
                if not is0(t):
                    act.wait_ge(stored, 16 * t)
                a.activation(ot[:, :], ot_ps[:, :, :], ACT.Copy).then_inc(S["otcopy"], 1)
                act.wait_ge(S["otcopy"], t + 1)
                dst = mix_t[t] if isinstance(t, int) else mix_t[ds(t, 1)]
                act.dma_start(dst[..., 12 * P:16 * P], ot[:, :]).then_inc(stored, 16)

            steps(act, tile)
            for t in range(NT - 3, NT):
                store(t)
            act.wait_ge(stored, 16 * NT)

        @block.vector
        def _(dve):
            v = nc.vector
            for i in range(2):
                m = slice(MT * i, MT * (i + 1))
                dve.wait_ge(S["ksq"], i + 1)
                v.reduce_sum(k_ss[:, MT * HM * i:MT * HM * (i + 1)], k_sq[:, m], AX.X).then_inc(S["kred"], 1)
                if i == 0:
                    dve.wait_ge(S["const"], 48)
                v.tensor_tensor(k_n[:, m], k_raw[:, m], bc(wk[:, :, :].unsqueeze(1), [P, MT, HM, DM]),
                                ALU.mult).then_inc(S["kn"], 1)
            kr = k_rstd[:, :].rearrange("p (t h) -> p t h", h=HM).unsqueeze(3)
            for i in range(2):
                m = slice(MT * i, MT * (i + 1))
                dve.wait_ge(S["kpow"], 2 * i + 2)
                dve.wait_ge(S["kn"], i + 1)
                v.tensor_tensor(k_n[:, m], k_n[:, m], bc(kr[:, m], [P, MT, HM, DM]), ALU.mult
                                ).then_inc(S["kn"], 1)

            def queries(t):
                dve.wait_ge(S["sq"], t + 1)
                if not is0(t):
                    dve.wait_ge(S["pow"], 2 * t)
                v.reduce_sum(q_ss[:, :], q_sq[:, :, :], AX.X).then_inc(S["red"], 1)
                dve.wait_ge(S["pow"], 2 * t + 2)
                dve.wait_ge(S["qw"], t + 1)
                if not is0(t):
                    dve.wait_ge(S["qt"], t)
                v.tensor_tensor(q_n[:, :, :], q_w[:, :, :], bc(q_rstd[:, :].unsqueeze(2), [P, HM, DM]),
                                ALU.mult).then_inc(S["qn"], 1)

            queries(0)
            queries(1)

            def invert(t, s):
                if not is0(t):
                    dve.wait_ge(S["oscaled"], t)
                dve.wait_ge(S["e"], 2 * t + 2)
                v.reciprocal(rec[:, :], rowsum[:, s]).then_inc(S["rec"], 1)

            def scale(t):
                dve.wait_ge(S["rec"], t + 1)
                dve.wait_ge(S["o"], t + 1)
                if not is0(t):
                    dve.wait_ge(S["ot"], t)
                v.tensor_tensor(o_sb[:, :, :], o_ps[:, :, :], bc(rec[:, :].unsqueeze(2), [P, HM, DM]),
                                ALU.mult).then_inc(S["oscaled"], 1)

            def tile(t, s):
                if not is0(t, 1):
                    invert(t - 2, s)
                for c in range(2):
                    two = slice(2 * c, 2 * c + 2)
                    dve.wait_ge(S["s"], 2 * t + c + 1)
                    if not is0(t):
                        dve.wait_ge(S["nm"], 2 * t + c - 1)
                    v.reduce_max(mx[:, two], s_ps[:, two, :], AX.X).then_inc(S["mx"], 1)
                    dve.wait_ge(S["mx"], 2 * t + c + 1)
                    if not is0(t):
                        dve.wait_ge(S["e"], 2 * t + c - 1)
                    v.tensor_scalar(nm[:, two], mx[:, two], -SC, None, ALU.mult).then_inc(S["nm"], 1)
                if not is0(t, 1):
                    scale(t - 2)
                if not is_last(t, 2):
                    queries(t + 2)
                if not is0(t, 1):
                    dve.wait_ge(S["o"], t - 1)
                for c in range(2):
                    dve.wait_ge(S["t"], 2 * t + c + 1)
                    v.tensor_copy(pt[:, s, 2 * c:2 * c + 2], t_ps[:, 2 * c:2 * c + 2]).then_inc(S["tcopy"], 1)

            steps(dve, tile)
            for t in (NT - 2, NT - 1):
                invert(t, t % 2)
                scale(t)

        @block.tensor
        def _(pe):
            T = nc.tensor
            pe.wait_ge(S["const"], 48)
            for k in range(NMT):
                pe.wait_ge(S["kn"], 3 + k // MT)
                if k >= 2:
                    pe.wait_ge(S["kcopy"], k - 1)
                for h in range(HM):
                    m = T.transpose(t_ps[:, 2 * (k % 2) + h // 2, h % 2], k_n[:, k, h], ident[:, :])
                m.then_inc(S["kt"], 1)
            pe.wait_ge(S["kcopy"], NMT)
            pe.wait_ge(S["v"], 16)

            def q_t(t):
                pe.wait_ge(S["qn"], t + 1)
                if not is0(t):
                    pe.wait_ge(S["qcopy"], t)
                for h in range(HM):
                    m = T.transpose(q_ps[:, h], q_n[:, h], ident[:, :])
                m.then_inc(S["qt"], 1)

            def scores(t, sequence, c):
                pe.wait_ge(S["qcopy"], t + 1)
                if not is0(t):
                    pe.wait_ge(S["e"], 2 * t + c - 1)
                c0 = sequence * NK
                for h in (2 * c, 2 * c + 1):
                    m = T.matmul(s_ps[:, h], qt[:, h], kt[:, h, c0:c0 + NK], start=True, stop=True)
                m.then_inc(S["s"], 1)

            def o_t(t):
                pe.wait_ge(S["oscaled"], t + 1)
                if not is0(t):
                    pe.wait_ge(S["otcopy"], t)
                for h in range(HM):
                    m = T.transpose(ot_ps[:, h], o_sb[:, h], ident[:, :])
                m.then_inc(S["ot"], 1)

            def seq(t):
                return int(isinstance(t, int) and t >= TP)

            def output(t, s, sequence):
                pe.wait_ge(S["tcopy"], 2 * t + 2)
                if not is0(t):
                    pe.wait_ge(S["oscaled"], t)
                for h in range(HM):
                    for k in range(MT):
                        m = T.matmul(o_ps[:, h], pt[:, s, h, k], v_sb[:, MT * sequence + k, h],
                                     start=(k == 0), stop=(k == MT - 1))
                m.then_inc(S["o"], 1)

            q_t(0)
            for c in range(2):
                scores(0, 0, c)

            def tile(t, s, last_of_prompt=False):
                if not is_last(t, 1):
                    q_t(t + 1)
                for c in range(2):
                    pe.wait_ge(S["e"], 2 * t + c + 1)
                    if not is0(t):
                        pe.wait_ge(S["tcopy"], 2 * t + c - 1)
                    for h in (2 * c, 2 * c + 1):
                        for k in range(MT):
                            m = T.transpose(t_ps[:, h, k], pr[:, h, k * P:(k + 1) * P], ident[:, :])
                    m.then_inc(S["t"], 1)
                if not is_last(t, 1):
                    for c in range(2):
                        scores(t + 1, 1 if last_of_prompt else seq(t), c)
                if not is0(t):
                    output(t - 1, 1 - s, int(isinstance(t, int) and t > TP))
                if not is0(t, 1):
                    o_t(t - 2)

            for t in range(2):
                tile(t, t)
            with pe.Fori(1, TP // 2 - 1) as j:
                for s in range(2):
                    tile(2 * j + s, s)
            for t in range(TP - 2, NT):
                tile(t, t % 2, t == TP - 1)
            output(NT - 1, 1, 1)
            o_t(NT - 2)
            o_t(NT - 1)


def ssm_backward(nc, xbc_c, ident_dram, R):
    with ExitStack() as ctx:
        b = Bufs(nc, ctx)
        ident = b.sb("sb_ident", [P, P])
        xc = b.sb("sb_xc", [P, 2, XBC])
        x_dec = b.sb("sb_xdec", [P, NS, PS])
        b_tok = b.sb("sb_btok", [P, NG, ST])
        state = b.sb("sb_state", [P, NS, PS])
        scaled = b.sb("sb_scaled", [P, NS, PS])
        x_ps = b.ps("sb_xps", [P, NS, PS])
        b_ps = b.ps("sb_bps", [P, NG, ST])
        s_ps = b.ps("sb_sps", [P, NS, PS])
        y_ps = b.ps("sb_yps", [P, NS, PS])
        S = {n: b.sem(f"sb_s_{n}") for n in ("const", "turn", "x", "b", "off", "st", "y", "h", "zero", "sp_ready", "dve_ready")}
        loaded = b.sems("sb_l", 2)
        block = b.block()
        y_back, e_acs, e_tot, dec = R["y_back"], R["e_acs"], R["e_tot"], R["dec"]

        def order(engine, body, reset=None):
            if reset:
                reset(0)
            for s in range(2):
                body(s, s, NT - 1 - s, s == 0)
            if reset:
                reset(1)
            with engine.Fori(1, NT // 2) as j:
                for s in range(2):
                    body(2 * j + s, s, NT - 1 - (2 * j + s), False)

        def at(buf, t):
            return buf[:, t:t + 1] if isinstance(t, int) else buf[:, ds(t, 1)]

        @block.sync
        def _(sp):
            sp.dma_start(ident[:, :], ident_dram).then_inc(S["const"], 16)

            def load(i, s, t, first):
                if not isinstance(i, int):
                    sp.wait_ge(S["off"], i - 1)
                sp.sem_inc(S["sp_ready"], 1)
                sp.dma_start(xc[:, s], xbc_c[t] if isinstance(t, int) else xbc_c[ds(t, 1)]
                             ).then_inc(loaded[s], 16)

            order(sp, load)

        def loaded_value(i, s):
            return 16 if isinstance(i, int) else 8 * (i - s) + 16

        @block.tensor
        def _(pe):
            T = nc.tensor
            pe.wait_ge(S["const"], 16)

            def body(i, s, t, first):
                pe.wait_ge(loaded[s], loaded_value(i, s))
                if not first:
                    pe.wait_ge(S["x"], i)
                    pe.wait_ge(S["b"], i)
                for c in range(4):
                    T.transpose(x_ps[:, 2 * c:2 * c + 2], xc[:, s, c * P:(c + 1) * P], ident[:, :])
                for g in range(NG):
                    m = T.transpose(b_ps[:, g], xc[:, s, (4 + g) * P:(5 + g) * P], ident[:, :])
                m.then_inc(S["turn"], 1)
                if first:
                    pe.wait_ge(S["zero"], 1)
                else:
                    pe.wait_ge(S["h"], 2 * i)
                    pe.wait_ge(S["y"], i)
                for g in range(NG):
                    m = T.matmul(y_ps[:, 4 * g:4 * g + 4], xc[:, s, (6 + g) * P:(7 + g) * P],
                                 state[:, 4 * g:4 * g + 4], start=True, stop=True)
                m.then_inc(S["off"], 1)
                pe.wait_ge(S["x"], i + 1)
                pe.wait_ge(S["b"], i + 1)
                for g in range(NG):
                    m = T.matmul(s_ps[:, 4 * g:4 * g + 4], b_tok[:, g], x_dec[:, 4 * g:4 * g + 4],
                                 start=True, stop=True)
                m.then_inc(S["st"], 1)

            def reset(k):
                if k:
                    pe.wait_ge(S["zero"], 2)

            order(pe, body, reset)

        @block.gpsimd
        def _(pool):
            b.clear_previous(pool)

        @block.scalar
        def _(act):
            def body(i, s, t, first):
                act.wait_ge(S["turn"], i + 1)
                if not first:
                    act.wait_ge(S["st"], i)
                nc.scalar.activation(b_tok[:, :, :], b_ps[:, :, :], ACT.Copy).then_inc(S["b"], 1)

            order(act, body)

        @block.vector
        def _(dve):
            v = nc.vector

            def factor(buf, t):
                return bc(at(buf, t)[:, 0, NS:2 * NS].unsqueeze(2), [P, NS, PS])

            def body(i, s, t, first):
                dve.wait_ge(S["turn"], i + 1)
                if not first:
                    dve.wait_ge(S["st"], i)
                dve.sem_inc(S["dve_ready"], 1)
                v.tensor_tensor(x_dec[:, :, :], x_ps[:, :, :], factor(dec, t), ALU.mult).then_inc(S["x"], 1)
                dve.wait_ge(S["off"], i + 1)
                yb = y_back[:, t] if isinstance(t, int) else y_back[:, ds(t, 1)]
                yb = yb.rearrange("p (h q) -> p h q", q=PS) if isinstance(t, int) else \
                    yb.rearrange("p o (h q) -> p (o h) q", q=PS)
                v.tensor_tensor(yb, y_ps[:, :, :], factor(e_acs, t), ALU.mult).then_inc(S["y"], 1)
                v.tensor_tensor(scaled[:, :, :], state[:, :, :], factor(e_tot, t), ALU.mult).then_inc(S["h"], 1)
                dve.wait_ge(S["st"], i + 1)
                dve.wait_ge(S["h"], 2 * i + 1)
                v.tensor_tensor(state[:, :, :], scaled[:, :, :], s_ps[:, :, :], ALU.add).then_inc(S["h"], 1)

            def reset(k):
                if k:
                    dve.wait_ge(S["h"], 4)
                v.memset(state[:, :, :], 0.0).then_inc(S["zero"], 1)
                dve.wait_ge(S["zero"], k + 1)

            order(dve, body, reset)


def ssm_forward(nc, proj, xbc_c, ident_dram, small, R, mix_t):
    XW = NS * PS
    with ExitStack() as ctx:
        b = Bufs(nc, ctx)
        ident = b.sb("sf_ident", [P, P])
        wn = b.sb("sf_wn", [P, XW])
        dsk = b.sb("sf_dskip", [P, NS])
        half = b.sb("sf_half", [P, 1])
        eps = b.sb("sf_eps", [P, 1])
        z = b.sb("sf_z", [P, 2, XW])
        xc = b.sb("sf_xc", [P, 2, XBC])
        b_tok = b.sb("sf_btok", [P, NG, ST])
        x_tok = b.sb("sf_xtok", [P, NS, PS])
        x_dec = b.sb("sf_xdec", [P, NS, PS])
        x_dt = b.sb("sf_xdt", [P, 2, NS, PS])
        state = b.sb("sf_state", [P, NS, PS])
        scaled = b.sb("sf_scaled", [P, NS, PS])
        cb = b.sb("sf_cb", [P, 2, NG, 1, P])
        a_tri = b.sb("sf_atri", [P, 2, NS, P])
        acs_t = b.sb("sf_acst", [P, 2, 2 * NS])
        drop = b.sb("sf_drop", [P, 2, NS, P])
        m_t = b.sb("sf_mt", [P, 2, NS, P])
        y = b.sb("sf_y", [P, 2, XW])
        y2 = b.sb("sf_y2", [P, XW])
        sq = b.sb("sf_sq", [P, XW])
        ms = b.sb("sf_ms", [P, 1])
        mse = b.sb("sf_mse", [P, 1])
        rstd = b.sb("sf_rstd", [P, 1])
        yn = b.sb("sf_yn", [P, 2, XW])
        ot = b.sb("sf_ot", [P, XW])
        ones = b.sb("sf_ones", [P, P])
        x_ps = b.ps("sf_xps", [P, NS, PS])
        m_ps = b.ps("sf_mps", [P, 4, P])
        s_ps = b.ps("sf_sps", [P, NS, PS])
        y_ps = b.ps("sf_yps", [P, NS, PS])
        d_ps = b.ps("sf_dps", [P, NS, P])
        g_ps = b.ps("sf_gps", [P, NS, PS])
        t_ps = b.ps("sf_tps", [P, 4, P])
        S = {n: b.sem(f"sf_s_{n}") for n in (
            "const", "half", "ones", "turn", "xcopy", "bcopy", "xd", "off", "st", "h", "zero", "cb", "cbm", "atri",
            "rows", "acs", "drop", "e", "m", "diag", "y", "gated", "sq", "pow", "yn", "tn", "tcopy", "xdt")}
        loaded, z_loaded = b.sems("sf_l", 2), b.sems("sf_zl", 2)
        stored = b.sem("sf_stored")
        block = b.block()
        y_back, e_acs, e_tot, dec, dt, acs, a_sb, tri = (
            R[k] for k in ("y_back", "e_acs", "e_tot", "dec", "dt", "acs", "a", "tri"))

        def order(engine, body, reset=None):
            if reset:
                reset(0)
            for s in range(2):
                body(s, s)
            with engine.Fori(1, TP // 2) as j:
                for s in range(2):
                    body(2 * j + s, s)
            if reset:
                reset(1)
            for s in range(2):
                body(TP + s, s)

        def before(t, n):
            return isinstance(t, int) and t < n

        def loaded_value(t, s):
            return 16 * (t // 2 + 1) if isinstance(t, int) else 8 * (t - s) + 16

        def row(buf, t, lo_, hi_):
            r = buf[:, t:t + 1] if isinstance(t, int) else buf[:, ds(t, 1)]
            return r[:, 0, lo_:hi_].unsqueeze(2)

        @block.sync
        def _(sp):
            for dst, src in ((ident[:, :], ident_dram), (wn[:, :], small["ssm_norm_w"].broadcast_to([P, XW])),
                             (dsk[:, :], small["ssm_D"].broadcast_to([P, NS]))):
                sp.dma_start(dst, src).then_inc(S["const"], 16)

            def load(t, s):
                if not before(t, 2):
                    sp.wait_ge(S["cb"], t - 1)
                sp.dma_start(xc[:, s], xbc_c[t] if isinstance(t, int) else xbc_c[ds(t, 1)]
                             ).then_inc(loaded[s], 16)
                if not before(t, 2):
                    sp.wait_ge(S["gated"], 2 * (t - 1))
                rows = slice(t * P, (t + 1) * P) if isinstance(t, int) else ds(t * P, P)
                sp.dma_start(z[:, s], proj[rows, 1536:2048]).then_inc(z_loaded[s], 16)

            order(sp, load)

        @block.tensor
        def _(pe):
            T = nc.tensor
            pe.wait_ge(S["const"], 48)
            pe.wait_ge(S["ones"], 1)

            def within(t, first=False):
                pe.wait_ge(S["xdt"], 2 * t + 2)
                pe.wait_ge(S["m"], 2 * t + 2)
                if not first:
                    pe.wait_ge(S["gated"], 2 * t - 1)
                for h in range(NS):
                    for d in range(2):
                        m = T.matmul(g_ps[:, h], m_t[:, d, h], x_dt[:, d, h], start=(d == 0), stop=(d == 1))
                m.then_inc(S["diag"], 1)

            def turn_back(t, s, first=False):
                pe.wait_ge(S["yn"], t + 1)
                if not first:
                    pe.wait_ge(S["tcopy"], t)
                for c in range(4):
                    m = T.transpose(t_ps[:, c], yn[:, s, c * P:(c + 1) * P], ident[:, :])
                m.then_inc(S["tn"], 1)

            def body(t, s):
                first = before(t, 1)
                pe.wait_ge(loaded[s], loaded_value(t, s))
                if not first:
                    pe.wait_ge(S["xcopy"], t)
                    pe.wait_ge(S["bcopy"], t)
                    pe.wait_ge(S["cbm"], 2 * t)
                for c in range(4):
                    T.transpose(x_ps[:, 2 * c:2 * c + 2], xc[:, s, c * P:(c + 1) * P], ident[:, :])
                for g in range(NG):
                    m = T.transpose(m_ps[:, g], xc[:, s, (4 + g) * P:(5 + g) * P], ident[:, :])
                m.then_inc(S["turn"], 1)
                for d in range(2):
                    pe.wait_ge(S["atri"], 2 * t + d + 1)
                    if not (first and d == 0):
                        pe.wait_ge(S["drop"], 2 * t + d)
                    for g in range(NG):
                        m = T.matmul(d_ps[:, 4 * g:4 * g + 4], ones[:, :], a_tri[:, d, 4 * g:4 * g + 4],
                                     start=True, stop=True)
                    m.then_inc(S["rows"], 1)
                    if d == 0:
                        if first:
                            pe.wait_ge(S["zero"], 1)
                        else:
                            pe.wait_ge(S["h"], 2 * t)
                            pe.wait_ge(S["y"], 4 * t - 3)
                        for g in range(NG):
                            m = T.matmul(y_ps[:, 4 * g:4 * g + 4], xc[:, s, (6 + g) * P:(7 + g) * P],
                                         state[:, 4 * g:4 * g + 4], start=True, stop=True)
                        m.then_inc(S["off"], 1)
                        pe.wait_ge(S["bcopy"], t + 1)
                        for g in range(NG):
                            m = T.matmul(m_ps[:, 2 + g], xc[:, s, (4 + g) * P:(5 + g) * P],
                                         xc[:, s, (6 + g) * P:(7 + g) * P], start=True, stop=True)
                        m.then_inc(S["cb"], 1)
                        if not first:
                            within(t - 1, before(t, 2))
                        pe.wait_ge(S["xd"], t + 1)
                        for g in range(NG):
                            m = T.matmul(s_ps[:, 4 * g:4 * g + 4], b_tok[:, g], x_dec[:, 4 * g:4 * g + 4],
                                         start=True, stop=True)
                        m.then_inc(S["st"], 1)
                if not before(t, 2):
                    turn_back(t - 2, s, before(t, 3))

            def reset(k):
                if k:
                    pe.wait_ge(S["zero"], 2)

            order(pe, body, reset)
            within(NT - 1)
            turn_back(NT - 2, 0)
            turn_back(NT - 1, 1)

        @block.gpsimd
        def _(pool):
            b.clear_previous(pool)
            g = nc.gpsimd
            g.memset(ones[:, :], 1.0).then_inc(S["ones"], 1)
            g.memset(half[:, :], -0.5).then_inc(S["half"], 1)
            g.memset(eps[:, :], EPS).then_inc(S["half"], 1)
            pool.wait_ge(S["half"], 2)

            def triangle_of(t, d, first=False):
                if not first:
                    pool.wait_ge(S["rows"], 2 * t + d - 1)
                g.tensor_tensor(a_tri[:, d], bc(row(a_sb, t, d * NS, (d + 1) * NS), [P, NS, P]),
                                bc(tri[:, d:d + 1, :], [P, NS, P]), ALU.mult).then_inc(S["atri"], 1)

            def rstd_of(t, first=False):
                pool.wait_ge(S["sq"], t + 1)
                g.tensor_tensor(mse[:, :], ms[:, :], eps[:, :], ALU.add).then_inc(S["pow"], 1)
                pool.wait_ge(S["pow"], 2 * t + 1)
                if not first:
                    pool.wait_ge(S["yn"], t)
                g.tensor_tensor(rstd[:, :], mse[:, :], half[:, :], ALU.pow).then_inc(S["pow"], 1)

            def body(t, s):
                pool.wait_ge(S["xcopy"], t + 1)
                for d in range(2):
                    if not before(t, 1):
                        pool.wait_ge(S["diag"], t)
                    g.tensor_tensor(x_dt[:, d], x_tok[:, :, :], bc(row(dt, t, d * NS, (d + 1) * NS), [P, NS, PS]),
                                    ALU.mult).then_inc(S["xdt"], 1)
                end = isinstance(t, int) and t == NT - 1
                if not end:
                    triangle_of(t + 1, 0)
                if not before(t, 1):
                    rstd_of(t - 1, before(t, 2))
                if not end:
                    triangle_of(t + 1, 1)

            for d in range(2):
                triangle_of(0, d, True)
            order(pool, body)
            rstd_of(NT - 1)

        @block.scalar
        def _(act):
            a = nc.scalar

            def squares(t, s, first=False):
                act.wait_ge(S["gated"], 2 * t + 2)
                if not first:
                    act.wait_ge(S["pow"], 2 * t - 1)
                    act.wait_ge(S["sq"], t)
                a.activation(sq[:, :], y[:, s], ACT.Square, scale=XW ** -0.5, accum_out=ms[:, :]
                             ).then_inc(S["sq"], 1)

            def store(t, first=False):
                act.wait_ge(S["tn"], t + 1)
                if not first:
                    act.wait_ge(stored, 16 * t)
                a.activation(ot[:, :], t_ps[:, :, :], ACT.Copy).then_inc(S["tcopy"], 1)
                act.wait_ge(S["tcopy"], t + 1)
                dst = mix_t[t] if isinstance(t, int) else mix_t[ds(t, 1)]
                act.dma_start(dst[..., 8 * P:12 * P], ot[:, :]).then_inc(stored, 16)

            def body(t, s):
                act.wait_ge(S["turn"], t + 1)
                if not before(t, 1):
                    act.wait_ge(S["st"], t)
                    act.wait_ge(S["y"], 4 * t - 2)
                    act.wait_ge(S["xdt"], 2 * t)
                    act.wait_ge(S["xd"], t)
                a.activation(b_tok[:, :, :], m_ps[:, 0:2], ACT.Copy).then_inc(S["bcopy"], 1)
                a.activation(x_tok[:, :, :], x_ps[:, :, :], ACT.Copy).then_inc(S["xcopy"], 1)
                act.wait_ge(S["acs"], t + 1)
                for d in range(2):
                    act.wait_ge(S["rows"], 2 * t + d + 1)
                    if not before(t, 1):
                        act.wait_ge(S["m"], 2 * t - 1 + d)
                    for h in range(NS):
                        m = a.activation(drop[:, d, h], d_ps[:, h], ACT.Relu, scale=-1.0,
                                         bias=acs_t[:, s, d * NS + h:d * NS + h + 1])
                    m.then_inc(S["drop"], 1)
                    if d == 1 and not before(t, 1):
                        squares(t - 1, 1 - s, before(t, 2))
                    act.wait_ge(S["drop"], 2 * t + d + 1)
                    a.activation(drop[:, d], drop[:, d], ACT.Exp, scale=-1.0).then_inc(S["e"], 1)
                if not before(t, 2):
                    store(t - 2, before(t, 3))

            order(act, body)
            squares(NT - 1, 1)
            store(NT - 2)
            store(NT - 1)
            act.wait_ge(stored, 16 * NT)

        @block.vector
        def _(dve):
            v = nc.vector
            dve.wait_ge(S["const"], 48)

            def hp(ap):
                return ap.rearrange("p (h q) -> p h q", q=PS)

            def gate(t, s):
                dve.wait_ge(S["diag"], t + 1)
                dve.wait_ge(S["y"], 4 * t + 4)
                v.tensor_tensor(hp(y[:, s]), hp(y[:, s]), g_ps[:, :, :], ALU.add).then_inc(S["gated"], 1)
                dve.wait_ge(S["gated"], 2 * t + 1)
                dve.wait_ge(z_loaded[s], loaded_value(t, s))
                v.tensor_tensor(y[:, s], y[:, s], z[:, s], ALU.mult).then_inc(S["gated"], 1)

            def norm(t, s, first=False):
                dve.wait_ge(S["pow"], 2 * t + 2)
                if not first:
                    dve.wait_ge(S["tn"], t - 1)
                v.scalar_tensor_tensor(yn[:, s], y[:, s], rstd[:, :], wn[:, :], ALU.mult, ALU.mult
                                       ).then_inc(S["yn"], 1)

            def body(t, s):
                if not before(t, 2):
                    dve.wait_ge(S["drop"], 2 * t - 2)
                at = acs[:, t:t + 1] if isinstance(t, int) else acs[:, ds(t, 1)]
                v.tensor_copy(acs_t[:, s:s + 1], at).then_inc(S["acs"], 1)
                dve.wait_ge(S["xcopy"], t + 1)
                if not before(t, 1):
                    dve.wait_ge(S["st"], t)
                v.tensor_tensor(x_dec[:, :, :], x_tok[:, :, :], bc(row(dec, t, 0, NS), [P, NS, PS]),
                                ALU.mult).then_inc(S["xd"], 1)
                dve.wait_ge(S["off"], t + 1)
                if not before(t, 2):
                    dve.wait_ge(S["sq"], t - 1)
                    dve.wait_ge(S["yn"], t - 1)
                v.tensor_tensor(hp(y[:, s]), y_ps[:, :, :], bc(row(e_acs, t, 0, NS), [P, NS, PS]),
                                ALU.mult).then_inc(S["y"], 1)
                if not before(t, 1):
                    dve.wait_ge(S["y"], 4 * t)
                v.tensor_tensor(hp(y2[:, :]), x_tok[:, :, :], bc(dsk[:, :].unsqueeze(2), [P, NS, PS]),
                                ALU.mult).then_inc(S["y"], 1)
                dve.wait_ge(S["cb"], t + 1)
                if not before(t, 1):
                    dve.wait_ge(S["m"], 2 * t)
                for d in range(2):
                    v.tensor_tensor(cb[:, d, :, 0], m_ps[:, 2:4], bc(tri[:, d:d + 1, :], [P, NG, P]),
                                    ALU.mult).then_inc(S["cbm"], 1)
                dve.wait_ge(S["y"], 4 * t + 2)
                yb = y_back[:, t] if isinstance(t, int) else y_back[:, ds(t, 1)].rearrange("p o n -> p (o n)")
                v.tensor_tensor(y2[:, :], y2[:, :], yb, ALU.add).then_inc(S["y"], 1)
                if not before(t, 1):
                    dve.wait_ge(S["h"], 2 * t)
                v.tensor_tensor(scaled[:, :, :], state[:, :, :], bc(row(e_tot, t, 0, NS), [P, NS, PS]),
                                ALU.mult).then_inc(S["h"], 1)
                dve.wait_ge(S["y"], 4 * t + 3)
                v.tensor_tensor(y[:, s], y[:, s], y2[:, :], ALU.add).then_inc(S["y"], 1)
                if not before(t, 1):
                    gate(t - 1, 1 - s)
                dve.wait_ge(S["st"], t + 1)
                dve.wait_ge(S["h"], 2 * t + 1)
                v.tensor_tensor(state[:, :, :], scaled[:, :, :], s_ps[:, :, :], ALU.add).then_inc(S["h"], 1)
                dve.wait_ge(S["cbm"], 2 * t + 2)
                for d in range(2):
                    dve.wait_ge(S["e"], 2 * t + d + 1)
                    if not before(t, 1):
                        dve.wait_ge(S["diag"], t)
                    v.tensor_tensor(m_t[:, d].rearrange("p (g h) l -> p g h l", g=NG),
                                    drop[:, d].rearrange("p (g h) l -> p g h l", g=NG),
                                    bc(cb[:, d], [P, NG, NS // NG, P]), ALU.mult).then_inc(S["m"], 1)
                if not before(t, 1):
                    norm(t - 1, 1 - s, before(t, 3))

            def reset(k):
                if k:
                    dve.wait_ge(S["h"], 2 * TP)
                v.memset(state[:, :, :], 0.0).then_inc(S["zero"], 1)
                dve.wait_ge(S["zero"], k + 1)

            order(dve, body, reset)
            gate(NT - 1, 1)
            norm(NT - 1, 1)


def ssm(nc, proj, ident, small, R, mix_t, xbc_c):
    with ExitStack() as ctx:
        R = {**R, "y_back": Bufs(nc, ctx).sb("ss_yback", [P, NT, NS * PS])}
        ssm_backward(nc, xbc_c, ident, R)
        ssm_forward(nc, proj, xbc_c, ident, small, R, mix_t)


def out_projection(nc, w_out, mix_t, x_dram, x1, norm_wt, ident_dram, h_hi, h_lo):
    CHUNKS = (KC + 2, KC - 2)
    REST = TOK - D
    with ExitStack() as ctx:
        b = Bufs(nc, ctx)
        raw = b.sb("wo_raw", [P, 2, D])
        w1_hi = b.sb("wo_hi", [P, CHUNKS[1], D], F32R)
        w1_lo = b.sb("wo_lo", [P, CHUNKS[1], D], F32R)
        mix = b.sb("wo_mix", [P, CHUNKS[0], P])
        m_hi = b.sb("wo_mhi", [P, 2, CHUNKS[0], P], F32R)
        m_lo = b.sb("wo_mlo", [P, 2, CHUNKS[0], P], F32R)
        ident = b.sb("wo_ident", [P, P])
        wt = b.sb("wo_wt", [P, KC])
        xn = b.sb("wo_xn", [P, D])
        ms = b.sb("wo_ms", [P, NT])
        mse = b.sb("wo_mse", [P, NT])
        rstd = b.sb("wo_rstd", [P, NT])
        half_ = b.sb("wo_half", [P, 1])
        eps = b.sb("wo_eps", [P, 1])
        bank = b.ps("wo_bank", [P, 2, 2, PW])
        xt = b.ps("wo_xt", [P, KC, P])
        x_loaded = b.sems("wo_xl", 2)
        w_loaded = b.sems("wo_rawl", 2)
        mix_loaded = b.sem("wo_mixl")
        const_loaded = b.sem("wo_const")
        w_hi_done, w_split = b.sem("wo_whid"), b.sem("wo_wsplit")
        m_hi_done, m_split = b.sem("wo_mhid"), b.sem("wo_msplit")
        multiplied, added = b.sem("wo_mm"), b.sem("wo_added")
        half_set, squared, mse_done, rstd_done = (b.sem(f"wo_{n}") for n in ("hs", "sq", "mses", "rs"))
        normed, transposed, scaled = b.sem("wo_xns"), b.sem("wo_tr"), b.sem("wo_scaled")
        h_hi_done, h_lo_done = b.sem("wo_hhi"), b.sem("wo_hlo")
        block = b.block()

        def columns(buf, k, c0, n):
            if k < KC:
                return buf[:, k, c0:c0 + n]
            row = (k - KC) * (D // REST) + c0 // REST
            return buf[:, row:row + n // REST, D:TOK]

        def second_part(engine, body):
            for u in range(2):
                body(u, u)
            with engine.Fori(1, NT // 2 - 1) as j:
                for s in range(2):
                    body(2 * j + s, s)
            for u in (NT - 2, NT - 1):
                body(u, u % 2)

        def cols(t):
            return slice(t * P, (t + 1) * P) if isinstance(t, int) else ds(t * P, P)

        def tile_of(buf, t):
            return buf[:, t:t + 1] if isinstance(t, int) else buf[:, ds(t, 1)]

        @block.sync
        def _(sp):
            def chunk(k, s):
                if not (isinstance(k, int) and k < 2):
                    sp.wait_ge(w_split, k - 1)
                rows = slice(k * P, (k + 1) * P) if isinstance(k, int) else ds(k * P, P)
                sp.dma_start(raw[:, s], w_out[rows, :]).then_inc(w_loaded[s], 16)

            x_v = x_dram.rearrange("(t p) d -> p t d", p=P)
            sp.dma_start(mix[:, :, :], mix_t[0][:, 0:CHUNKS[0] * P]).then_inc(mix_loaded, 16)
            for k in range(2):
                chunk(k, k)
            with sp.Fori(1, CHUNKS[0] // 2) as j:
                for s in range(2):
                    chunk(2 * j + s, s)
            sp.dma_start(x1[:, 0:2, :], x_v[:, 0:2, :]).then_inc(x_loaded[0], 16)
            sp.dma_start(x1[:, 2:NT, :], x_v[:, 2:NT, :]).then_inc(x_loaded[1], 16)
            sp.dma_start(ident[:, :], ident_dram).then_inc(const_loaded, 16)
            sp.dma_start(wt[:, :], norm_wt).then_inc(const_loaded, 16)
            with sp.Fori(CHUNKS[0] // 2, KC) as j:
                for s in range(2):
                    chunk(2 * j + s, s)

        @block.gpsimd
        def _(pool):
            b.clear_previous(pool)
            nc.gpsimd.memset(half_[:, :], -0.5).then_inc(half_set, 1)
            nc.gpsimd.memset(eps[:, :], EPS).then_inc(half_set, 1)
            pool.wait_ge(half_set, 2)
            with pool.Fori(0, NT) as t:
                pool.wait_ge(squared, t + 1)
                nc.gpsimd.tensor_tensor(mse[:, ds(t, 1)], ms[:, ds(t, 1)], eps[:, :],
                                        ALU.add).then_inc(mse_done, 1)
                pool.wait_ge(mse_done, t + 1)
                nc.gpsimd.tensor_tensor(rstd[:, ds(t, 1)], mse[:, ds(t, 1)], half_[:, :],
                                        ALU.pow).then_inc(rstd_done, 1)

        @block.scalar
        def _(act):
            def high(n, s, count):
                act.wait_ge(mix_loaded, 16 * n + 16)
                if not (isinstance(n, int) and n < 2):
                    act.wait_ge(multiplied, n - 1)
                nc.scalar.activation(m_hi[:, s, 0:count], mix[:, 0:count], ACT.Copy).then_inc(m_hi_done, 1)

            def following(n, part, t, s):
                act.wait_ge(m_split, n)
                first, count = (0, CHUNKS[0]) if part == 0 else CHUNKS
                src = mix_t[t] if isinstance(t, int) else mix_t[ds(t, 1)]
                act.dma_start(mix[:, 0:count], src[..., first * P:(first + count) * P]).then_inc(mix_loaded, 16)
                high(n, s, count)

            def square(t):
                act.wait_ge(added, NT + t + 1)
                if isinstance(t, int) and t == 0:
                    act.wait_ge(w_split, 2 * KC)
                else:
                    act.wait_ge(squared, t)
                x = x1[:, t, :] if isinstance(t, int) else x1[:, ds(t, 1), :]
                nc.scalar.activation(raw[:, 0], x, ACT.Square, scale=D ** -0.5,
                                     accum_out=ms[:, ds(t, 1)]).then_inc(squared, 1)

            def norm_high(t):
                act.wait_ge(scaled, t + 1)
                nc.scalar.activation(h_hi[:, :, cols(t)], xt[:, :, :], ACT.Copy).then_inc(h_hi_done, 1)

            high(0, 0, CHUNKS[0])
            following(1, 0, 1, 1)
            with act.Fori(1, NT // 2) as j:
                for s in range(2):
                    following(2 * j + s, 0, 2 * j + s, s)
            following(NT, 1, 0, 0)

            def step(u, s):
                if not (isinstance(u, int) and u == NT - 1):
                    following(NT + u + 1, 1, u + 1, 1 - s)
                if not (isinstance(u, int) and u < 1):
                    square(u - 1)
                if not (isinstance(u, int) and u < 2):
                    norm_high(u - 2)

            second_part(act, step)
            square(NT - 1)
            norm_high(NT - 2)
            norm_high(NT - 1)

        @block.vector
        def _(dve):
            v = nc.vector

            def split(n, s, w_hi, w_lo, shape):
                w = raw[:, s].rearrange("p (a b) -> p a b", a=shape) if shape > 1 else raw[:, s]
                dve.wait_ge(w_loaded[s], 8 * (n - s) + 16)
                v.tensor_copy(w_hi, w).then_inc(w_hi_done, 1)
                dve.wait_ge(w_hi_done, n + 1)
                v.tensor_tensor(w_lo, w, w_hi.bitcast(FP32), ALU.subtract).then_inc(w_split, 1)

            def weights_0(k):
                split(k, k % 2, columns(h_hi, k, 0, D), columns(h_lo, k, 0, D), 1 if k < KC else D // REST)

            def weights_1(k, s):
                kk = slice(k, k + 1) if isinstance(k, int) else ds(k, 1)
                split(CHUNKS[0] + k, s, w1_hi[:, kk], w1_lo[:, kk], 1)

            def low(n, s, part):
                count = CHUNKS[part]
                dve.wait_ge(m_hi_done, n + 1)
                v.tensor_tensor(m_lo[:, s, 0:count], mix[:, 0:count], m_hi[:, s, 0:count].bitcast(FP32),
                                ALU.subtract).then_inc(m_split, 1)

            def add(n, t, s):
                dve.wait_ge(multiplied, n + 1)
                x = x1[:, t, :] if isinstance(t, int) else x1[:, ds(t, 1), :]
                v.tensor_tensor(x, x, bank[:, s], ALU.add).then_inc(added, 1)

            def norm(t):
                dve.wait_ge(rstd_done, t + 1)
                if not (isinstance(t, int) and t == 0):
                    dve.wait_ge(transposed, t)
                x = x1[:, t, :] if isinstance(t, int) else x1[:, ds(t, 1), :]
                v.tensor_scalar(xn[:, :], x, rstd[:, ds(t, 1)], None, ALU.mult).then_inc(normed, 1)

            def turned(t):
                dve.wait_ge(transposed, t + 1)
                v.tensor_tensor(xt[:, :, :], xt[:, :, :],
                                bc(wt[:, :].unsqueeze(2), [P, KC, P]), ALU.mult).then_inc(scaled, 1)
                dve.wait_ge(h_hi_done, t + 1)
                v.tensor_tensor(h_lo[:, :, cols(t)], xt[:, :, :],
                                h_hi[:, :, cols(t)].bitcast(FP32), ALU.subtract).then_inc(h_lo_done, 1)

            low(0, 0, 0)
            weights_0(0)
            low(1, 1, 0)
            for k in range(1, CHUNKS[0]):
                weights_0(k)
            dve.wait_ge(x_loaded[0], 16)
            for s in range(2):
                add(s, s, s)
                low(s + 2, s, 0)
                weights_1(s, s)
            dve.wait_ge(x_loaded[1], 16)
            with dve.Fori(1, CHUNKS[1] // 2) as j:
                for s in range(2):
                    add(2 * j + s, 2 * j + s, s)
                    low(2 * j + s + 2, s, 0)
                    weights_1(2 * j + s, s)
            for t in range(CHUNKS[1], NT):
                add(t, t, t % 2)
                low(t + 2, t % 2, int(t + 2 >= NT))
            dve.wait_ge(added, NT)
            dve.wait_ge(const_loaded, 32)

            def step(u, s):
                if not (isinstance(u, int) and u in (0, NT - 1)):
                    low(NT + u + 1, 1 - s, 1)
                if not (isinstance(u, int) and u < 1):
                    norm(u - 1)
                if not (isinstance(u, int) and u < 2):
                    turned(u - 2)
                add(NT + u, u, s)

            second_part(dve, step)
            turned(NT - 2)
            norm(NT - 1)
            turned(NT - 1)

        @block.tensor
        def _(pe):
            def operands(part, s, k, c):
                hi, lo = (columns(h_hi, k, c * PW, PW), columns(h_lo, k, c * PW, PW)) if part == 0 else \
                    (w1_hi[:, k, c * PW:(c + 1) * PW], w1_lo[:, k, c * PW:(c + 1) * PW])
                return ((m_hi[:, s, k], hi), (m_hi[:, s, k], lo), (m_lo[:, s, k], hi))

            def tile(part, n, s):
                pe.wait_ge(m_split, n + 1)
                pe.wait_ge(added, n - 1)
                last = CHUNKS[part] - 1
                for c in range(2):
                    for k in range(CHUNKS[part]):
                        for i, (l, r) in enumerate(operands(part, s, k, c)):
                            m = nc.tensor.matmul(bank[:, s, c], l, r, start=(k == 0 and i == 0),
                                                 stop=(k == last and i == 2))
                m.then_inc(multiplied, 1)

            def turn(t):
                pe.wait_ge(normed, t + 1)
                if not (isinstance(t, int) and t == 0):
                    pe.wait_ge(h_lo_done, t)
                for k in range(KC):
                    m = nc.tensor.transpose(xt[:, k], xn[:, k * P:(k + 1) * P], ident[:, :])
                m.then_inc(transposed, 1)

            for k in range(CHUNKS[0]):
                pe.wait_ge(w_split, k + 1)
                for s in range(2):
                    if k == 0:
                        pe.wait_ge(m_split, s + 1)
                    for c in range(2):
                        for i, (l, r) in enumerate(operands(0, s, k, c)):
                            m = nc.tensor.matmul(bank[:, s, c], l, r, start=(k == 0 and i == 0),
                                                 stop=(k == CHUNKS[0] - 1 and i == 2))
                    if k == CHUNKS[0] - 1:
                        m.then_inc(multiplied, 1)
            with pe.Fori(1, NT // 2) as j:
                for s in range(2):
                    tile(0, 2 * j + s, s)
            pe.wait_ge(w_split, 2 * KC)
            pe.wait_ge(const_loaded, 32)

            def step(u, s):
                if not (isinstance(u, int) and u < 2):
                    turn(u - 2)
                tile(1, NT + u, s)

            second_part(pe, step)
            turn(NT - 2)
            turn(NT - 1)


def ffn(nc, hi, lo, w_up, w_down, conv_w, conv_b, y, out):
    PAD = TOK + 3
    GAP = SEQ + 1
    with ExitStack() as ctx:
        b = Bufs(nc, ctx)
        raw_u = b.sb("ff_rawu", [P, KC, 2, P])
        raw_d = b.sb("ff_rawd", [P, D])
        u_hi = b.sb("ff_uhi", [P, 2, KC, 2, P], F32R)
        u_lo = b.sb("ff_ulo", [P, 2, KC, 2, P], F32R)
        d_hi = b.sb("ff_dhi", [P, 2, D], F32R)
        d_lo = b.sb("ff_dlo", [P, 2, D], F32R)
        taps = b.sb("ff_taps", [P, 2 * NF, 3])
        bias = b.sb("ff_bias", [P, 2 * NF])
        padded = b.sb("ff_padded", [P, PAD])
        gate = b.sb("ff_gate", [P, PAD])
        up = b.sb("ff_up", [P, PAD])
        a_hi = b.sb("ff_ahi", [P, PAD], F32R)
        a_lo = b.sb("ff_alo", [P, PAD], F32R)
        proj = b.ps("ff_proj", [P, 2, 3 * PW])
        sums = b.ps("ff_sums", [P, 2, PW])
        const_loaded = b.sem("ff_const")
        first_loaded = b.sems("ff_fl", 2)
        u_loaded, d_loaded = b.sem("ff_ul"), b.sem("ff_dl")
        u_hi_done, u_split = b.sem("ff_uhid"), b.sem("ff_usplit")
        d_hi_done, d_split = b.sem("ff_dhid"), b.sem("ff_dsplit")
        zeroed = b.sem("ff_zeroed")
        projected, copied = b.sem("ff_proj_s"), b.sem("ff_copied")
        conved = b.sem("ff_conv")
        gated, acted = b.sem("ff_gated"), b.sem("ff_acted")
        a_hi_done, a_lo_done = b.sem("ff_ahid"), b.sem("ff_alod")
        summed, added = b.sem("ff_summed"), b.sem("ff_added")
        stored = b.sem("ff_stored")
        block = b.block()
        G = 2 * NT
        RING = 5

        def ring(g):
            k = g % RING
            return proj[:, 0, k * PW:(k + 1) * PW] if k < 3 else sums[:, k - 3]

        w_up_v = w_up.rearrange("(k p) (g n) -> p k g n", p=P, g=2)

        @block.sync
        def _(sp):
            def load(i, first=False):
                if not first:
                    sp.wait_ge(u_split, i + 1)
                for g in range(2):
                    sp.dma_start(raw_u[:, :, g], w_up_v[:, :, g, ds(i * P, P)]
                                 ).then_inc(first_loaded[g] if first else u_loaded, 16)
                if not first:
                    sp.wait_ge(d_split, i)
                sp.dma_start(raw_d[:, :], w_down[ds(i * P, P), :]).then_inc(d_loaded, 16)

            load(0, True)
            sp.dma_start(taps[:, :, :], conv_w).then_inc(const_loaded, 16)
            sp.wait_ge(const_loaded, 16)
            sp.dma_start(bias[:, :], conv_b).then_inc(const_loaded, 16)
            with sp.Fori(1, NF) as i:
                load(i)
            with sp.Fori(0, NT) as t:
                sp.wait_ge(added, (NF - 1) * G + 2 * t + 2)
                sp.dma_start(out[ds(t * P, P), :], y[:, ds(t, 1), :]).then_inc(stored, 16)
            sp.wait_ge(stored, 16 * NT)

        @block.gpsimd
        def _(pool):
            b.clear_previous(pool)

        @block.scalar
        def _(act):
            def first_up_weights(g):
                act.wait_ge(first_loaded[g], 16)
                nc.scalar.activation(u_hi[:, 0, :, g], raw_u[:, :, g], ACT.Copy).then_inc(u_hi_done, 1)

            def up_weights(i, s, first=False):
                act.wait_ge(u_loaded, 32 * i)
                if not first:
                    act.wait_ge(projected, 2 * i - 2)
                nc.scalar.activation(u_hi[:, s], raw_u[:, :, :, :], ACT.Copy).then_inc(u_hi_done, 1)

            def down_weights(i, s, first=False):
                act.wait_ge(d_loaded, 16 * i + 16)
                if not first:
                    act.wait_ge(summed, G * (i - 1))
                nc.scalar.activation(d_hi[:, s], raw_d[:, :], ACT.Copy).then_inc(d_hi_done, 1)

            def copy(i, g, first=False):
                act.wait_ge(projected, 2 * i + g + 1)
                if not first:
                    act.wait_ge(conved, 3 * (2 * i + g))
                nc.scalar.activation(padded[:, 1:1 + SEQ], proj[:, g, 0:SEQ], ACT.Copy)
                nc.scalar.activation(padded[:, GAP + 1:GAP + 1 + DEC], proj[:, g, SEQ:TOK],
                                     ACT.Copy).then_inc(copied, 1)

            def hidden(i, first=False):
                act.wait_ge(conved, 6 * i + 3)
                nc.scalar.activation(gate[:, 1:GAP + 1 + DEC], gate[:, 1:GAP + 1 + DEC],
                                     ACT.Silu).then_inc(gated, 1)
                act.wait_ge(acted, i + 1)
                if not first:
                    act.wait_ge(summed, G * i)
                nc.scalar.activation(a_hi[:, 1:GAP + 1 + DEC], gate[:, 1:GAP + 1 + DEC],
                                     ACT.Copy).then_inc(a_hi_done, 1)

            act.wait_ge(zeroed, 1)
            for g in range(2):
                first_up_weights(g)
            down_weights(0, 0, True)
            up_weights(1, 1, True)
            copy(0, 0, True)
            copy(0, 1)
            hidden(0, True)
            down_weights(1, 1, True)
            with act.Fori(0, (NF - 2) // 2) as j:
                for s in range(2):
                    i = 2 * j + s + 1
                    up_weights(i + 1, s)
                    copy(i, 0)
                    copy(i, 1)
                    hidden(i)
                    down_weights(i + 1, s)
            copy(NF - 1, 0)
            copy(NF - 1, 1)
            hidden(NF - 1)

        @block.vector
        def _(dve):
            nc.vector.memset(padded[:, :], 0.0).then_inc(zeroed, 1)

            def first_up_weights(g):
                dve.wait_ge(u_hi_done, g + 1)
                nc.vector.tensor_tensor(u_lo[:, 0, :, g], raw_u[:, :, g], u_hi[:, 0, :, g].bitcast(FP32),
                                        ALU.subtract).then_inc(u_split, 1)

            def up_weights(i, s):
                dve.wait_ge(u_hi_done, i + 2)
                nc.vector.tensor_tensor(u_lo[:, s], raw_u[:, :, :, :], u_hi[:, s].bitcast(FP32),
                                        ALU.subtract).then_inc(u_split, 1)

            def down_weights(i, s):
                dve.wait_ge(d_hi_done, i + 1)
                nc.vector.tensor_tensor(d_lo[:, s], raw_d[:, :], d_hi[:, s].bitcast(FP32),
                                        ALU.subtract).then_inc(d_split, 1)

            def conv(i, g, dst):
                n = 3 * (2 * i + g)
                c = i + g * NF
                mid = slice(1, GAP + 1 + DEC)
                dve.wait_ge(copied, 2 * i + g + 1)
                if g == 0 and not (isinstance(i, int) and i == 0):
                    dve.wait_ge(a_lo_done, i)
                nc.vector.tensor_scalar(dst[:, mid], padded[:, mid], taps[:, ds(c, 1), 1],
                                        bias[:, ds(c, 1)], ALU.mult, ALU.add).then_inc(conved, 1)
                dve.wait_ge(conved, n + 1)
                nc.vector.scalar_tensor_tensor(dst[:, mid], padded[:, 0:GAP + DEC], taps[:, ds(c, 1), 0],
                                               dst[:, mid], ALU.mult, ALU.add).then_inc(conved, 1)
                dve.wait_ge(conved, n + 2)
                nc.vector.scalar_tensor_tensor(dst[:, mid], padded[:, 2:GAP + 2 + DEC],
                                               taps[:, ds(c, 1), 2], dst[:, mid],
                                               ALU.mult, ALU.add).then_inc(conved, 1)

            def hidden(i):
                mid = slice(1, GAP + 1 + DEC)
                dve.wait_ge(gated, i + 1)
                dve.wait_ge(conved, 6 * i + 6)
                nc.vector.tensor_tensor(gate[:, mid], gate[:, mid], up[:, mid], ALU.mult).then_inc(acted, 1)
                dve.wait_ge(a_hi_done, i + 1)
                nc.vector.tensor_tensor(a_lo[:, mid], gate[:, mid], a_hi[:, mid].bitcast(FP32),
                                        ALU.subtract).then_inc(a_lo_done, 1)

            def adds(i):
                for t in range(NT):
                    for c in range(2):
                        g = 2 * t + c
                        dve.wait_ge(summed, G * i + g + 1)
                        v = y[:, t, c * PW:(c + 1) * PW]
                        nc.vector.tensor_tensor(v, v, ring(g), ALU.add).then_inc(added, 1)

            for g in range(2):
                first_up_weights(g)
            dve.wait_ge(const_loaded, 32)
            down_weights(0, 0)
            up_weights(1, 1)
            conv(0, 0, gate)
            conv(0, 1, up)
            hidden(0)
            down_weights(1, 1)
            with dve.Fori(0, (NF - 2) // 2) as j:
                for s in range(2):
                    i = 2 * j + s + 1
                    up_weights(i + 1, s)
                    conv(i, 0, gate)
                    adds(i - 1)
                    conv(i, 1, up)
                    hidden(i)
                    down_weights(i + 1, s)
            conv(NF - 1, 0, gate)
            adds(NF - 2)
            conv(NF - 1, 1, up)
            hidden(NF - 1)
            adds(NF - 1)

        @block.tensor
        def _(pe):
            X, U = (hi, lo), (u_hi, u_lo)

            def project(i, s, first=False):
                for g in range(2):
                    pe.wait_ge(u_split, g + 1 if first else i + 2)
                    if not first:
                        pe.wait_ge(copied, 2 * i - 1 + g)
                    if g == 0 and not (isinstance(i, int) and i < 2):
                        pe.wait_ge(added, G * (i - 1) - 2)
                    for k in range(KC):
                        for r, (w, x) in enumerate(((0, 0), (0, 1), (1, 0))):
                            for t0, n in ((0, PW), (PW, PW), (2 * PW, TOK - 2 * PW)):
                                m = nc.tensor.matmul(proj[:, g, t0:t0 + n], U[w][:, s, k, g],
                                                     X[x][:, k, t0:t0 + n],
                                                     start=(k == 0 and r == 0), stop=(k == KC - 1 and r == 2))
                    m.then_inc(projected, 1)

            def down(i, s, first=False, last=False):
                pe.wait_ge(a_lo_done, i + 1)
                pe.wait_ge(d_split, i + 1)
                if not last:
                    pe.wait_ge(copied, 2 * i + 3)
                for t in range(NT):
                    c0 = 1 + t * P + (t >= TP)
                    for c in range(2):
                        g = 2 * t + c
                        if not (first and g < RING):
                            pe.wait_ge(added, G * i + g + 1 - RING)
                        cols = slice(c * PW, (c + 1) * PW)
                        for r, (a, w) in enumerate(((a_hi, d_hi), (a_hi, d_lo), (a_lo, d_hi))):
                            m = nc.tensor.matmul(ring(g), a[:, c0:c0 + P], w[:, s, cols],
                                                 start=(r == 0), stop=(r == 2))
                        m.then_inc(summed, 1)

            project(0, 0, True)
            project(1, 1)
            down(0, 0, True)
            with pe.Fori(1, NF // 2) as j:
                for s in range(2):
                    i = 2 * j + s
                    project(i, s)
                    down(i - 1, 1 - s)
            down(NF - 1, 1, last=True)


def encoder(nc, tokens, w_in, w_mem, w_out, w_up, w_down, norm_w, norm2_t, small, ident, masks, rope, tri,
            conv_w, conv_b, ssm_conv, out, scratch):
    proj, mem_proj, xbc_c, mix_t = scratch
    with ExitStack() as ctx:
        b = Bufs(nc, ctx)
        R = {k: b.sb(f"ss_{k}", [P, NT, 2 * NS]) for k in ("dt", "acs", "e_acs", "e_tot", "dec", "a")}
        R["tri"] = b.sb("ss_tri", [P, 2, P])
        with nc.sbuf_tensor("act_hi", [P, KC, TOK + NMT * P], F32R) as hi, \
                nc.sbuf_tensor("act_lo", [P, KC, TOK + NMT * P], F32R) as lo:
            norm_transpose(nc, "n1", NT + NMT, [(norm_w[0:1, :], 0, NT), (norm_w[1:2, :], NT, NMT)],
                           ident, hi, lo, tokens)
            projections(nc, hi, lo, w_in, w_mem, proj, mem_proj, xbc_c, small, ident, tri, ssm_conv,
                        R)
        ssm(nc, proj, ident, small, R, mix_t, xbc_c)
    attention(nc, proj, ident, masks, rope, small, mix_t)
    memory(nc, proj, mem_proj, ident, small, mix_t)
    with nc.sbuf_tensor("x1", [P, NT, D], FP32) as x1:
        with nc.sbuf_tensor("h_hi", [P, KC, TOK], F32R) as hi, \
                nc.sbuf_tensor("h_lo", [P, KC, TOK], F32R) as lo:
            out_projection(nc, w_out, mix_t, tokens[0:TOK, :], x1, norm2_t, ident, hi, lo)
            ffn(nc, hi, lo, w_up, w_down, conv_w, conv_b, x1, out)
    Bufs.clear_last(nc)


def window_masks():
    q, k = np.arange(P)[:, None], np.arange(3 * P)[None] - P
    band = np.abs(k - q) <= 128
    return np.array([np.where(band & (t * P + k >= 0) & (t * P + k < n * P), 0, NEG)
                     for n in (TP, TS) for t in range(n)], np.float32)


def rope_tables():
    inv = np.float32(10000.0) ** (-np.arange(0, DH, 2, dtype=np.float32) / np.float32(DH))
    ang = np.arange(SEQ, dtype=np.float32)[:, None] * inv.astype(np.float32)[None]
    c, s = np.cos(ang), np.sin(ang)
    tab = np.stack([np.concatenate([c, c], 1), np.concatenate([-s, s], 1)])
    return tab.reshape(2, TP, P, DH).transpose(2, 0, 1, 3).astype(np.float32)


def triangles():
    i = np.arange(P)
    return np.stack([i[:, None] <= i[None], i[:, None] >= i[None]], 1).astype(np.float32)


def kernel(**inputs):
    import concourse.bacc as bacc
    from concourse.bass_utils import run_bass_kernel_spmd

    a = {k: np.asarray(v) for k, v in inputs.items()}
    w_in = a["w_in"][0]
    dt0, mq0 = 3072, 3088
    arrays = {
        "tokens": np.concatenate([a["x_prompt"][0], a["x_sample"][0], a["mem_prompt"][0], a["mem_sample"][0]]),
        "w_in": np.concatenate([w_in[:, :2048], w_in[:, mq0:], w_in[:, 2048:dt0], w_in[:, dt0:mq0]], 1),
        "w_mem": a["w_mem_kv"][0], "w_out": a["w_out"][0],
        "w_up": a["w_ffn_up"][0], "w_down": a["w_ffn_down"][0],
        "norm_w": np.concatenate([a["norm1_w"], a["mem_norm_w"]]),
        "norm2_t": a["norm2_w"].reshape(KC, P).T,
        "ident": np.eye(P, dtype=np.float32), "masks": window_masks(), "rope": rope_tables(),
        "tri": triangles(),
        "conv_w": a["ffn_conv_w"][0].reshape(3, 2 * NF, P).transpose(2, 1, 0),
        "conv_b": a["ffn_conv_b"][0].reshape(2 * NF, P).T,
        "ssm_conv": np.concatenate([a["ssm_conv_w"][0], a["ssm_conv_b"]]).reshape(6, XBC // P, P).transpose(2, 1, 0),
    }
    small = {k: a[k].reshape(1, -1) for k in (
        "q_norm_w", "k_norm_w", "attn_sink", "mq_norm_w", "mk_norm_w", "ssm_norm_w", "ssm_D",
        "ssm_dt_bias", "ssm_A_log")}
    nc = bacc.Bacc("TRN2", target_bir_lowering=False, num_devices=1)
    maps = {k: np.ascontiguousarray(v) for k, v in {**arrays, **small}.items()}
    ap = {k: nc.dram_tensor(k, v.shape, FP32, kind="ExternalInput").ap() for k, v in maps.items()}
    out = nc.dram_tensor("out", (TOK, D), FP32, kind="ExternalOutput").ap()
    scratch = [nc.dram_tensor(f"scratch_{n}", s, FP32, kind="Internal").ap() for n, s in (
        ("proj", (TOK, NPAN * PW)), ("mem", (NMT * P, 2 * PW)), ("xbc_tiles", (NT, P, XBC)), ("mix", (NT, P, 16 * P)))]
    encoder(nc, *(ap[k] for k in ("tokens", "w_in", "w_mem", "w_out", "w_up", "w_down", "norm_w", "norm2_t")),
            {k: ap[k] for k in small}, *(ap[k] for k in ("ident", "masks", "rope", "tri", "conv_w", "conv_b",
                                                          "ssm_conv")), out, scratch)
    r = run_bass_kernel_spmd(nc, [maps], core_ids=[0])
    y = r.results[0]["out"]
    return y[None, :SEQ], y[None, SEQ:]
```
